# Optimizing a Trainium2 kernel written in Bass

```python
import jax, jax.numpy as jnp
from jax import lax
import numpy as np
import math

D_MODEL = 1024
BATCH = 1
SEQ = 256
DEPTH = 1

CHUNK = 64
Q_BLOCK = 128
HEAD_DIM = 64
D_MIX = D_MODEL
SB_HEADS = 8
SB_WIDTH = SB_HEADS * HEAD_DIM
RW_WIDTH = D_MIX - SB_WIDTH
RW_HEADS = RW_WIDTH // HEAD_DIM
DECAY_LORA = 64
AAA_LORA = 64
GATE_LORA = 128
RW_PROJ = 3 * RW_WIDTH + DECAY_LORA + AAA_LORA + GATE_LORA
PROJ_WIDTH = 3 * SB_WIDTH + RW_PROJ
D_FF = 2816
FFN_HALF = 0.5
RMS_EPS = 1e-6
LNX_EPS = 64e-5


def rms_norm(x, g, eps=RMS_EPS):
    xf = x.astype(jnp.float32)
    ms = jnp.mean(xf * xf, axis=-1, keepdims=True)
    return (xf * lax.rsqrt(ms + eps) * g.astype(jnp.float32)).astype(x.dtype)

def swiglu(x, w_gate, w_up, w_down):
    return (jax.nn.silu(x @ w_gate) * (x @ w_up)) @ w_down

def token_shift(u):
    return jnp.pad(u[:, :-1], ((0, 0), (1, 0), (0, 0)))

def stick_breaking_attention(q, k, v):
    S, Dh = q.shape[1], q.shape[-1]
    scale = Dh ** -0.5
    outs = []
    for blk in range(S // Q_BLOCK):
        q0 = blk * Q_BLOCK
        kv_len = q0 + Q_BLOCK
        qb, kb, vb = q[:, q0:kv_len], k[:, :kv_len], v[:, :kv_len]
        z = jnp.einsum('bqhd,bkhd->bhqk', qb, kb).astype(jnp.float32) * scale
        q_pos = q0 + jnp.arange(Q_BLOCK)[:, None]
        k_pos = jnp.arange(kv_len)[None, :]
        mask = k_pos < q_pos
        log_beta = jax.nn.log_sigmoid(z)
        log_1m_beta = jnp.where(mask, jax.nn.log_sigmoid(-z), 0.0)
        log_remain = lax.cumsum(log_1m_beta, axis=3, reverse=True) - log_1m_beta
        att = jnp.where(mask, jnp.exp(log_beta + log_remain), 0.0)
        outs.append(jnp.einsum('bhqk,bkhd->bqhd', att.astype(vb.dtype), vb))
    return jnp.concatenate(outs, axis=1)

def rwkv7_recurrence(r, decay, k, v, a_vec, b_vec):
    B, S, H, N = r.shape
    n_chunks = S // CHUNK

    def to_chunks(t):
        return t.astype(jnp.float32).transpose(1, 0, 2, 3).reshape(n_chunks, CHUNK, B, H, N)

    xs = (to_chunks(r), to_chunks(decay), to_chunks(k), to_chunks(v),
          to_chunks(a_vec), to_chunks(b_vec))

    def step(state, inp):
        r_t, w_t, k_t, v_t, a_t, b_t = inp
        sa = jnp.einsum('bhvk,bhk->bhv', state, a_t)
        state = (state * w_t[:, :, None, :] + sa[..., None] * b_t[:, :, None, :]
                 + v_t[..., None] * k_t[:, :, None, :])
        return state, jnp.einsum('bhvk,bhk->bhv', state, r_t)

    def chunk_step(state, chunk_xs):
        return lax.scan(step, state, chunk_xs)

    state0 = jnp.zeros((B, H, N, N), jnp.float32)
    _, y = lax.scan(chunk_step, state0, xs)
    return y.reshape(S, B, H, N).transpose(1, 0, 2, 3)

def rwkv7_time_mix(u, mu, w0, w2, a0, a2, g2, k_k, k_a, r_k, ln_w, ln_b):
    B, S, _ = u.shape
    u = u + (token_shift(u) - u) * mu
    x_r, x_k, x_v, x_w, x_a, x_g = jnp.split(
        u, [RW_WIDTH, 2 * RW_WIDTH, 3 * RW_WIDTH, 3 * RW_WIDTH + DECAY_LORA,
            3 * RW_WIDTH + DECAY_LORA + AAA_LORA], axis=-1)
    log_w = -jax.nn.softplus(-(w0 + jnp.tanh(x_w) @ w2)) - 0.5
    decay = jnp.exp(-jnp.exp(log_w.astype(jnp.float32)))
    a = jax.nn.sigmoid(a0 + x_a @ a2).astype(jnp.float32)
    g = jax.nn.sigmoid(x_g) @ g2

    def heads(t):
        return t.reshape(B, S, RW_HEADS, HEAD_DIM)

    r = heads(x_r).astype(jnp.float32)
    v = heads(x_v).astype(jnp.float32)
    kk = heads(x_k * k_k).astype(jnp.float32)
    kk = kk / jnp.maximum(jnp.linalg.norm(kk, axis=-1, keepdims=True), 1e-12)
    kf = heads(x_k * (1.0 + (a - 1.0) * k_a)).astype(jnp.float32)
    a = heads(a)
    y = rwkv7_recurrence(r, heads(decay), kf, v, -kk, kk * a)
    mean = jnp.mean(y, axis=-1, keepdims=True)
    var = jnp.mean(jnp.square(y - mean), axis=-1, keepdims=True)
    yn = (y - mean) * lax.rsqrt(var + LNX_EPS)
    yn = yn * ln_w.astype(jnp.float32).reshape(RW_HEADS, HEAD_DIM) + ln_b.astype(jnp.float32).reshape(RW_HEADS, HEAD_DIM)
    bonus = jnp.sum(r * kf * r_k.astype(jnp.float32), axis=-1, keepdims=True) * v
    return ((yn + bonus).reshape(B, S, RW_WIDTH) * g.astype(jnp.float32)).astype(u.dtype)

def first_inputs(seed: int = 0) -> dict:
    key = jax.random.key(seed)
    ks = jax.random.split(key, 26)
    L, D = DEPTH, D_MODEL
    f32 = jnp.float32

    def nrm(k, shape, scale):
        return scale * jax.random.normal(k, shape, f32)

    def gain(k, shape):
        return 1.0 + 0.05 * jax.random.normal(k, shape, f32)

    return {
        "x": jax.random.normal(ks[0], (BATCH, SEQ, D), f32),
        "norm_ffn1": gain(ks[1], (L, D)),
        "ffn1_gate": nrm(ks[2], (L, D, D_FF), D ** -0.5),
        "ffn1_up": nrm(ks[3], (L, D, D_FF), D ** -0.5),
        "ffn1_down": nrm(ks[4], (L, D_FF, D), D_FF ** -0.5),
        "norm_mix": gain(ks[5], (L, D)),
        "w_in": nrm(ks[6], (L, D, PROJ_WIDTH), D ** -0.5),
        "sb_q_norm": gain(ks[7], (L, HEAD_DIM)),
        "sb_k_norm": gain(ks[8], (L, HEAD_DIM)),
        "sb_out_norm": gain(ks[9], (L, SB_WIDTH)),
        "rw_mu": jax.random.uniform(ks[10], (L, RW_PROJ), f32),
        "rw_w0": jax.random.uniform(ks[11], (L, RW_WIDTH), f32, minval=-5.0, maxval=-1.0),
        "rw_w2": nrm(ks[12], (L, DECAY_LORA, RW_WIDTH), 0.5 * DECAY_LORA ** -0.5),
        "rw_a0": nrm(ks[13], (L, RW_WIDTH), 0.1),
        "rw_a2": nrm(ks[14], (L, AAA_LORA, RW_WIDTH), 0.5 * AAA_LORA ** -0.5),
        "rw_g2": nrm(ks[15], (L, GATE_LORA, RW_WIDTH), GATE_LORA ** -0.5),
        "rw_k_k": 0.85 + 0.05 * jax.random.normal(ks[16], (L, RW_WIDTH), f32),
        "rw_k_a": gain(ks[17], (L, RW_WIDTH)),
        "rw_r_k": nrm(ks[18], (L, RW_HEADS, HEAD_DIM), 0.1),
        "rw_ln_w": gain(ks[19], (L, RW_WIDTH)),
        "rw_ln_b": nrm(ks[20], (L, RW_WIDTH), 0.01),
        "w_out": nrm(ks[21], (L, D_MIX, D), D_MIX ** -0.5),
        "norm_ffn2": gain(ks[22], (L, D)),
        "ffn2_gate": nrm(ks[23], (L, D, D_FF), D ** -0.5),
        "ffn2_up": nrm(ks[24], (L, D, D_FF), D ** -0.5),
        "ffn2_down": nrm(ks[25], (L, D_FF, D), D_FF ** -0.5),
    }

def first_block(x, norm_ffn1, ffn1_gate, ffn1_up, ffn1_down, norm_mix, w_in,
              sb_q_norm, sb_k_norm, sb_out_norm, rw_mu, rw_w0, rw_w2, rw_a0, rw_a2,
              rw_g2, rw_k_k, rw_k_a, rw_r_k, rw_ln_w, rw_ln_b, w_out, norm_ffn2,
              ffn2_gate, ffn2_up, ffn2_down):
    B, S, _ = x.shape
    for l in range(DEPTH):
        x = x + FFN_HALF * swiglu(rms_norm(x, norm_ffn1[l]), ffn1_gate[l], ffn1_up[l], ffn1_down[l])

        h = rms_norm(x, norm_mix[l])
        p = h @ w_in[l]
        sb_q, sb_k, sb_v, rw_in = jnp.split(p, [SB_WIDTH, 2 * SB_WIDTH, 3 * SB_WIDTH], axis=-1)

        q = rms_norm(sb_q.reshape(B, S, SB_HEADS, HEAD_DIM), sb_q_norm[l])
        k = rms_norm(sb_k.reshape(B, S, SB_HEADS, HEAD_DIM), sb_k_norm[l])
        v = sb_v.reshape(B, S, SB_HEADS, HEAD_DIM)
        o_sb = stick_breaking_attention(q, k, v)
        o_sb = rms_norm(o_sb, sb_out_norm[l].reshape(SB_HEADS, HEAD_DIM)).reshape(B, S, SB_WIDTH)

        o_rw = rwkv7_time_mix(rw_in, rw_mu[l], rw_w0[l], rw_w2[l], rw_a0[l], rw_a2[l], rw_g2[l],
                              rw_k_k[l], rw_k_a[l], rw_r_k[l], rw_ln_w[l], rw_ln_b[l])

        x = x + jnp.concatenate([o_sb, o_rw], axis=-1) @ w_out[l]

        x = x + FFN_HALF * swiglu(rms_norm(x, norm_ffn2[l]), ffn2_gate[l], ffn2_up[l], ffn2_down[l])
    return x


GRID_W = 64
CTX_LEN = 256
EPS = 1e-6
N_HEADS = 8
HEAD_DIM_2 = D_MODEL // 16
QK_W = N_HEADS * 2 * HEAD_DIM_2
V_W = N_HEADS * 2 * HEAD_DIM_2
ATTN_SCALE = HEAD_DIM_2 ** -0.5
ROT_FREQS = HEAD_DIM_2 // 4
ROPE_BASE = 10000.0
LAMBDA_STD = 0.1
F_GROUPS = 4
F_GROUP_DIM = D_MODEL // 8
F_W = F_GROUPS * F_GROUP_DIM
Q_OFF = 0
K_OFF = Q_OFF + QK_W
V_OFF = K_OFF + QK_W
F_OFF = V_OFF + V_W
GA_OFF = F_OFF + F_W
GF_OFF = GA_OFF + D_MODEL
PROJ_W = GF_OFF + D_MODEL
N_GROUPS = 4
EXPERTS_PER_GROUP = 4
N_EXPERTS = N_GROUPS * EXPERTS_PER_GROUP
TOP_K_IN_GROUP = 2
EXPERT_HIDDEN = D_MODEL // 2


def rmsnorm(x, g):
    x32 = x.astype(jnp.float32)
    y = x32 * lax.rsqrt(jnp.mean(x32 * x32, axis=-1, keepdims=True) + EPS)
    return (y * g.astype(jnp.float32)).astype(x.dtype)

def modulate(h, shift, scale):
    return h * (1 + scale) + shift

def axial_angles(rows):
    inv = 1.0 / (ROPE_BASE ** (jnp.arange(ROT_FREQS, dtype=jnp.float32) / ROT_FREQS))
    row = jnp.broadcast_to(jnp.arange(rows, dtype=jnp.float32)[:, None], (rows, GRID_W)).reshape(-1)
    col = jnp.broadcast_to(jnp.arange(GRID_W, dtype=jnp.float32)[None, :], (rows, GRID_W)).reshape(-1)
    return row[:, None] * inv[None, :], col[:, None] * inv[None, :]

def rotate(x, ang):
    cos = jnp.cos(ang)[:, None, None, :].astype(x.dtype)
    sin = jnp.sin(ang)[:, None, None, :].astype(x.dtype)
    x1, x2 = x[..., :ROT_FREQS], x[..., ROT_FREQS:]
    return jnp.concatenate([x1 * cos - x2 * sin, x2 * cos + x1 * sin], axis=-1)

def axial_rope(x, ang_row, ang_col):
    half = 2 * ROT_FREQS
    return jnp.concatenate([rotate(x[..., :half], ang_row), rotate(x[..., half:], ang_col)], axis=-1)

def split_proj(p):
    b, n = p.shape[:2]
    q = p[..., Q_OFF:K_OFF].reshape(b, n, N_HEADS, 2, HEAD_DIM_2)
    k = p[..., K_OFF:V_OFF].reshape(b, n, N_HEADS, 2, HEAD_DIM_2)
    v = p[..., V_OFF:F_OFF].reshape(b, n, N_HEADS, 2 * HEAD_DIM_2)
    f = p[..., F_OFF:GA_OFF]
    ga = p[..., GA_OFF:GF_OFF]
    gf = p[..., GF_OFF:PROJ_W]
    return q, k, v, f, ga, gf

def diff_attend(q, k, v, lam):
    s = jnp.einsum('bqhid,bkhid->bhiqk', q, k, preferred_element_type=jnp.float32) * ATTN_SCALE
    p = jax.nn.softmax(s, axis=-1)
    a = p[:, :, 0] - lam * p[:, :, 1]
    return jnp.einsum('bhqk,bkhe->bqhe', a.astype(v.dtype), v)

def blocked_latent_attention(q, k_all, v_all, lam):
    b, n = q.shape[:2]
    qb = q.reshape(b, n // Q_BLOCK, Q_BLOCK, N_HEADS, 2, HEAD_DIM_2).transpose(1, 0, 2, 3, 4, 5)
    out = lax.map(lambda qblk: diff_attend(qblk, k_all, v_all, lam), qb)
    return out.transpose(1, 0, 2, 3, 4).reshape(b, n, N_HEADS, 2 * HEAD_DIM_2)

def merge_branches(heads, f, ga, gf, subln_g, lam_init, w_ao, w_fo, w_o):
    b, n = heads.shape[:2]
    attn = (rmsnorm(heads, subln_g) * (1.0 - lam_init)).reshape(b, n, V_W)
    fg = f.reshape(b, n, F_GROUPS, F_GROUP_DIM).astype(jnp.float32)
    four = jnp.fft.fftn(fg, axes=(1, 3), norm='ortho').real.astype(f.dtype).reshape(b, n, F_W)
    y = jax.nn.sigmoid(ga) * (attn @ w_ao) + jax.nn.sigmoid(gf) * (four @ w_fo)
    return y @ w_o

def hier_moe(h, w_rg, b_rg, w_re, b_re, w1, w3, w2):
    b, n, d = h.shape
    t = h.reshape(-1, d)
    lg = (t @ w_rg + b_rg).astype(jnp.float32)
    g_sel = jnp.argmax(lg, axis=-1)
    w_grp = jnp.take_along_axis(jax.nn.softmax(lg, axis=-1), g_sel[:, None], axis=-1)
    le = (t @ w_re + b_re).astype(jnp.float32).reshape(-1, N_GROUPS, EXPERTS_PER_GROUP)
    le_g = jnp.take_along_axis(le, g_sel[:, None, None], axis=1)[:, 0]
    top_v, top_i = lax.top_k(le_g, TOP_K_IN_GROUP)
    w_top = jax.nn.softmax(top_v, axis=-1) * w_grp
    eid = g_sel[:, None] * EXPERTS_PER_GROUP + top_i
    gates = jnp.einsum('tk,tke->et', w_top, jax.nn.one_hot(eid, N_EXPERTS, dtype=jnp.float32)).astype(t.dtype)

    def expert_step(acc, xs):
        w1e, w3e, w2e, ge = xs
        y = (jax.nn.silu(t @ w1e) * (t @ w3e)) @ w2e
        return acc + ge[:, None] * y, None

    acc, _ = lax.scan(expert_step, jnp.zeros_like(t), (w1, w3, w2, gates))
    return acc.reshape(b, n, d)

def second_inputs(seed: int = 0) -> dict:
    key = jax.random.key(seed)
    ks = jax.random.split(key, 32)
    f32 = jnp.float32
    d = D_MODEL

    def nrm(k, shape, scale):
        return jax.random.normal(k, shape, f32) * scale

    return {
        'x': nrm(ks[0], (BATCH, SEQ, d), 1.0),
        'c': nrm(ks[1], (BATCH, d), 1.0),
        'ctx': nrm(ks[2], (BATCH, CTX_LEN, d), 1.0),
        'c_ctx': nrm(ks[3], (d,), 1.0),
        'w_mod': nrm(ks[4], (DEPTH, d, 6 * d), 0.5 * d ** -0.5),
        'b_mod': nrm(ks[5], (DEPTH, 6 * d), 0.02),
        'norm1_g': 1.0 + nrm(ks[6], (DEPTH, d), 0.02),
        'norm2_g': 1.0 + nrm(ks[7], (DEPTH, d), 0.02),
        'w_in': nrm(ks[8], (DEPTH, d, PROJ_W), d ** -0.5),
        'lam_q1': nrm(ks[9], (DEPTH, HEAD_DIM_2), LAMBDA_STD),
        'lam_k1': nrm(ks[10], (DEPTH, HEAD_DIM_2), LAMBDA_STD),
        'lam_q2': nrm(ks[11], (DEPTH, HEAD_DIM_2), LAMBDA_STD),
        'lam_k2': nrm(ks[12], (DEPTH, HEAD_DIM_2), LAMBDA_STD),
        'subln_g': 1.0 + nrm(ks[13], (DEPTH, 2 * HEAD_DIM_2), 0.02),
        'w_attn_out': nrm(ks[14], (DEPTH, V_W, d), V_W ** -0.5),
        'w_four_out': nrm(ks[15], (DEPTH, F_W, d), F_W ** -0.5),
        'w_out': nrm(ks[16], (DEPTH, d, d), d ** -0.5),
        'w_router_group': nrm(ks[17], (DEPTH, d, N_GROUPS), d ** -0.5),
        'b_router_group': nrm(ks[18], (DEPTH, N_GROUPS), 0.01),
        'w_router_expert': nrm(ks[19], (DEPTH, d, N_EXPERTS), d ** -0.5),
        'b_router_expert': nrm(ks[20], (DEPTH, N_EXPERTS), 0.01),
        'w_exp_gate': nrm(ks[21], (DEPTH, N_EXPERTS, d, EXPERT_HIDDEN), d ** -0.5),
        'w_exp_up': nrm(ks[22], (DEPTH, N_EXPERTS, d, EXPERT_HIDDEN), d ** -0.5),
        'w_exp_down': nrm(ks[23], (DEPTH, N_EXPERTS, EXPERT_HIDDEN, d), EXPERT_HIDDEN ** -0.5),
        'final_g': 1.0 + nrm(ks[24], (d,), 0.02),
    }

def second_block(x, c, ctx, c_ctx, w_mod, b_mod, norm1_g, norm2_g, w_in, lam_q1, lam_k1, lam_q2, lam_k2,
              subln_g, w_attn_out, w_four_out, w_out, w_router_group, b_router_group, w_router_expert,
              b_router_expert, w_exp_gate, w_exp_up, w_exp_down, final_g):
    n = x.shape[1]
    rows = n // GRID_W
    ang_row, ang_col = axial_angles(rows)
    x_lat, x_ctx = x, ctx
    for l in range(DEPTH):
        update_ctx = l < DEPTH - 1
        lam_init = 0.8 - 0.6 * math.exp(-0.3 * l)
        lam = (jnp.exp(jnp.sum(lam_q1[l].astype(jnp.float32) * lam_k1[l].astype(jnp.float32)))
               - jnp.exp(jnp.sum(lam_q2[l].astype(jnp.float32) * lam_k2[l].astype(jnp.float32)))
               + lam_init)
        sh1, sc1, g1, sh2, sc2, g2 = [m[:, None, :] for m in jnp.split(jax.nn.silu(c) @ w_mod[l] + b_mod[l], 6, axis=-1)]
        csh1, csc1, cg1, csh2, csc2, cg2 = jnp.split(jax.nn.silu(c_ctx) @ w_mod[l] + b_mod[l], 6, axis=-1)

        h_c = modulate(rmsnorm(x_ctx, norm1_g[l]), csh1, csc1)
        if update_ctx:
            q_c, k_c, v_c, f_c, ga_c, gf_c = split_proj(h_c @ w_in[l])
        else:
            kv_c = h_c @ w_in[l][:, K_OFF:F_OFF]
            k_c = kv_c[..., :QK_W].reshape(x_ctx.shape[0], x_ctx.shape[1], N_HEADS, 2, HEAD_DIM_2)
            v_c = kv_c[..., QK_W:].reshape(x_ctx.shape[0], x_ctx.shape[1], N_HEADS, 2 * HEAD_DIM_2)
        h_l = modulate(rmsnorm(x_lat, norm1_g[l]), sh1, sc1)
        q_l, k_l, v_l, f_l, ga_l, gf_l = split_proj(h_l @ w_in[l])
        q_l = axial_rope(q_l, ang_row, ang_col)
        k_l = axial_rope(k_l, ang_row, ang_col)
        k_all = jnp.concatenate([k_c, k_l], axis=1)
        v_all = jnp.concatenate([v_c, v_l], axis=1)
        heads_l = blocked_latent_attention(q_l, k_all, v_all, lam)
        mix_l = merge_branches(heads_l, f_l, ga_l, gf_l, subln_g[l], lam_init, w_attn_out[l], w_four_out[l], w_out[l])
        x_lat = x_lat + g1 * mix_l
        if update_ctx:
            heads_c = diff_attend(q_c, k_c, v_c, lam)
            mix_c = merge_branches(heads_c, f_c, ga_c, gf_c, subln_g[l], lam_init, w_attn_out[l], w_four_out[l], w_out[l])
            x_ctx = x_ctx + cg1 * mix_c

        h2_l = modulate(rmsnorm(x_lat, norm2_g[l]), sh2, sc2)
        x_lat = x_lat + g2 * hier_moe(h2_l, w_router_group[l], b_router_group[l], w_router_expert[l],
                                      b_router_expert[l], w_exp_gate[l], w_exp_up[l], w_exp_down[l])
        if update_ctx:
            h2_c = modulate(rmsnorm(x_ctx, norm2_g[l]), csh2, csc2)
            x_ctx = x_ctx + cg2 * hier_moe(h2_c, w_router_group[l], b_router_group[l], w_router_expert[l],
                                          b_router_expert[l], w_exp_gate[l], w_exp_up[l], w_exp_down[l])
    return rmsnorm(x_lat, final_g)


def setup_inputs(seed=0):
    out = dict(first_inputs(seed))
    for name, value in second_inputs(seed + 1).items():
        if name != "x":
            out[name + "_2"] = value
    return out


def reference(
    x, norm_ffn1, ffn1_gate, ffn1_up, ffn1_down, norm_mix, w_in, sb_q_norm, sb_k_norm,
    sb_out_norm, rw_mu, rw_w0, rw_w2, rw_a0, rw_a2, rw_g2, rw_k_k, rw_k_a, rw_r_k, rw_ln_w,
    rw_ln_b, w_out, norm_ffn2, ffn2_gate, ffn2_up, ffn2_down, c_2, ctx_2, c_ctx_2, w_mod_2,
    b_mod_2, norm1_g_2, norm2_g_2, w_in_2, lam_q1_2, lam_k1_2, lam_q2_2, lam_k2_2, subln_g_2,
    w_attn_out_2, w_four_out_2, w_out_2, w_router_group_2, b_router_group_2, w_router_expert_2,
    b_router_expert_2, w_exp_gate_2, w_exp_up_2, w_exp_down_2, final_g_2,
):
    x = first_block(
        x, norm_ffn1, ffn1_gate, ffn1_up, ffn1_down, norm_mix, w_in, sb_q_norm, sb_k_norm,
        sb_out_norm, rw_mu, rw_w0, rw_w2, rw_a0, rw_a2, rw_g2, rw_k_k, rw_k_a, rw_r_k, rw_ln_w,
        rw_ln_b, w_out, norm_ffn2, ffn2_gate, ffn2_up, ffn2_down,
    )
    return second_block(
        x, c_2, ctx_2, c_ctx_2, w_mod_2, b_mod_2, norm1_g_2, norm2_g_2, w_in_2, lam_q1_2,
        lam_k1_2, lam_q2_2, lam_k2_2, subln_g_2, w_attn_out_2, w_four_out_2, w_out_2,
        w_router_group_2, b_router_group_2, w_router_expert_2, b_router_expert_2, w_exp_gate_2,
        w_exp_up_2, w_exp_down_2, final_g_2,
    )


_drawn_inputs = setup_inputs


def setup_inputs(seed=0):
    import zlib

    import numpy as np

    out = dict(_drawn_inputs(seed))
    spreads = {}
    factors = {'sb_q_norm': 3.624,
     'sb_k_norm': 3.914,
     'rw_w2': 5.597,
     'rw_a0': 3.681,
     'rw_k_k': 4.615,
     'rw_k_a': 3.308,
     'rw_ln_w': 3.91,
     'rw_ln_b': 8.0,
     'norm_ffn2': 3.319,
     'b_mod_2': 3.524,
     'norm1_g_2': 8.0,
     'norm2_g_2': 6.545,
     'lam_q1_2': 64.0,
     'lam_k1_2': 64.0,
     'lam_q2_2': 5.192,
     'lam_k2_2': 4.702,
     'subln_g_2': 8.0,
     'b_router_group_2': 8.0,
     'b_router_expert_2': 8.0,
     'final_g_2': 8.106}
    for name, (base, spread) in spreads.items():
        noise = np.random.default_rng([zlib.crc32(name.encode()), seed]).standard_normal(out[name].shape)
        drawn = base * np.exp(spread * noise) if base else spread * noise
        out[name] = __import__('jax').numpy.asarray(drawn.astype(out[name].dtype))
    for name, factor in factors.items():
        out[name] = (out[name] * factor).astype(out[name].dtype)
    return out
```

```python
from contextlib import ExitStack

import numpy as np

import concourse.bass as bass
from concourse import mybir

P = 128
F32 = mybir.dt.float32
F32R = mybir.dt.float32r
U32 = mybir.dt.uint32
ACT = mybir.ActivationFunctionType
ALU = mybir.AluOpType
AX_X = mybir.AxisListType.X

T = 256
TT = T // P
D = 1024
KT = D // P
D_FF = 2816
FFC = D_FF // 256
HD = 64
CH = 64
NCH = T // CH
E = 16
EPG = 4
EH = 512
EPS = 1e-6
LNX_EPS = 64e-5
DECAY = float(np.exp(-0.5))
LAM_INIT = 0.8 - 0.6

SLOT = 2048
RING = 6
HI_RING = 3

CONSTS = {}


def _columns(name, n, _at=[0]):
    CONSTS[name] = (_at[0], n)
    _at[0] += n
    return _at[0]


for _n, _w in (("ident", 128), ("eps", 2), ("head_mean", 128), ("ones", 128), ("neg_tri", 128), ("neg_ones", 128),
               ("causal", 384), ("causal_add", 384), ("levels", 6 * 128), ("strict", 64), ("incl", 64),
               ("cos", 256), ("sin", 256), ("dft_d", 256), ("dft_n", 1024), ("iota", 64), ("rev", 16),
               ("eye_st", 64), ("half_bd", 128), ("half", 2), ("neg_half", 2)):
    N_CONST = _columns(_n, _w)


def constant_table():
    c = np.zeros((P, N_CONST), np.float64)

    def put(name, a):
        at, n = CONSTS[name]
        c[:, at:at + n] = np.asarray(a).reshape(P, n)

    i = np.arange(P)
    put("ident", np.eye(P))
    put("head_mean", (i[:, None] // HD == i[None, :] // HD) / HD)
    put("ones", np.ones((P, P)))
    put("neg_tri", -1.0 * (i[:, None] >= i[None, :]))
    put("neg_ones", -np.ones((P, P)))
    strict = (i[:, None] < i[None, :]) * 1.0
    put("causal", np.concatenate([strict, np.ones((P, P)), strict], 1))
    put("causal_add", np.concatenate([strict - 1, np.zeros((P, P)), strict - 1], 1) * 1e30)
    s, t = (i % CH)[:, None], np.arange(CH)[None, :]
    lev = [(s // (2 * b) == t // (2 * b)) & (s % (2 * b) < b) & (t % (2 * b) >= b) for b in (1, 2, 4, 8, 16, 32)]
    half_bd = (i[:, None] // CH == i[None, :] // CH) * 1.0
    put("levels", np.concatenate([np.tile(m, (1, 2)) * half_bd for m in lev], 1))
    put("half_bd", half_bd)
    put("eps", np.tile([EPS, LNX_EPS], (P, 1)))
    put("eye_st", s == t)
    put("strict", s < t)
    put("incl", s <= t)
    inv = (1.0 / (np.float32(10000.0) ** (np.arange(16, dtype=np.float32) / np.float32(16)))).astype(np.float32)
    tok = np.arange(T)
    within = i % HD
    pos = np.where((within < 32)[:, None], (tok // 64)[None, :], (tok % 64)[None, :]).astype(np.float32)
    ang = (pos * inv[within % 16][:, None]).astype(np.float32).astype(np.float64)
    put("cos", np.cos(ang))
    put("sin", np.where((within % 32 < 16)[:, None], -np.sin(ang), np.sin(ang)))
    k = np.outer(i, i) % P
    put("dft_d", np.concatenate([np.cos(2 * np.pi * k / P), np.sin(2 * np.pi * k / P)], 1) / np.sqrt(T * P))
    kn = 2 * np.pi * (np.outer(tok, tok) % T) / T
    dn = np.stack([np.cos(kn), -np.sin(kn)], 1).reshape(TT, P, 2, T)
    put("dft_n", dn.transpose(1, 0, 2, 3))
    half = (i[:, None] // CH == np.arange(2)[None, :]) * 1.0
    put("half", half)
    put("neg_half", -half)
    put("iota", np.tile(np.arange(64), (P, 1)))
    put("rev", np.tile(16 - np.arange(16), (P, 1)))
    return c.astype(np.float32)


VECS = [("norm_ffn1", 8), ("norm_mix", 8), ("norm_ffn2", 8), ("norm1_g_2", 8), ("norm2_g_2", 8),
        ("sb_q_norm", 1), ("sb_k_norm", 1), ("sb_out_norm", 4), ("rw_mu", 14), ("rw_w0", 4), ("rw_a0", 4),
        ("rw_k_k", 4), ("rw_k_a", 4), ("rw_r_k", 4), ("rw_ln_w", 4), ("rw_ln_b", 4), ("b_mod_2", 48),
        ("subln_g_2", 1), ("c_2", 8), ("c_ctx_2", 8), ("lam_q1_2", 1), ("lam_q2_2", 1), ("lam_k1_2", 1),
        ("lam_k2_2", 1)]
VEC_AT, _a = {}, 0
for _n, _w in VECS:
    VEC_AT[_n] = (_a, _w)
    _a += _w
N_VEC = _a
ROWS = [("final_g_2", 1024), ("b_router_group_2", 4), ("b_router_expert_2", 16), ("b_mod_2", 6144)]
ROW_AT, _a = {}, 0
for _n, _w in ROWS:
    ROW_AT[_n] = (_a, _w)
    _a += _w
N_ROW = _a


def pack_vectors(inputs):
    v = np.zeros((P, N_VEC), np.float32)
    for name, (at, n) in VEC_AT.items():
        a = np.asarray(inputs[name]).reshape(-1)
        if a.size == HD:
            a = np.concatenate([a, a]) if name.startswith("sb_") else np.concatenate([a, np.zeros(HD, np.float32)])
        v[:, at:at + n] = a.reshape(n, P).T
    r = np.zeros((1, N_ROW), np.float32)
    for name, (at, n) in ROW_AT.items():
        r[0, at:at + n] = np.asarray(inputs[name]).reshape(-1)
    return v, r


MATRICES = ["x", "ffn1_gate", "ffn1_up", "ffn1_down", "w_in", "rw_w2", "rw_a2", "rw_g2", "w_out", "ffn2_gate",
            "ffn2_up", "ffn2_down", "ctx_2", "w_mod_2", "w_in_2", "w_attn_out_2", "w_four_out_2", "w_out_2",
            "w_router_group_2", "w_router_expert_2", "w_exp_gate_2", "w_exp_up_2", "w_exp_down_2"]


def build(nc, a, out):
    ctx = ExitStack()
    with ctx:
        shared = {
            "act_mix": [("tanh_w", 1), ("sig_g", 1), ("sig_w", 4), ("sig_a", 4), ("decays", 3), ("w_end", 1),
                        ("kk_sq", 1), ("g_copied", 2), ("kk_norm", 1), ("q_sq", 1), ("b_tok", 2), ("k_sq", 1),
                        ("q_root", 1), ("k_tok", 2), ("k_root", 1)],
            "act_rms": [("sbo_sq", 2), ("sbo_root", 1), ("y_sq", 2), ("y_root", 1)],
            "act_tail": [("dft_mid", 4), ("heads_sq", 2), ("four_t", 2), ("heads_root", 4), ("gates_sig", 2),
                         ("route_exp", 2)],
            "pe_mix": [("lora_w", 2), ("lora_a", 2), ("lora_g", 2), ("kk_ms", 2), ("bonus_sum", 2),
                       ("v_turned", 2), ("b_turned", 2), ("k_turned", 2), ("q_ms", 2), ("k_ms", 2),
                       ("gram_b", 4), ("gram_k", 4)],
            "pe_rms": [("sbo_ms", 2), ("y_mean", 2), ("y_var", 2)],
            "pe_tail": [("dft_1", 4), ("dft_2", 2), ("heads_ss", 4), ("logits", 1), ("places", 1), ("moe_sum", 1),
                        ("final_gain", 1)],
                        "dve_mix": [("cum", 2), ("kk_raw", 4), ("bonus_prod", 1), ("kk_unit", 1), ("b_bar", 1), ("k_bar", 1),
                        ("arz", 4), ("bonus_v", 1), ("v_tok", 4), ("qz", 2), ("kn", 1), ("gram_b_masked", 8),
                        ("gram_k_masked", 8)],
            "dve_out": [("sb_out", 4), ("y_centred", 2), ("rw_out", 1)],
            "dve_tail": [("lam_prod", 1), ("head_gain", 1), ("heads_normed", 2), ("y_four", 2), ("y_mix", 4),
                         ("route_max", 1), ("route_diff", 1), ("chosen", 1), ("tables", 10), ("rounds", 1)],
        }
        for what, count, tags in (("ss", 2, ("n1", "n2", "n3", "ctx", "n4", "n5", "n6")),
                                  ("root", 2, ("n1", "n2", "n3", "ctx", "n4", "n5", "n6")),
                                  ("scaled", 2, ("n1", "n2", "n3", "ctx", "n4", "n5")),
                                  ("turned", 4, ("n1", "n2", "n3", "ctx", "n4", "n5")),
                                  ("cols_a", 4, ("n2", "ctx", "n4", "n5")),
                                  ("cols_v", 4, ("n2", "ctx", "n4", "n5")),
                                  ("hi", 8, ("n1", "n3")), ("lo", 8, ("n1", "n3")),
                                  ("silu", FFC, ("f1", "f2")), ("hidden", FFC, ("f1", "f2")),
                                  ("prod", FFC, ("f1", "f2")), ("hid_hi", FFC, ("f1", "f2"))):
            shared["each_" + what] = [(f"{tag}_{what}", count) for tag in tags]
        shared["mod_half"] = [("mod_half_1", 16 * 2), ("mod_half_2", 8 * 2 * 2)]
        shared["mod_prod"] = [("mod_prod_1", 16), ("mod_prod_2", 16)]
        shared["mod_kept"] = [("mod_kept_1", 16), ("mod_kept_2", 16)]
        sems, base = {}, {}
        for group, events in shared.items():
            count = 0
            for name, n in events:
                base[name] = (group, count)
                count += n

        def S(name):
            group = base.get(name, (name, 0))[0]
            if group not in sems:
                sems[group] = ctx.enter_context(nc.semaphore(group))
            return sems[group]

        def W(name, n):
            before = base.get(name, (name, 0))[1]
            return S(name), n + before if before else n

        def sb(name, shape):
            return ctx.enter_context(nc.sbuf_tensor(name, shape, F32))

        def with_r(name, shape):
            whole = sb(name, shape)
            offset = nc.sbuf_base - 4 * int(np.prod(shape[1:]))
            return whole, nc.alloc_sbuf_tensor_at(name + "_r", shape, F32R, offset=offset)

        ring, ring_r = with_r("ring", [P, RING * SLOT])
        cst = sb("cst", [P, N_CONST])
        vec = sb("vec", [P, N_VEC])
        x = sb("x", [P, TT, D])
        hall, hall_r = with_r("hall", [P, 2, KT, T])
        gb = sb("gb", [P, 2, D])
        arena, arena_r = with_r("arena", [P, 27 * 1024])
        modc = sb("modc", [P, 48])
        small = sb("small", [P, 72])
        ps = ctx.enter_context(nc.psum_tensor("ps", [P, 8, 512], F32))

        def C(name):
            at, n = CONSTS[name]
            return cst[:, at:at + n]

        def V(name, i=0):
            at, _ = VEC_AT[name]
            return vec[:, at + i:at + i + 1]

        def A(blk, n=1024, off=0):
            return arena[:, blk * 1024 + off:blk * 1024 + off + n]

        def AR(blk, n=1024, off=0):
            return arena_r[:, blk * 1024 + off:blk * 1024 + off + n]

        def tiles(blk, k=4, n=T, off=0):
            return A(blk, k * n, off).rearrange("p (k n) -> p k n", k=k)

        ident, ones, head_mean = C("ident"), C("ones"), C("head_mean")

        def slot(n):
            return ring[:, (n % RING) * SLOT:(n % RING + 1) * SLOT]

        def cols(n):
            return slot(n).rearrange("p (k n) -> p k n", k=KT)

        def rows(n):
            return slot(n).rearrange("p (k n) -> p k n", k=2)

        def hi(n):
            blocks = (15, 13, 17) if n < N_WIN2 else (15, 0, 17) if n < N_GATES else (19, 0, 21)
            return AR(blocks[n % HI_RING], SLOT)

        def lo(n):
            return ring_r[:, (n % RING) * SLOT:(n % RING + 1) * SLOT]

        def n_split(n):
            return n if n < N_WIN else n - (N_FFN2 - N_WIN)

        def hi_cols(n):
            return hi(n).rearrange("p (k n) -> p k n", k=KT)

        def lo_cols(n):
            return lo(n).rearrange("p (k n) -> p k n", k=KT)

        def hi_rows(n):
            return hi(n).rearrange("p (k n) -> p k n", k=2)

        def lo_rows(n):
            return lo(n).rearrange("p (k n) -> p k n", k=2)

        def at(static, it, per):
            return static if it is None else it * per + static

        tag_of_norm = {"f1": "n1", "f2": "n3"}
        norm_after = {"n2": ("x1_done", 4), "n3": ("x2_done", 4), "n4": ("x3_done", 4), "n5": ("x4_done", 4)}

        N_FFN1 = 0
        N_WIN = N_FFN1 + 3 * FFC
        N_WOUT = N_WIN + 13
        N_FFN2 = N_WOUT + 4
        N_WIN2 = N_FFN2 + 3 * FFC
        N_GATES = N_WIN2 + 14
        N_FO = N_WIN2 + 22
        N_AO = N_FO + 2
        N_O2 = N_AO + 4
        N_EXP = N_O2 + 4

        def n_gate(i):
            return 0 if i == 0 else 3 * i - 1

        def n_up(i):
            return 1 if i == 0 else 3 * i

        def n_down(i):
            return 3 * i + 4 if i < FFC - 1 else 3 * FFC - 1

        def ffn_chunks(i):
            use = [n_gate(i), n_up(i)] + ([n_down(i - 1)] if i else [])
            return [n for n in use if n + HI_RING < 3 * FFC]

        FFN_PEEL = 3
        FFN_LOOP = (FFC - 2 - FFN_PEEL) // 2
        RW_ORDER = (6, 2, 3, 0, 1, 4, 5)

        wmod, wmod_2 = ([A(j, 2048).rearrange("p (k n) -> p k n", k=KT) for j in js] for js in ((0, 2), (4, 6)))
        mod_acc, mod_acc_2, ctx_acc = A(4, 4096), A(8, 2048), A(10, 2048)
        mod_prod = [A(2, 2048).rearrange("p (k n) -> p k n", k=KT)] * 2
        sg = A(19).rearrange("p (b n) -> p b n", b=2)
        hid, hid_lo, hid_hi = (m.rearrange("p (b f n) -> p b f n", b=2, f=2) for m in (A(20), AR(20), AR(12)))
        h_lo, h_hi = hall_r[:, 0], hall_r[:, 1]
        xn = A(25, 2048).rearrange("p (t n) -> p t n", t=TT)
        gate_rows = A(25, 2048)
        rw_x = {0: tiles(0), 4: tiles(1), 8: tiles(2)}
        xr, xk, xv = rw_x[0], rw_x[4], rw_x[8]
        x_wa, x_g, t_w, s_g = (A(3, 256, 256 * j) for j in range(4))
        ubuf = A(4, 1028).rearrange("p (b f n) -> p b f n", b=2, f=2)
        ushift = A(4, 512, 1028).rearrange("p (f n) -> p f n", f=2)
        sig_w, cum, av, w_in_, w_inv, w_ex, g_rw = (tiles(j) for j in (6, 7, 8, 9, 10, 11, 12))
        kk, sq, kf = tiles(13), tiles(14), tiles(15)
        arz = A(16, 4096).rearrange("p (q k c j n) -> p q k c j n", q=2, k=4, c=NCH, j=2)
        b_bar, k_bar, bonus = tiles(20), tiles(21), tiles(22)
        vz = A(0, 2048).rearrange("p (q t n) -> p q t n", q=2, t=TT)
        b_tok = A(13).rearrange("p (t n) -> p t n", t=TT)
        k_tok = A(23).rearrange("p (t n) -> p t n", t=TT)
        ab_t, rb_t, ak_t, rk_t = (A(j).rearrange("p (i n) -> p i n", n=CH) for j in (6, 7, 8, 9))
        q_raw, kn = tiles(23), tiles(24)
        v_sb = A(25).rearrange("p (t n) -> p t n", t=TT)
        qz = A(4, 2048).rearrange("p (q k n) -> p q k n", q=2, k=4)
        sb_e, sb_sp, sb_att = ([A(j, 768).rearrange("p (h n) -> p h n", h=2) for j in js]
                               for js in ((10, 20), (11, 21), (15, 3)))
        mix = [tiles(26), tiles(2)]
        inv_t, inv_tt, inv_x = (A(j).rearrange("p (i n) -> p i n", n=CH) for j in (10, 11, 15))
        tt_bd, x_bd, lev_bd = (A(j, 2048).rearrange("p (i n) -> p i n", n=P) for j in (4, 24, 20))
        rhs_z, u_z = (A(j).rearrange("p (q n) -> p q n", q=2) for j in (20, 21))
        state = A(10, 512).rearrange("p (b k n) -> p b k n", b=2, k=4)
        state_sum = A(10, 256, 512).rearrange("p (k n) -> p k n", k=4)
        y_rw, y_c, y_n = tiles(15), tiles(24), tiles(4)
        w_end = small[:, 0:16].rearrange("p (k c) -> p k c", k=4)
        ssum, rstd = small[:, 16:18], small[:, 18:20]
        sb_sq_q, sb_sq_k = tiles(14), tiles(3)
        small_w = {"w2": A(16, 512), "a2": A(16, 512), "g2": A(16, 512, 512)}
        r_scan = A(14)

        ctx_x = A(0, 2048).rearrange("p (t n) -> p t n", t=TT)
        qz2 = A(2, 4096).rearrange("p (i h n) -> p i h n", i=2, h=8)
        k_all = A(6, 4096).rearrange("p (h n) -> p h n", h=8)
        v_all = A(10, 4096).rearrange("p (t n) -> p t n", t=4)
        f_t, four_t = tiles(14), tiles(14)
        ga, gf = (A(j, 2048).rearrange("p (k n) -> p k n", k=8) for j in (15, 17))
        rope_raw, rope_sh = ([A(j + g, 512).rearrange("p (f n) -> p f n", f=2) for g in range(2)] for j in (19, 21))
        probs = [A(19 + j).rearrange("p (i n) -> p i n", i=2) for j in range(4)]
        att = [A(23 + j).rearrange("p (t n) -> p t n", t=TT) for j in range(2)]
        att_t = [tiles(j) for j in range(2)]
        heads = A(25, 2048).rearrange("p (h n) -> p h n", h=8)
        heads_sq = A(23, 2048).rearrange("p (h n) -> p h n", h=8)
        heads_rms = A(19, 2048).rearrange("p (h n) -> p h n", h=8)
        dft_mid = A(2, 2048).rearrange("p (t g n) -> p t g n", t=TT, g=4)
        y_mix = A(4, 2048).rearrange("p (k n) -> p k n", k=8)
        gated = A(6, 2048).rearrange("p (t n) -> p t n", t=TT)
        SLOTS = 64
        w_route, row_f = A(9, 160).rearrange("p (k n) -> p k n", k=KT), A(10, 1044)[0:1, :]
        h_sel = A(0).rearrange("p (k n) -> p k n", k=KT)
        hs, hs_t = A(1, 512), A(1, 512, 512).rearrange("p (k n) -> p k n", k=4)
        y_e = A(2)
        pick, pick_g = (A(3, 256, j).rearrange("p (t n) -> p t n", t=TT) for j in (0, 256))
        pick_t = A(3, 256, 512).rearrange("p (t n) -> p t n", t=TT)
        pos_tab, gate_tab = A(4, 132), A(4, 132, 132)
        n_rounds = A(4, 1, 264)
        rt = lambda j, n=32: A(8, n, 32 * j)
        zero_blk = A(7, 128)
        EPS_COL, LNX_COL = C("eps")[:, 0:1], C("eps")[:, 1:2]

        def banks(b0):
            return ps[:, b0:b0 + 2, :].rearrange("p b (f n) -> p (b f) n", f=2)

        block = ctx.enter_context(nc.Block())

        w_four = a["w_four_out_2"].rearrange("(k p) n -> p k n", p=P)
        w_gu = [a[k].rearrange("e (k p) n -> e p k n", p=P) for k in ("w_exp_gate_2", "w_exp_up_2")]
        w_dn = a["w_exp_down_2"].rearrange("e (k p) n -> e p k n", p=P)
        w_cols = {k: a[k].rearrange("(k p) n -> p k n", p=P) for k in
                  ("ffn1_gate", "ffn1_up", "w_in", "ffn2_gate", "ffn2_up", "w_mod_2", "w_in_2", "w_attn_out_2")}
        w_rows = {k: a[k].rearrange("(k p) n -> p k n", p=P) for k in
                  ("ffn1_down", "w_out", "ffn2_down", "w_out_2")}

        @block.sync
        def _(sp):
            def load(n, src, it=None, per=0):
                if n >= RING:
                    sp.wait_ge(*W("w_used", at(n - RING + 1, it, per)))
                view = slot(n).rearrange("p (k n) -> p k n", k=src.shape[1])
                sp.dma_start(view, src).then_inc(S(f"w_in_slot{n % RING}"), 16)

            def c256(name, c):
                return w_cols[name][:, :, bass.ds(c * 256, 256)]

            def r256(name, c):
                return w_rows[name][:, bass.ds(c * 2, 2), :]

            def ffn(n0, tag):
                def chunk(i, it=None):
                    load(n0 + n_gate(i), c256(tag + "_gate", at(i, it, 2)), it, 6)
                    load(n0 + n_up(i), c256(tag + "_up", at(i, it, 2)), it, 6)
                    if i >= 1:
                        load(n0 + n_down(i - 1), r256(tag + "_down", at(i - 1, it, 2)), it, 6)

                for i in range(FFN_PEEL):
                    chunk(i)
                with sp.Fori(0, FFN_LOOP) as it:
                    chunk(FFN_PEEL, it)
                    chunk(FFN_PEEL + 1, it)
                for i in range(FFN_PEEL + 2 * FFN_LOOP, FFC):
                    chunk(i)
                load(n0 + n_down(FFC - 1), r256(tag + "_down", FFC - 1))

            for t in range(TT):
                sp.dma_start(x[:, t, :], a["x"][t * P:(t + 1) * P, :]).then_inc(S(f"x_in{t}"), 16)
            ffn(N_FFN1, "ffn1")
            for j, c in enumerate([6 + c for c in RW_ORDER] + list(range(6))):
                load(N_WIN + j, c256("w_in", c))
            for c in range(4):
                load(N_WOUT + c, r256("w_out", c))
            ffn(N_FFN2, "ffn2")
            W2_ORDER = (4, 5, 6, 7, 0, 1, 2, 3) + tuple(range(8, 22))
            for j, c in enumerate(W2_ORDER):
                load(N_WIN2 + j, c256("w_in_2", c))
            for c in range(2):
                load(N_FO + c, w_four[:, :, c * 512:(c + 1) * 512])
            for c in range(4):
                load(N_AO + c, c256("w_attn_out_2", c))
            for c in range(4):
                load(N_O2 + c, r256("w_out_2", c))

            def expert_pair(e0, it):
                for e in range(2):
                    for w in range(2):
                        for c in range(2):
                            load(N_EXP + 4 * e + 2 * w + c,
                                 w_gu[w][bass.ds(e0 + e, 1), :, :, c * 256:(c + 1) * 256].squeeze(0), it, 12)
                for e in range(2):
                    for c in range(2):
                        load(N_EXP + 8 + 2 * e + c, w_dn[bass.ds(e0 + e, 1), :, 2 * c:2 * c + 2, :].squeeze(0), it, 12)

            sp.wait_ge(*W("rounds", 1))
            n_r = sp.value_load(n_rounds[0:1, 0:1].bitcast(U32), min_val=1, max_val=4)
            with sp.Fori(0, n_r) as r:
                with sp.Fori(0, E // 2) as pair:
                    expert_pair(pair * 2, r * (E // 2) + pair)
            sp.wait_ge(*W("final", 2))
            for t in range(TT):
                sp.dma_start(out[t * P:(t + 1) * P, :], xn[:, t, :]).then_inc(S("stored"), 16)
            sp.wait_ge(*W("stored", 16 * 2))

        @block.gpsimd
        def _(pool):
            def modulate(tag, places, pairs, first, vectors):
                n = len(vectors)

                def load(b, col):
                    pool.dma_start(places[b], w_cols["w_mod_2"][:, :, bass.ds(col, 256)]).then_inc(
                        S(f"wmod_in{b}_{tag}"), 16)

                def chunk(b, it, done, load_next=True):
                    before = 2 * done + b
                    for i, (prod, o) in enumerate(vectors):
                        prod = prod[b]
                        pool.wait_ge(*W("mod_prod_" + tag, it * (2 * n) + (before * n + i + 1)))
                        pool.tensor_tensor(prod[:, 0:4, :], prod[:, 0:4, :], prod[:, 4:8, :], ALU.add).then_inc(
                            S("mod_half_" + tag), 1)
                        pool.wait_ge(*W("mod_half_" + tag, it * (4 * n) + (2 * (before * n + i) + 1)))
                        pool.tensor_tensor(prod[:, 0:2, :], prod[:, 0:2, :], prod[:, 2:4, :], ALU.add).then_inc(
                            S("mod_half_" + tag), 1)
                        pool.wait_ge(*W("mod_half_" + tag, it * (4 * n) + (2 * (before * n + i) + 2)))
                        pool.tensor_tensor(o[:, bass.ds(it * 512 + (done * 512 + b * 256), 256)], prod[:, 0, :],
                                           prod[:, 1, :], ALU.add).then_inc(S("mod_kept_" + tag), 1)
                    pool.wait_ge(*W("mod_kept_" + tag, it * (2 * n) + (before + 1) * n))
                    if load_next:
                        load(b, it * 512 + (first + 512 * (done + 1) + b * 256))

                load(0, first)
                load(1, first + 256)
                with pool.Fori(0, pairs - 1) as it:
                    for b in range(2):
                        chunk(b, it, 0)
                for b in range(2):
                    chunk(b, 0, pairs - 1, False)

            pool.wait_ge(*W("n1_lo", 8))
            modulate("1", wmod, 8, 2 * D, [(wmod, mod_acc)])
            pool.wait_ge(*W("w_used", N_FFN1 + 3 * FFC))
            pool.memset(r_scan, 1.0).then_inc(S("reset_ones"), 1)
            pool.wait_ge(*W("reset_ones", 1))
            pool.memset(r_scan.rearrange("p (c n) -> p c n", n=CH)[:, :, 0:1], 0.0).then_inc(S("reset_mask"), 1)
            pool.wait_ge(*W("gates_summed", 4))
            pool.memset(ubuf[:, :, :, 0:1], 0.0).then_inc(S("ubuf_zero"), 1)

            def diagonal(o, src, mask, sem):
                pool.tensor_tensor(o.rearrange("p i (q n) -> p i q n", q=2),
                                   src.unsqueeze(2).broadcast_to([P, 8, 2, CH]),
                                   mask.rearrange("p (q n) -> p q n", q=2).unsqueeze(1).broadcast_to([P, 8, 2, CH]),
                                   ALU.mult).then_inc(S(sem), 1)

            pool.wait_ge(*W("gram_b_masked", 8))
            pool.wait_ge(*W("sb_sum", 4))
            for m in (inv_t, inv_tt):
                pool.tensor_copy(m, C("eye_st").unsqueeze(1).broadcast_to([P, 16, CH])).then_inc(S("inv_init"), 1)
            for t in range(TT):
                pool.tensor_copy(tt_bd[:, 8 * t:8 * t + 8, :], ident.unsqueeze(1).broadcast_to([P, 8, P])).then_inc(
                    S("tt_bd"), 1)
            for level in range(6):
                for t in range(TT):
                    i = 2 * level + t
                    if level:
                        pool.wait_ge(*W("inv_x", i - 1))
                    diagonal(lev_bd[:, 8 * t:8 * t + 8, :], ab_t[:, 8 * t:8 * t + 8, :],
                             C("levels")[:, level * P:(level + 1) * P], "lev_bd")
                    if 1 <= level < 5:
                        pool.wait_ge(*W("tt_added", i - 1))
                        diagonal(tt_bd[:, 8 * t:8 * t + 8, :], inv_tt[:, 8 * t:8 * t + 8, :], C("half_bd"), "tt_bd")
            pool.wait_ge(*W("inv_x", 12))
            pool.memset(A(20, 2048), 0.0).then_inc(S("u_zero"), 1)
            pool.wait_ge(*W("w_used", N_FFN2))
            modulate("2", wmod_2, 4, 0, [(mod_prod, ctx_acc), (wmod_2, mod_acc_2)])
            pool.wait_ge(*W("x4_done", 4))
            pool.memset(y_e, 0.0).then_inc(S("y_kept_v"), 1)
            pool.memset(pick_t, 0.0).then_inc(S("pick_t"), 1)
            pool.memset(zero_blk, 0.0).then_inc(S("zeros"), 1)

        @block.tensor
        def _(pe):
            def weight(n, it=None, per=0):
                pe.wait_ge(*W(f"w_in_slot{n % RING}", at(16 * (n // RING + 1), it, 16 * per // RING)))

            def split_weight(n, it=None, per=0):
                pe.wait_ge(*W("w_lo", at(n_split(n) + 1, it, per)))

            def mm(out_, lhsT, rhs, start=True, stop=True, group=False):
                return pe.matmul(out_, lhsT, rhs, start=start, stop=stop, skip_group_check=group)

            def norm_transposes(tag, b0=0, src=None):
                for t in range(TT):
                    pe.wait_ge(*W(tag + "_scaled", t + 1))
                    for k in range(KT):
                        m = pe.transpose(ps[:, b0 + k // 2, (k % 2) * T + t * P:(k % 2) * T + (t + 1) * P],
                                         (xn if src is None else src)[:, t, k * P:(k + 1) * P], ident)
                        if t == TT - 1 and k % 2:
                            m.then_inc(S(tag + "_turned"), 1)

            def normed(tag):
                pe.wait_ge(*W(tag + "_cols_v", 4))
                pe.wait_ge(*W(tag + "_cols_a", 4))

            def mm3(out_, w, h, start=True, stop=True, group=False):
                for i, j in ((0, 0), (1, 0), (0, 1)):
                    m = pe.matmul(out_, w[i], h[j], start=start and i + j == 0, stop=stop and j == 1,
                                  skip_group_check=group)
                return m

            def ffn(n0, tag):
                def half(n, bank, it, first=False):
                    split_weight(n, it, 6)
                    for f in range(2):
                        for k in range(KT):
                            if first and f == 0:
                                pe.wait_ge(*W(tag_of_norm[tag] + "_lo", k + 1))
                            m = mm3(ps[:, bank, f * T:(f + 1) * T],
                                    [w[:, k, f * P:(f + 1) * P] for w in (hi_cols(n), lo_cols(n))],
                                    [h_hi[:, k, :], h_lo[:, k, :]], start=k == 0, stop=k == KT - 1)
                    m.then_inc(S("w_used"), 1)

                def down(i, it=None):
                    n = n0 + n_down(i)
                    split_weight(n, it, 6)
                    pe.wait_ge(*W(tag + "_hidden", at(i + 1, it, 2)))
                    for f in range(2):
                        for t in range(TT):
                            for h in range(2):
                                m = mm3(ps[:, 4 + 2 * t + h, :],
                                        [z[:, i % 2, f, t * P:(t + 1) * P] for z in (hid_hi, hid_lo)],
                                        [w[:, f, h * 512:(h + 1) * 512] for w in (hi_rows(n), lo_rows(n))],
                                        start=i == 0 and f == 0, stop=i == FFC - 1 and f == 1, group=True)
                    m.then_inc(S("w_used"), 1)

                def chunk(i, it=None):
                    if i >= 2:
                        pe.wait_ge(*W(tag + "_silu", at(i - 1, it, 2)))
                    half(n0 + n_gate(i), 2 * (i % 2), it, i == 0)
                    if i >= 2:
                        pe.wait_ge(*W(tag + "_hidden", at(i - 1, it, 2)))
                    half(n0 + n_up(i), 2 * (i % 2) + 1, it)
                    if i >= 1:
                        down(i - 1, it)

                for i in range(FFN_PEEL):
                    chunk(i)
                with pe.Fori(0, FFN_LOOP) as it:
                    chunk(FFN_PEEL, it)
                    chunk(FFN_PEEL + 1, it)
                for i in range(FFN_PEEL + 2 * FFN_LOOP, FFC):
                    chunk(i)
                if n0 == N_FFN2:
                    pe.wait_ge(*W("mod_kept_2", 16))
                    pe.wait_ge(*W("f2_hidden", FFC))
                    mod_columns(0, mod_acc_2)
                    mod_columns(32, ctx_acc).then_inc(S("mod_sums"), 1)
                down(FFC - 1)

            def out_rows(n0, lhs, tag):
                for c in range(4):
                    weight(n0 + c)
                    for f in range(2):
                        for t in range(TT):
                            for h in range(2):
                                m = mm(ps[:, 4 + 2 * t + h, :], lhs(2 * c + f)[:, t * P:(t + 1) * P],
                                       rows(n0 + c)[:, f, h * 512:(h + 1) * 512],
                                       start=c == 0 and f == 0, stop=c == 3 and f == 1, group=True)
                    m.then_inc(S("w_used"), 1)

            def mod_columns(at_, sums):
                for k in range(16):
                    m = mm(ps[:, 0, at_ + k:at_ + k + 1], sums[:, k * P:(k + 1) * P], ones[:, 0:1])
                return m

            pe.wait_ge(*W("ident_in", 16))
            norm_transposes("n1", 4)
            ffn(N_FFN1, "f1")

            pe.wait_ge(*W("mod_kept_1", 16))
            pe.wait_ge(*W("consts", 16))
            pe.wait_ge(*W("gate_rows", 32))
            pe.wait_ge(*W("f1_hidden", FFC))
            mod_columns(16, mod_acc[:, D:3 * D]).then_inc(S("mod_sums"), 1)
            for g in range(2):
                for h in range(2):
                    bank = 1 + h if g == 0 else (3 if h == 0 else 0)
                    if bank == 0:
                        pe.wait_ge(*W("mod_cols", 1))
                    first = 3 * g * D + h * 512
                    mm(ps[:, bank, :], ones, mod_acc[:, first:first + 512], stop=False)
                    m = mm(ps[:, bank, :], ones[0:1, :], gate_rows[0:1, g * D + h * 512:g * D + h * 512 + 512],
                           start=False)
                    m.then_inc(S("gates_summed"), 1)

            pe.wait_ge(*W("gates_kept", 4))
            norm_transposes("n2")
            normed("n2")
            h_t = hall[:, 1]

            def project(j, token_major=False):
                n = N_WIN + j
                weight(n)
                if j >= 4:
                    pe.wait_ge(*W("win_copied", j - 3))
                for f in range(2):
                    for k in range(KT):
                        if token_major:
                            m = mm(ps[:, j % 4, f * 256:(f + 1) * 256], h_t[:, k, f * P:(f + 1) * P],
                                   cols(n)[:, k, :], start=k == 0, stop=k == KT - 1)
                        else:
                            m = mm(ps[:, j % 4, f * T:(f + 1) * T], cols(n)[:, k, f * P:(f + 1) * P], h_t[:, k, :],
                                   start=k == 0, stop=k == KT - 1)
                m.then_inc(S("w_used"), 1)

            lora_w, lora_a, lora_g = small_w["w2"], small_w["a2"], small_w["g2"]

            def four(b0, f, sem):
                for k in range(4):
                    m = f(ps[:, b0 + k // 2, (k % 2) * T:(k % 2 + 1) * T], k)
                    if k % 2:
                        m.then_inc(S(sem), 1)

            project(0)
            project(1)
            pe.wait_ge(*W("small_w", 48))
            pe.wait_ge(*W("x1_done", 4))
            pe.wait_ge(*W("tanh_w", 1))
            four(4, lambda o, k: mm(o, lora_w[0:64, k * P:(k + 1) * P], t_w[0:64, :]), "lora_w")
            four(6, lambda o, k: mm(o, lora_a[64:128, k * P:(k + 1) * P], x_wa[64:128, :]), "lora_a")
            project(2)
            project(3)
            pe.wait_ge(*W("sig_g", 1))
            pe.wait_ge(*W("sig_w", 4))
            four(4, lambda o, k: mm(o, lora_g[:, k * P:(k + 1) * P], s_g), "lora_g")
            project(4)
            pe.wait_ge(*W("kk_sq", 1))
            pe.wait_ge(*W("sig_a", 4))
            four(6, lambda o, k: mm(o, head_mean, sq[:, k, :]), "kk_ms")
            project(5)
            project(6)
            pe.wait_ge(*W("g_copied", 2))
            pe.wait_ge(*W("bonus_prod", 1))
            four(4, lambda o, k: mm(o, head_mean, bonus[:, k, :]), "bonus_sum")
            project(7)
            project(8)
            def by_token(src, b0, sem):
                for t in range(TT):
                    for k in range(4):
                        m = pe.transpose(ps[:, b0 + t, k * P:(k + 1) * P], src[:, k, t * P:(t + 1) * P], ident)
                    m.then_inc(S(sem), 1)

            pe.wait_ge(*W("kk_norm", 1))
            pe.wait_ge(*W("shifted", 7))
            by_token(xv, 6, "v_turned")
            project(9)
            pe.wait_ge(*W("bonus_v", 1))
            pe.wait_ge(*W("b_bar", 1))
            by_token(b_bar, 4, "b_turned")
            project(10)
            pe.wait_ge(*W("v_tok", 4))
            pe.wait_ge(*W("k_bar", 1))
            by_token(k_bar, 6, "k_turned")
            project(11, True)
            project(12, True)

            pe.wait_ge(*W("b_tok", 2))
            pe.wait_ge(*W("q_sq", 1))
            four(4, lambda o, k: mm(o, head_mean, sb_sq_q[:, k, :]), "q_ms")
            pe.wait_ge(*W("k_tok", 2))
            pe.wait_ge(*W("k_sq", 1))
            four(6, lambda o, k: mm(o, head_mean, sb_sq_k[:, k, :]), "k_ms")

            def gram(src, t, b0, sem):
                for h in range(8):
                    for c in range(2):
                        m = mm(ps[c * CH:(c + 1) * CH, b0 + h // 4, (h % 4) * P:(h % 4 + 1) * P],
                               src[:, h // 2, (2 * t + c) * CH:(2 * t + c + 1) * CH],
                               arz[:, h % 2, h // 2, 2 * t + c, :, :])
                    if h % 4 == 3:
                        m.then_inc(S(sem), 1)

            pe.wait_ge(*W("arz", 4))
            pe.wait_ge(*W("win_copied", 13))
            gram(b_bar, 0, 0, "gram_b")
            gram(b_bar, 1, 2, "gram_b")
            pe.wait_ge(*W("qz", 2))
            pe.wait_ge(*W("kn", 1))
            gram(k_bar, 0, 4, "gram_k")
            gram(k_bar, 1, 6, "gram_k")

            def sb_scores(p):
                g = p % 2
                if p < 2:
                    pe.wait_ge(*W("gram_b_masked", 4 * (p + 1)))
                else:
                    pe.wait_ge(*W("sb_expo", p - 1))
                for h in range(2):
                    mm(ps[:, 2 * g + h, 0:256], kn[:, p, 0:P], qz[:, h, p, :], group=True)
                    m = mm(ps[:, 2 * g + h, 256:384], kn[:, p, P:T], qz[:, h, p, P:T], start=False, group=True)
                m.then_inc(S("sb_z"), 1)

            def sb_sums(p):
                g = p % 2
                pe.wait_ge(*W("sb_sp", p + 1))
                for h in range(2):
                    sp_ = sb_sp[g][:, h, :]
                    mm(ps[:, 2 * g + h, 0:256], C("neg_tri"), sp_[:, 0:256], start=False, group=True)
                    mm(ps[:, 2 * g + h, 128:256], C("neg_ones"), sp_[:, 256:384], start=False, group=True)
                    m = mm(ps[:, 2 * g + h, 256:384], C("neg_tri"), sp_[:, 256:384], start=False, group=True)
                m.then_inc(S("sb_sum"), 1)

            def sb_values(p):
                g = p % 2
                pe.wait_ge(*W("sb_att", p + 1))
                if p == 0:
                    pe.wait_ge(*W("gram_k_masked", 4))
                for h in range(2):
                    o = ps[h * HD:(h + 1) * HD, 4 + p // 2, (p % 2) * T:(p % 2 + 1) * T]
                    v_ = v_sb[:, :, (2 * p + h) * HD:(2 * p + h + 1) * HD]
                    mm(o, v_[:, 0, :], sb_att[g][:, h, 0:256], group=True)
                    m = mm(o[:, P:T], v_[:, 1, :], sb_att[g][:, h, 256:384], start=False, group=True)
                m.then_inc(S("sb_o"), 1)

            sb_scores(0)
            sb_scores(1)
            for p in range(4):
                sb_sums(p)
                if p >= 1:
                    sb_values(p - 1)
                if p + 2 < 4:
                    sb_scores(p + 2)
            sb_values(3)
            pe.wait_ge(*W("sbo_sq", 2))
            pe.wait_ge(*W("gram_k_masked", 8))
            four(6, lambda o, k: mm(o, head_mean, sq[:, k, :]), "sbo_ms")

            def inv(level, t, what):
                for h in range(8):
                    i = 8 * t + h
                    if what == "x":
                        m = mm(ps[:, t, h * CH:(h + 1) * CH], lev_bd[:, i, :], inv_t[:, i, :])
                    elif what == "t":
                        m = mm(ps[:, 2, h * CH:(h + 1) * CH], tt_bd[:, i, :], inv_x[:, i, :])
                    else:
                        m = mm(ps[:, 3, h * CH:(h + 1) * CH], x_bd[:, i, :], inv_tt[:, i, :])
                m.then_inc(S("inv_" + what), 1)

            n = 0
            for level in range(6):
                for t in range(TT):
                    pe.wait_ge(*W("lev_bd", 2 * level + t + 1))
                    if level == 0:
                        pe.wait_ge(*W("inv_init", 2))
                        pe.wait_ge(*W("sb_expo", 4))
                    else:
                        pe.wait_ge(*W("t_added", 2 * level + t - 1))
                    inv(level, t, "x")
                for t in range(TT):
                    if level < 5:
                        pe.wait_ge(*W("x_kept", 2 * level + t + 1))
                        pe.wait_ge(*W("tt_bd", 2 * level + t + 1))
                        if 2 * level + t:
                            pe.wait_ge(*W("t_added", 2 * level + t))
                        inv(level, t, "t")
                    pe.wait_ge(*W("x_bd", 2 * (2 * level + t + 1)))
                    if 2 * level + t:
                        pe.wait_ge(*W("tt_added", 2 * level + t))
                    inv(level, t, "tt")

            for c in range(NCH):
                t, base = c // 2, (c % 2) * CH
                rows_ = slice(base, base + CH)
                pe.wait_ge(*W("tt_added", 12))
                if c:
                    pe.wait_ge(*W("state", c))
                for h in range(8):
                    o = ps[rows_, 0, h * CH:(h + 1) * CH]
                    if c:
                        mm(o, arz[:, h % 2, h // 2, c, 0, :], state[:, c % 2, h // 2, :], stop=False)
                    m = mm(o, ak_t[:, 8 * t + h, :], vz[:, c % 2, t, h * HD:(h + 1) * HD], start=c == 0)
                m.then_inc(S("rec_rhs"), 1)
                pe.wait_ge(*W("rhs_kept", c + 1))
                for h in range(8):
                    m = mm(ps[rows_, 1, h * CH:(h + 1) * CH], inv_tt[:, 8 * t + h, :],
                           rhs_z[:, c % 2, h * HD:(h + 1) * HD])
                m.then_inc(S("rec_u"), 1)
                pe.wait_ge(*W("u_kept", c + 1))
                if c == 0:
                    pe.wait_ge(*W("sb_out", 4))
                if c < NCH - 1:
                    for h in range(8):
                        o = ps[(h % 2) * HD:(h % 2 + 1) * HD, 4, (h // 2) * HD:(h // 2 + 1) * HD]
                        mm(o, b_tok[:, t, h * HD:(h + 1) * HD], u_z[:, c % 2, h * HD:(h + 1) * HD], stop=False)
                        m = mm(o, k_tok[:, t, h * HD:(h + 1) * HD], vz[:, c % 2, t, h * HD:(h + 1) * HD],
                               start=False)
                    m.then_inc(S("rec_state"), 1)
                if c >= 2:
                    pe.wait_ge(*W("y_kept", c - 1))
                for h in range(8):
                    o = ps[(h % 2) * HD:(h % 2 + 1) * HD, 2 + c % 2, (h // 2) * CH:(h // 2 + 1) * CH]
                    if c:
                        mm(o, state[:, c % 2, h // 2, :], arz[:, h % 2, h // 2, c, 1, :], stop=False)
                    mm(o, u_z[:, c % 2, h * HD:(h + 1) * HD], rb_t[:, 8 * t + h, :], start=c == 0, stop=False)
                    m = mm(o, vz[:, c % 2, t, h * HD:(h + 1) * HD], rk_t[:, 8 * t + h, :], start=False)
                m.then_inc(S("rec_y"), 1)
            pe.wait_ge(*W("y_kept", 4))
            four(4, lambda o, k: mm(o, head_mean, y_rw[:, k, :]), "y_mean")
            pe.wait_ge(*W("y_sq", 2))
            four(6, lambda o, k: mm(o, head_mean, sq[:, k, :]), "y_var")
            pe.wait_ge(*W("rw_out", 1))
            pe.wait_ge(*W("y_centred", 2))
            out_rows(N_WOUT, lambda k: mix[k // 4][:, k % 4, :], "wout")
            norm_transposes("n3", 4)
            ffn(N_FFN2, "f2")
            pe.wait_ge(*W("ctx_scaled", 2))
            pe.wait_ge(*W("mod_cols", 3))
            pe.wait_ge(*W("f2_hidden", FFC))
            norm_transposes("ctx", 0, ctx_x)
            norm_transposes("n4", 4)
            normed("ctx")
            normed("n4")

            def product(n, group):
                j = n - N_WIN2
                weight(n)
                if j >= 2:
                    pe.wait_ge(*W("w2_copied", j - 1))
                b0 = 2 * (j % 2)
                if group == "v":
                    for t in range(4):
                        for k in range(KT):
                            m = mm(ps[:, b0 + t // 2, (t % 2) * 256:(t % 2 + 1) * 256],
                                   hall[:, t // 2, k, (t % 2) * P:(t % 2 + 1) * P], cols(n)[:, k, :], start=k == 0, stop=k == KT - 1)
                else:
                    for f in range(2):
                        for k in range(KT):
                            o = ps[:, b0 + f, :] if group == "k" else ps[:, b0, f * T:(f + 1) * T]
                            m = mm(o, cols(n)[:, k, f * P:(f + 1) * P], hall[:, :, k, :] if group == "k" else hall[:, 1, k, :],
                                   start=k == 0, stop=k == KT - 1)
                m.then_inc(S("w_used"), 1)

            for j in range(14):
                product(N_WIN2 + j, "k" if j < 4 else "q" if j < 8 else "v" if j < 12 else "f")

            def scores(h):
                pe.wait_ge(*W("roped_q", 4))
                pe.wait_ge(*W("roped_k", 4))
                for t in range(TT):
                    if h:
                        pe.wait_ge(*W("att_p", 2 * (2 * (h - 1) + t + 1)))
                    for i in range(2):
                        m = mm(ps[:, 4 + 2 * t + i, :], qz2[:, i, h, t * P:(t + 1) * P], k_all[:, h, :])
                    m.then_inc(S("att_s"), 1)

            def gate_chunk(j):
                n = N_WIN2 + 14 + j
                weight(n)
                if j:
                    pe.wait_ge(*W("gates_copied", j))
                for f in range(2):
                    for k in range(KT):
                        m = mm(ps[:, 0, f * T:(f + 1) * T], cols(n)[:, k, f * P:(f + 1) * P], hall[:, 1, k, :],
                               start=k == 0, stop=k == KT - 1)
                m.then_inc(S("w_used"), 1)

            pe.wait_ge(*W("w2_copied", 14))
            scores(0)
            pe.wait_ge(*W("lam_prod", 1))
            mm(ps[:, 1, 0:2], ones, small[:, 34:36]).then_inc(S("lam_sum"), 1)
            for h in range(8):
                gate_chunk(h)
                if h + 1 < 8:
                    scores(h + 1)
                for t in range(TT):
                    pe.wait_ge(*W("att_a", 2 * h + t + 1))
                    if h:
                        pe.wait_ge(*W("att_t", 2 * (h - 1) + t + 1))
                    for k in range(4):
                        m = pe.transpose(ps[:, 2 + t, k * P:(k + 1) * P], att[h % 2][:, t, k * P:(k + 1) * P], ident)
                    m.then_inc(S("att_turned"), 1)
                pe.wait_ge(*W("att_t", 2 * h + 2))
                pe.wait_ge(*W("lam_exp", 1))
                if h:
                    pe.wait_ge(*W("heads_kept", h))
                for k in range(4):
                    m = mm(ps[:, 1, 0:T], v_all[:, k, h * P:(h + 1) * P], att_t[h % 2][:, k, :], start=k == 0,
                           stop=k == 3)
                m.then_inc(S("att_o"), 1)

            pe.wait_ge(*W("att_p", 32))
            for t in range(TT):
                for g in range(4):
                    m = mm(ps[:, 4 + 2 * t + g // 2, (g % 2) * T:(g % 2 + 1) * T], f_t[:, g, t * P:(t + 1) * P],
                           C("dft_d"))
                    if g % 2:
                        m.then_inc(S("dft_1"), 1)
            pe.wait_ge(*W("att_t", 16))
            pe.wait_ge(*W("dft_mid", 4))
            dft_n = C("dft_n").rearrange("p (t c n) -> p t c n", t=TT, c=2)
            for g in range(4):
                for t in range(TT):
                    for c in range(2):
                        m = mm(ps[:, 2 + g // 2, (g % 2) * T:(g % 2 + 1) * T], dft_mid[:, t, g, c * P:(c + 1) * P],
                               dft_n[:, t, c, :], start=t == 0 and c == 0, stop=t == 1 and c == 1)
                if g % 2:
                    m.then_inc(S("dft_2"), 1)
            pe.wait_ge(*W("heads_sq", 2))
            for h in range(8):
                m = mm(ps[:, 4 + h // 2, (h % 2) * T:(h % 2 + 1) * T], ones, heads_sq[:, h, :])
                if h % 2:
                    m.then_inc(S("heads_ss"), 1)
            pe.wait_ge(*W("four_t", 2))
            pe.wait_ge(*W("gates_copied", 8))
            pe.wait_ge(*W("heads_kept", 8))
            for c in range(2):
                weight(N_FO + c)
                w = slot(N_FO + c).rearrange("p (k n) -> p k n", k=4)
                for m_ in range(4):
                    for k in range(4):
                        m = mm(ps[:, 2 * c + m_ // 2, (m_ % 2) * T:(m_ % 2 + 1) * T], w[:, k, m_ * P:(m_ + 1) * P],
                               four_t[:, k, :], start=k == 0, stop=k == 3)
                m.then_inc(S("w_used"), 1)
            pe.wait_ge(*W("heads_normed", 2))
            for c in range(4):
                weight(N_AO + c)
                for f in range(2):
                    for k in range(KT):
                        m = mm(ps[:, 4 + c, f * T:(f + 1) * T], cols(N_AO + c)[:, k, f * P:(f + 1) * P],
                               heads[:, k, :], start=k == 0, stop=k == KT - 1)
                m.then_inc(S("w_used"), 1)
            pe.wait_ge(*W("y_mix", 4))
            out_rows(N_O2, lambda k: y_mix[:, k, :], "o2")
            norm_transposes("n5")
            normed("n5")

            pe.wait_ge(*W("route_in", 48))
            for t in range(TT):
                for k in range(KT):
                    mm(ps[:, 0, 32 * t:32 * t + 20], hall[:, 1, k, t * P:(t + 1) * P], w_route[:, k, :],
                       start=k == 0, stop=False)
                m = mm(ps[:, 0, 32 * t:32 * t + 20], ones[0:1, :], row_f[:, 1024:1044], start=False)
            m.then_inc(S("logits"), 1)
            pe.wait_ge(*W("chosen", 1))
            before = C("causal")[:, 0:P]
            sel = rt(4).rearrange("p (t e) -> p t e", t=TT)
            mm(ps[:, 1, 0:16], before, sel[:, 0, :])
            mm(ps[:, 1, 16:32], before, sel[:, 1, :], stop=False)
            mm(ps[:, 1, 16:32], ones, sel[:, 0, :], start=False)
            mm(ps[:, 1, 32:48], ones, sel[:, 0, :], stop=False)
            mm(ps[:, 1, 32:48], ones, sel[:, 1, :], start=False).then_inc(S("places"), 1)
            pe.wait_ge(*W("zeros", 1))
            pe.wait_ge(*W("x4_done", 4))
            for b in range(4):
                m = mm(ps[:, 4 + b, :], zero_blk, cst[:, 0:512], stop=False, group=True)
            m.then_inc(S("gathered"), 1)

            def scatter(i):
                pe.wait_ge(*W("y_kept_v", i + 1))
                pe.wait_ge(*W("y_kept_a", i + 1))
                pe.wait_ge(*W("pick_t", i + 1))
                for t in range(TT):
                    for h in range(2):
                        m = mm(ps[:, 4 + 2 * t + h, :], pick_t[:, t, :], y_e[:, h * 512:(h + 1) * 512], start=False,
                               stop=False, group=True)
                return m

            pe.wait_ge(*W("rounds", 1))
            n_r = pe.value_load(n_rounds[0:1, 0:1].bitcast(U32), min_val=1, max_val=4)
            with pe.Fori(0, n_r * (E // 2)) as i:
                pe.wait_ge(*W("picked", i + 1))
                for k in range(KT):
                    for t in range(TT):
                        m = mm(ps[:, k // 4, (k % 4) * P:(k % 4 + 1) * P], xn[:, t, k * P:(k + 1) * P],
                               pick[:, t, :], start=t == 0, stop=t == 1)
                    if k % 4 == 3:
                        m.then_inc(S("gathered"), 1)
                scatter(i)
                pe.wait_ge(*W("h_sel_v", i * 4 + 4))
                pe.wait_ge(*W("h_sel_a", i * 4 + 4))
                for e in range(2):
                    for w in range(2):
                        for c in range(2):
                            n = N_EXP + 4 * e + 2 * w + c
                            weight(n, i, 12)
                            for k in range(KT):
                                m = mm(ps[e * SLOTS:(e + 1) * SLOTS, w, c * 256:(c + 1) * 256],
                                       h_sel[:, k, e * SLOTS:(e + 1) * SLOTS], cols(n)[:, k, :], start=k == 0,
                                       stop=k == KT - 1)
                            m.then_inc(S("w_used"), 1)
                pe.wait_ge(*W("picked_g", i + 1))
                for t in range(TT):
                    m = pe.transpose(ps[:, 3, t * P:(t + 1) * P], pick_g[:, t, :], ident)
                m.then_inc(S("pick_turned"), 1)
                pe.wait_ge(*W("hs", i * 2 + 2))
                for k in range(4):
                    m = pe.transpose(ps[:, 2, k * P:(k + 1) * P], hs[:, k * P:(k + 1) * P], ident)
                m.then_inc(S("hs_turned"), 1)
                pe.wait_ge(*W("hs_t", i + 1))
                pe.wait_ge(*W("pick_t", i + 2))
                for e in range(2):
                    for c in range(2):
                        n = N_EXP + 8 + 2 * e + c
                        weight(n, i, 12)
                        for f in range(2):
                            for h in range(2):
                                m = mm(ps[e * SLOTS:(e + 1) * SLOTS, 2 + h, :],
                                       hs_t[:, 2 * c + f, e * SLOTS:(e + 1) * SLOTS],
                                       rows(n)[:, f, h * 512:(h + 1) * 512], start=c == 0 and f == 0,
                                       stop=c == 1 and f == 1, group=True)
                        m.then_inc(S("w_used"), 1)
            scatter(n_r * (E // 2)).then_inc(S("moe_sum"), 1)
            for h in range(2):
                m = mm(ps[:, h, :], ones[0:1, :], row_f[:, h * 512:(h + 1) * 512])
            m.then_inc(S("final_gain"), 1)

        @block.scalar
        def _(act):
            def f(out_, in_, func, **kw):
                return act.activation(out_, in_, func, **kw)

            def norm(tag):
                for t in range(TT):
                    if tag == "n1":
                        act.wait_ge(*W(f"x_in{t}", 16))
                    elif t == 0:
                        act.wait_ge(*W(norm_after[tag][0], norm_after[tag][1]))
                    f(xn[:, t, :], x[:, t, :], ACT.Square, accum_out=ssum[:, t:t + 1]).then_inc(S(tag + "_ss"), 1)
                    act.wait_ge(*W(tag + "_ss", t + 1))
                    f(rstd[:, t:t + 1], ssum[:, t:t + 1], ACT.Sqrt, scale=1.0 / D, bias=EPS_COL).then_inc(
                        S(tag + "_root"), 1)

            def norm_cols(tag, gain, shift=None, b0=0, c=1):
                for k in range(4, 8):
                    act.wait_ge(*W(tag + "_turned", k // 2 + 1))
                    f(hall[:, c, k, :], ps[:, b0 + k // 2, (k % 2) * T:(k % 2 + 1) * T], ACT.Identity,
                      scale=gain(k), bias=shift(k) if shift else 0.0).then_inc(S(tag + "_cols_a"), 1)

            def norm_cols_hi(tag, gain):
                for k in range(KT):
                    act.wait_ge(*W(tag + "_turned", k // 2 + 1))
                    f(h_hi[:, k, :], ps[:, 4 + k // 2, (k % 2) * T:(k % 2 + 1) * T], ACT.Copy,
                      scale=gain(k)).then_inc(S(tag + "_hi"), 1)

            def split(n, it=None, per=0):
                act.wait_ge(*W(f"w_in_slot{n % RING}", at(16 * (n // RING + 1), it, 16 * per // RING)))
                if n >= HI_RING:
                    act.wait_ge(*W("w_used", at(n - HI_RING + 1, it, per)))
                f(hi(n), slot(n), ACT.Copy).then_inc(S("w_hi"), 1)

            early = CONSTS["ident"][1] + CONSTS["eps"][1]
            act.dma_start(vec[:, :], a["vectors"]).then_inc(S("vec_in"), 16)
            act.dma_start(cst[:, 0:early], a["consts"][:, 0:early]).then_inc(S("ident_in"), 16)
            act.wait_ge(*W("ident_in", 16))
            norm("n1")
            for n in range(HI_RING):
                split(N_FFN1 + n)
            act.dma_start(cst[:, early:], a["consts"][:, early:]).then_inc(S("consts"), 16)
            act.wait_ge(*W("vec_in", 16))
            c0 = VEC_AT["c_2"][0]
            f(vec[:, c0:c0 + 16], vec[:, c0:c0 + 16], ACT.Silu).then_inc(S("c_silu"), 1)
            norm_cols_hi("n1", lambda k: V("norm_ffn1", k))
            for g in range(2):
                first = ROW_AT["b_mod_2"][0] + (2 + 3 * g) * D
                act.dma_start(gate_rows[0:1, g * D:(g + 1) * D], a["rows"][:, first:first + D]).then_inc(
                    S("gate_rows"), 16)

            def ffn(n0, tag):
                def chunk(i, it=None):
                    act.wait_ge(*W("w_used", at(n0 + n_gate(i) + 1, it, 6)))
                    if i >= 2:
                        act.wait_ge(*W(tag + "_hidden", at(i - 1, it, 2)))
                    f(sg[:, i % 2, :], ps[:, 2 * (i % 2), :], ACT.Silu).then_inc(S(tag + "_silu"), 1)
                    for n in ffn_chunks(i):
                        split(n0 + n + HI_RING, it, 6)

                for i in range(FFN_PEEL):
                    chunk(i)
                with act.Fori(0, FFN_LOOP) as it:
                    chunk(FFN_PEEL, it)
                    chunk(FFN_PEEL + 1, it)
                for i in range(FFN_PEEL + 2 * FFN_LOOP, FFC):
                    chunk(i)

            ffn(N_FFN1, "f1")
            for g in range(2):
                for h in range(2):
                    bank = 1 + h if g == 0 else (3 if h == 0 else 0)
                    act.wait_ge(*W("gates_summed", 2 * g + h + 1))
                    f(gb[:, g, h * 512:(h + 1) * 512], ps[:, bank, :], ACT.Copy).then_inc(S("gates_kept"), 1)
            act.dma_start(small_w["w2"][0:64, :], a["rw_w2"]).then_inc(S("small_w"), 16)
            act.dma_start(small_w["a2"][64:128, :], a["rw_a2"]).then_inc(S("small_w"), 16)
            act.dma_start(small_w["g2"], a["rw_g2"]).then_inc(S("small_w"), 16)
            norm("n2")
            norm_cols("n2", lambda k: V("norm_mix", k))

            def copy_out(j):
                act.wait_ge(*W("w_used", N_WIN + j + 1))
                bank = ps[:, j % 4, :].rearrange("p (f n) -> p f n", f=2)
                if j < 7:
                    if j >= 2:
                        act.wait_ge(*W("shifted", j - 1))
                    elif j == 0:
                        act.wait_ge(*W("ubuf_zero", 1))
                    o = ubuf[:, j % 2, :, 1:T + 1]
                elif j < 11:
                    o = (q_raw if j < 9 else kn)[:, 2 * ((j - 7) % 2):2 * ((j - 7) % 2) + 2, :]
                else:
                    o = v_sb[:, :, (j - 11) * 256:(j - 10) * 256]
                f(o, bank, ACT.Copy).then_inc(S("win_copied"), 1)

            copy_out(0)
            act.wait_ge(*W("shifted", 1))
            f(t_w[0:64, :], x_wa[0:64, :], ACT.Tanh).then_inc(S("tanh_w"), 1)
            f(s_g, x_g, ACT.Sigmoid).then_inc(S("sig_g"), 1)
            copy_out(1)
            for k in range(4):
                act.wait_ge(*W("lora_w", k // 2 + 1))
                f(sig_w[:, k, :], ps[:, 4 + k // 2, (k % 2) * T:(k % 2 + 1) * T], ACT.Sigmoid,
                  bias=V("rw_w0", k)).then_inc(S("sig_w"), 1)
            for k in range(4):
                act.wait_ge(*W("lora_a", k // 2 + 1))
                f(av[:, k, :], ps[:, 6 + k // 2, (k % 2) * T:(k % 2 + 1) * T], ACT.Sigmoid,
                  bias=V("rw_a0", k)).then_inc(S("sig_a"), 1)
            copy_out(2)
            act.wait_ge(*W("cum", 1))
            f(w_in_, cum, ACT.Exp, scale=-DECAY).then_inc(S("decays"), 1)
            f(w_inv, cum, ACT.Exp, scale=DECAY).then_inc(S("decays"), 1)
            act.wait_ge(*W("cum", 2))
            f(w_ex, sig_w, ACT.Exp, scale=-DECAY).then_inc(S("decays"), 1)
            act.wait_ge(*W("decays", 1))
            f(w_end, w_in_.rearrange("p k (c n) -> p k c n", n=CH)[:, :, :, CH - 1], ACT.Copy).then_inc(
                S("w_end"), 1)
            copy_out(3)
            act.wait_ge(*W("kk_raw", 4))
            f(sq, kk, ACT.Square).then_inc(S("kk_sq"), 1)
            for h in range(2):
                act.wait_ge(*W("lora_g", h + 1))
                f(g_rw[:, 2 * h:2 * h + 2, :], ps[:, 4 + h, :].rearrange("p (f n) -> p f n", f=2),
                  ACT.Copy).then_inc(S("g_copied"), 1)
            copy_out(4)
            act.wait_ge(*W("kk_ms", 2))
            f(sq, banks(6), ACT.Sqrt, scale=float(HD)).then_inc(S("kk_norm"), 1)
            copy_out(5)
            copy_out(6)
            copy_out(7)
            copy_out(8)
            act.wait_ge(*W("win_copied", 9))
            act.wait_ge(*W("bonus_v", 1))
            f(sb_sq_q, q_raw, ACT.Square).then_inc(S("q_sq"), 1)
            copy_out(9)
            copy_out(10)
            for t in range(TT):
                act.wait_ge(*W("b_turned", t + 1))
                f(b_tok[:, t, :], ps[:, 4 + t, :], ACT.Copy).then_inc(S("b_tok"), 1)
            act.wait_ge(*W("win_copied", 11))
            f(sb_sq_k, kn, ACT.Square).then_inc(S("k_sq"), 1)
            copy_out(11)
            copy_out(12)
            act.wait_ge(*W("q_ms", 2))
            f(sb_sq_q, banks(4), ACT.Sqrt, bias=EPS_COL).then_inc(S("q_root"), 1)
            act.wait_ge(*W("qz", 2))
            for t in range(TT):
                act.wait_ge(*W("k_turned", t + 1))
                f(k_tok[:, t, :], ps[:, 6 + t, :], ACT.Copy).then_inc(S("k_tok"), 1)
            act.wait_ge(*W("k_ms", 2))
            f(sb_sq_k, banks(6), ACT.Sqrt, bias=EPS_COL).then_inc(S("k_root"), 1)

            def sb_log(p):
                g = p % 2
                z = ps[:, 2 * g:2 * g + 2, 0:384]
                act.wait_ge(*W("sb_z", p + 1))
                if p == 0:
                    act.wait_ge(*W("gram_k", 4))
                if p >= 2:
                    act.wait_ge(*W("sb_sp", p - 1))
                f(sb_e[g], z, ACT.Abs).then_inc(S("sb_abs"), 1)
                act.wait_ge(*W("sb_abs", p + 1))
                f(sb_e[g], sb_e[g], ACT.Exp, scale=-1.0).then_inc(S("sb_exp"), 1)
                act.wait_ge(*W("sb_exp", p + 1))
                f(sb_e[g], sb_e[g], ACT.Ln, bias=1.0).then_inc(S("sb_ln"), 1)

            def sb_weights(p):
                g = p % 2
                act.wait_ge(*W("sb_expo", p + 1))
                f(sb_att[g], sb_att[g], ACT.Exp).then_inc(S("sb_att"), 1)

            sb_log(0)
            sb_log(1)
            for p in range(4):
                sb_weights(p)
                if p + 2 < 4:
                    sb_log(p + 2)
            for j in range(2):
                act.wait_ge(*W("sb_o", 2 * j + 2))
                f(sq[:, 2 * j:2 * j + 2, :], ps[:, 4 + j, :].rearrange("p (f n) -> p f n", f=2),
                  ACT.Square).then_inc(S("sbo_sq"), 1)
            act.wait_ge(*W("sbo_ms", 2))
            f(kn, banks(6), ACT.Sqrt, bias=EPS_COL).then_inc(S("sbo_root"), 1)

            act.wait_ge(*W("sb_out", 4))
            for level in range(6):
                for t in range(TT):
                    i = 2 * level + t
                    act.wait_ge(*W("inv_x", i + 1))
                    if level:
                        act.wait_ge(*W("inv_tt", i - 1))
                        act.wait_ge(*W("inv_t", i - 1))
                    src = ps[:, t, :].rearrange("p (i n) -> p i n", n=CH)
                    for q in range(2):
                        f(x_bd[:, 8 * t:8 * t + 8, q * CH:(q + 1) * CH], src, ACT.Copy,
                          scale=C("half")[:, q:q + 1]).then_inc(S("x_bd"), 1)
                    if level < 5:
                        f(inv_x[:, 8 * t:8 * t + 8, :], src, ACT.Copy).then_inc(S("x_kept"), 1)
            for c in range(NCH):
                rows_ = slice((c % 2) * CH, (c % 2 + 1) * CH)
                act.wait_ge(*W("rec_rhs", c + 1))
                act.wait_ge(*W("u_zero", 1))
                f(rhs_z[rows_, c % 2, :], ps[rows_, 0, :], ACT.Copy).then_inc(S("rhs_kept"), 1)
                act.wait_ge(*W("rec_y", c + 1))
                f(y_rw[:, :, c * CH:(c + 1) * CH], ps[:, 2 + c % 2, 0:256].rearrange("p (k n) -> p k n", k=4),
                  ACT.Copy).then_inc(S("y_kept"), 1)
            for j in range(2):
                act.wait_ge(*W("y_centred", j + 1))
                f(sq[:, 2 * j:2 * j + 2, :], y_c[:, 2 * j:2 * j + 2, :], ACT.Square).then_inc(S("y_sq"), 1)
            act.wait_ge(*W("y_var", 2))
            f(y_n, banks(6), ACT.Sqrt, bias=LNX_COL).then_inc(S("y_root"), 1)
            for t in range(TT):
                act.dma_start(ctx_x[:, t, :], a["ctx_2"][t * P:(t + 1) * P, :]).then_inc(S(f"ctx_in{t}"), 16)
            for n in range(HI_RING):
                split(N_FFN2 + n)
            norm("n3")
            norm_cols_hi("n3", lambda k: V("norm_ffn2", k))
            for t in range(TT):
                act.wait_ge(*W(f"ctx_in{t}", 16))
                f(A(23 + t), ctx_x[:, t, :], ACT.Square, accum_out=small[:, 22 + t:23 + t]).then_inc(S("ctx_ss"), 1)
                act.wait_ge(*W("ctx_ss", t + 1))
                f(small[:, 24 + t:25 + t], small[:, 22 + t:23 + t], ACT.Sqrt, scale=1.0 / D,
                  bias=EPS_COL).then_inc(S("ctx_root"), 1)
            ffn(N_FFN2, "f2")
            def mod(j, k):
                return modc[:, 8 * j + k:8 * j + k + 1]

            act.wait_ge(*W("mod_cols", 3))
            norm_cols("ctx", lambda k: mod(5, k), lambda k: mod(4, k), 0, 0)
            norm("n4")
            norm_cols("n4", lambda k: mod(1, k), lambda k: mod(0, k), 4)
            halves = lambda b: ps[:, b, :].rearrange("p (f n) -> p f n", f=2)
            for j in range(14):
                act.wait_ge(*W("w_used", N_WIN2 + j + 1))
                b0 = 2 * (j % 2)
                if j < 4:
                    f(k_all[:, 2 * j:2 * j + 2, 0:T], ps[:, b0:b0 + 2, 0:T], ACT.Copy)
                if j < 8:
                    if j >= 2:
                        act.wait_ge(*W("roped", j - 1))
                    f(rope_raw[j % 2], ps[:, b0:b0 + 2, T:2 * T] if j < 4 else halves(b0),
                      ACT.Copy).then_inc(S("w2_copied"), 1)
                elif j < 12:
                    f(v_all[:, :, (j - 8) * 256:(j - 7) * 256], banks(b0), ACT.Copy).then_inc(S("w2_copied"), 1)
                else:
                    f(f_t[:, 2 * (j - 12):2 * (j - 12) + 2, :], halves(b0), ACT.Copy).then_inc(S("w2_copied"), 1)

            def attend(h):
                for t in range(TT):
                    n = 2 * h + t
                    act.wait_ge(*W("att_max", n + 1))
                    if n >= 4:
                        act.wait_ge(*W("att_a", n - 3))
                    for i in range(2):
                        f(probs[n % 4][:, i, :], ps[:, 4 + 2 * t + i, :], ACT.Exp, scale=HD ** -0.5,
                          bias=small[:, 28 + 2 * t + i:29 + 2 * t + i],
                          accum_out=small[:, 36 + 2 * (n % 4) + i:37 + 2 * (n % 4) + i]).then_inc(S("att_p"), 1)

            attend(0)
            act.wait_ge(*W("lam_sum", 1))
            f(small[:, 32:34], ps[:, 1, 0:2], ACT.Exp).then_inc(S("lam_exp"), 1)
            for h in range(8):
                act.wait_ge(*W("w_used", N_WIN2 + 14 + h + 1))
                f((ga if h < 4 else gf)[:, 2 * (h % 4):2 * (h % 4) + 2, :], halves(0), ACT.Copy).then_inc(
                    S("gates_copied"), 1)
                if h + 1 < 8:
                    attend(h + 1)
                for t in range(TT):
                    act.wait_ge(*W("att_turned", 2 * h + t + 1))
                    if h >= 2 and t == 0:
                        act.wait_ge(*W("att_o", h - 1))
                    f(att_t[h % 2][:, :, t * P:(t + 1) * P], ps[:, 2 + t, :].rearrange("p (k n) -> p k n", k=4),
                      ACT.Copy).then_inc(S("att_t"), 1)
                act.wait_ge(*W("att_o", h + 1))
                f(heads[:, h, :], ps[:, 1, 0:T], ACT.Copy).then_inc(S("heads_kept"), 1)
            act.dma_start(w_route[:, :, 0:4], a["w_router_group_2"].rearrange("(k p) n -> p k n", p=P)).then_inc(
                S("route_in"), 16)
            act.dma_start(w_route[:, :, 4:20], a["w_router_expert_2"].rearrange("(k p) n -> p k n", p=P)).then_inc(
                S("route_in"), 16)
            act.dma_start(row_f, a["rows"][:, 0:1044]).then_inc(S("route_in"), 16)
            for t in range(TT):
                for g in range(2):
                    act.wait_ge(*W("dft_1", 2 * t + g + 1))
                    f(dft_mid[:, t, 2 * g:2 * g + 2, :], halves(4 + 2 * t + g), ACT.Copy).then_inc(S("dft_mid"), 1)
            act.wait_ge(*W("heads_kept", 8))
            for j in range(2):
                f(heads_sq[:, 4 * j:4 * j + 4, :], heads[:, 4 * j:4 * j + 4, :], ACT.Square).then_inc(
                    S("heads_sq"), 1)
            for g in range(2):
                act.wait_ge(*W("dft_2", g + 1))
                if g == 0:
                    act.wait_ge(*W("dft_mid", 4))
                f(four_t[:, 2 * g:2 * g + 2, :], halves(2 + g), ACT.Copy).then_inc(S("four_t"), 1)
            act.wait_ge(*W("att_a", 16))
            for j in range(4):
                act.wait_ge(*W("heads_ss", j + 1))
                f(heads_rms[:, 2 * j:2 * j + 2, :], halves(4 + j), ACT.Sqrt, scale=1.0 / P,
                  bias=EPS_COL).then_inc(S("heads_root"), 1)
            for m in (gf, ga):
                f(m, m, ACT.Sigmoid).then_inc(S("gates_sig"), 1)
            norm("n5")
            norm_cols("n5", lambda k: mod(3, k), lambda k: mod(2, k))
            act.wait_ge(*W("route_max", 1))
            f(rt(7, 8), rt(6, 8), ACT.Exp).then_inc(S("route_exp"), 1)
            act.wait_ge(*W("route_diff", 1))
            f(rt(9, 2), rt(8, 2), ACT.Exp).then_inc(S("route_exp"), 1)

            act.wait_ge(*W("y_kept_v", 1))
            act.sem_inc(S("y_kept_a"), 1)
            act.wait_ge(*W("rounds", 1))
            n_r = act.value_load(n_rounds[0:1, 0:1].bitcast(U32), min_val=1, max_val=4)
            with act.Fori(0, n_r * (E // 2)) as i:
                act.wait_ge(*W("gathered", i * 2 + 3))
                for k in range(4, 8):
                    f(h_sel[:, k, :], ps[:, 1, (k - 4) * P:(k - 3) * P], ACT.Identity, scale=mod(3, k),
                      bias=mod(2, k)).then_inc(S("h_sel_a"), 1)
                for e in range(2):
                    half = slice(e * SLOTS, (e + 1) * SLOTS)
                    act.wait_ge(*W("w_used", i * 12 + (N_EXP + 4 * e + 2)))
                    f(hs[half, :], ps[half, 0, :], ACT.Silu).then_inc(S("hs_silu"), 1)
                act.wait_ge(*W("hs_turned", i + 1))
                f(hs_t, ps[:, 2, :].rearrange("p (k n) -> p k n", k=4), ACT.Copy).then_inc(S("hs_t"), 1)
                act.wait_ge(*W("w_used", i * 12 + (N_EXP + 12)))
                f(y_e[:, 0:512], ps[:, 2, :], ACT.Copy).then_inc(S("y_kept_a"), 1)
            act.wait_ge(*W("x5_done", 4))
            for t in range(TT):
                f(gated[:, t, :], x[:, t, :], ACT.Square, accum_out=ssum[:, t:t + 1]).then_inc(S("n6_ss"), 1)
                act.wait_ge(*W("n6_ss", t + 1))
                f(rstd[:, t:t + 1], ssum[:, t:t + 1], ACT.Sqrt, scale=1.0 / D, bias=EPS_COL).then_inc(
                    S("n6_root"), 1)

        @block.vector
        def _(v):
            steps = [0]

            def link(ins):
                steps[0] += 1
                ins.then_inc(S("v_step"), 1)
                v.wait_ge(*W("v_step", steps[0]))

            stt, ts, tt = v.scalar_tensor_tensor, v.tensor_scalar, v.tensor_tensor

            def norm_rows(tag):
                for t in range(TT):
                    v.wait_ge(*W(tag + "_root", t + 1))
                    link(v.reciprocal(rstd[:, t:t + 1], rstd[:, t:t + 1]))
                    ts(xn[:, t, :], x[:, t, :], rstd[:, t:t + 1], None, ALU.mult).then_inc(
                        S(tag + "_scaled"), 1)

            def split(n, it=None, per=0):
                v.wait_ge(*W("w_hi", at(n_split(n) + 1, it, per)))
                tt(lo(n), slot(n), hi(n), ALU.subtract).then_inc(S("w_lo"), 1)

            def norm_cols_lo(tag, gain):
                for k in range(KT):
                    v.wait_ge(*W(tag + "_hi", (k // 2 + 1) * 2))
                    stt(h_lo[:, k, :], ps[:, 4 + k // 2, (k % 2) * T:(k % 2 + 1) * T], gain(k), h_hi[:, k, :],
                        ALU.mult, ALU.subtract).then_inc(S(tag + "_lo"), 1)

            def norm_cols(tag, gain, shift=None, b0=0, c=1):
                for k in range(4):
                    v.wait_ge(*W(tag + "_turned", k // 2 + 1))
                    src = ps[:, b0 + k // 2, (k % 2) * T:(k % 2 + 1) * T]
                    o = hall[:, c, k, :]
                    if shift:
                        m = ts(o, src, gain(k), shift(k), ALU.mult, ALU.add)
                    else:
                        m = ts(o, src, gain(k), None, ALU.mult)
                    m.then_inc(S(tag + "_cols_v"), 1)

            def add_rows(tag, used, scale):
                v.wait_ge(*W("w_used", used))
                for t in range(TT):
                    for h in range(2):
                        s = slice(h * 512, (h + 1) * 512)
                        stt(x[:, t, s], ps[:, 4 + 2 * t + h, :], scale, x[:, t, s], ALU.mult, ALU.add).then_inc(
                            S(tag), 1)

            def products(tag, j, it=None):
                v.wait_ge(*W(f"wmod_in{j % 2}_{tag}", at(16 * (j // 2 + 1), it, 16 * MOD_PER_IT[tag] // 2)))
                w = (wmod if tag == "1" else wmod_2)[j % 2]
                if tag == "2":
                    if j:
                        v.wait_ge(*W("mod_kept_2", at(2 * j - 1, it, 2 * MOD_PER_IT[tag])))
                    for k in range(KT):
                        m = ts(mod_prod[0][:, k, :], w[:, k, :], V("c_ctx_2", k), None, ALU.mult)
                    m.then_inc(S("mod_prod_2"), 1)
                    n = at(2 * j + 1, it, 2 * MOD_PER_IT[tag])
                    v.wait_ge(*W("mod_prod_2", n))
                for k in range(KT):
                    m = ts(w[:, k, :], w[:, k, :], V("c_2", k), None, ALU.mult)
                m.then_inc(S("mod_prod_" + tag), 1)

            MOD_PER_IT = {"1": 4, "2": 2}
            MOD_BESIDE = {"1": {1: (0, 1), 2: (2, 3), 3: (4, 5), 4: (6, 7)}, "2": {2: (0, 1), 3: (2,), 4: (3,)}}

            def ffn(n0, tag):
                def chunk(i, it=None):
                    ahead = [n0 + n + HI_RING for n in ffn_chunks(i)]
                    for n in ahead[:1]:
                        split(n, it, 6)
                    v.wait_ge(*W("w_used", at(n0 + n_up(i) + 1, it, 6)))
                    v.wait_ge(*W(tag + "_silu", at(i + 1, it, 2)))
                    if i >= 2:
                        v.wait_ge(*W("w_used", at(n0 + n_down(i - 2) + 1, it, 6)))
                    h, h_high, h_low = (m[:, i % 2, :, :] for m in (hid, hid_hi, hid_lo))
                    tt(h, sg[:, i % 2, :].rearrange("p (f n) -> p f n", f=2),
                       ps[:, 2 * (i % 2) + 1, :].rearrange("p (f n) -> p f n", f=2), ALU.mult).then_inc(
                        S(tag + "_prod"), 1)
                    v.wait_ge(*W(tag + "_prod", at(i + 1, it, 2)))
                    v.tensor_copy(h_high, h).then_inc(S(tag + "_hid_hi"), 1)
                    v.wait_ge(*W(tag + "_hid_hi", at(i + 1, it, 2)))
                    tt(h_low, h, h_high, ALU.subtract).then_inc(S(tag + "_hidden"), 1)
                    for n in ahead[1:]:
                        split(n, it, 6)
                    for j in MOD_BESIDE[tag[1]].get(i, ()):
                        products(tag[1], j, it)

                for i in range(FFN_PEEL):
                    chunk(i)
                with v.Fori(0, FFN_LOOP) as it:
                    chunk(FFN_PEEL, it)
                    chunk(FFN_PEEL + 1, it)
                for i in range(FFN_PEEL + 2 * FFN_LOOP, FFC):
                    chunk(i)

            norm_rows("n1")
            for n in range(HI_RING):
                split(N_FFN1 + n)
            norm_cols_lo("n1", lambda k: V("norm_ffn1", k))
            v.wait_ge(*W("c_silu", 1))
            ffn(N_FFN1, "f1")
            add_rows("x1_done", N_FFN1 + 3 * FFC, 0.5)
            def mod_columns(pieces):
                for j, bias, gain in pieces:
                    at_b, g0 = VEC_AT["b_mod_2"][0] + bias, VEC_AT[gain][0]
                    c_ = modc[:, 16 * j + 8:16 * j + 16]
                    link(tt(modc[:, 16 * j:16 * j + 16], ps[:, 0, 16 * j:16 * j + 16], vec[:, at_b:at_b + 16],
                            ALU.add))
                    stt(c_, c_, 1.0, vec[:, g0:g0 + 8], ALU.add, ALU.mult).then_inc(S("mod_cols"), 1)

            v.wait_ge(*W("mod_sums", 1))
            mod_columns([(1, 24, "norm2_g_2")])
            v.wait_ge(*W("consts", 16))
            for q in range(2):
                ts(small[:, 20 + q:21 + q], V("sb_q_norm"), C("half")[:, q:q + 1], 0.125, ALU.mult,
                   ALU.mult).then_inc(S("q_gain"), 1)
            norm_rows("n2")
            norm_cols("n2", lambda k: V("norm_mix", k))

            def shift(j):
                v.wait_ge(*W("win_copied", j + 1))
                if j:
                    v.wait_ge(*W("shifted", j))
                u = ubuf[:, j % 2, :, 1:T + 1]
                link(tt(ushift, ubuf[:, j % 2, :, 0:T], u, ALU.subtract))
                for f in range(2):
                    tile = 2 * RW_ORDER[j] + f
                    o = {12: x_wa, 13: x_g}.get(tile)
                    if o is None:
                        o = rw_x[tile // 4 * 4][:, tile % 4, :]
                    m = stt(o, ushift[:, f, :], V("rw_mu", tile), u[:, f, :], ALU.mult, ALU.add)
                m.then_inc(S("shifted"), 1)

            shift(0)
            shift(1)
            v.wait_ge(*W("sig_w", 4))
            v.wait_ge(*W("reset_mask", 1))
            v.tensor_tensor_scan(cum.rearrange("p k n -> p (k n)"), r_scan, sig_w.rearrange("p k n -> p (k n)"),
                                 0.0, ALU.mult, ALU.add).then_inc(S("cum"), 1)
            v.wait_ge(*W("cum", 1))
            tt(sig_w, cum, sig_w, ALU.subtract).then_inc(S("cum"), 1)
            shift(2)
            v.wait_ge(*W("shifted", 3))
            for k in range(4):
                ts(kk[:, k, :], xk[:, k, :], V("rw_k_k", k), None, ALU.mult).then_inc(S("kk_raw"), 1)
            v.wait_ge(*W("sig_a", 4))
            for k in range(4):
                m = ts(kf[:, k, :], av[:, k, :], 1.0, V("rw_k_a", k), ALU.subtract, ALU.mult)
            link(m)
            link(stt(kf, kf, 1.0, xk, ALU.add, ALU.mult))
            shift(3)
            shift(4)
            v.wait_ge(*W("shifted", 5))
            for k in range(4):
                m = stt(bonus[:, k, :], xr[:, k, :], V("rw_r_k", k), kf[:, k, :], ALU.mult, ALU.mult)
            m.then_inc(S("bonus_prod"), 1)
            v.wait_ge(*W("kk_norm", 1))
            link(ts(sq, sq, 1e-12, None, ALU.max))
            link(v.reciprocal(sq, sq))
            stt(kk, kk, 1.0, sq, ALU.mult, ALU.mult).then_inc(S("kk_unit"), 1)
            v.wait_ge(*W("kk_unit", 1))
            link(tt(av, kk, av, ALU.mult))
            v.wait_ge(*W("decays", 3))
            tt(b_bar, av, w_inv, ALU.mult).then_inc(S("b_bar"), 1)
            tt(k_bar, kf, w_inv, ALU.mult).then_inc(S("k_bar"), 1)
            chunks = lambda m: m.rearrange("p k (c n) -> p (k c) n", n=CH)
            v.wait_ge(*W("g_copied", 2))
            for j, src, scale, w in ((0, kk, "neg_half", w_ex), (1, xr, "half", w_in_)):
                for q in range(2):
                    stt(arz[:, q, :, :, j, :].rearrange("p k c n -> p (k c) n"), chunks(src),
                        C(scale)[:, q:q + 1], chunks(w), ALU.mult, ALU.mult).then_inc(S("arz"), 1)
            shift(5)
            shift(6)
            v.wait_ge(*W("bonus_sum", 2))
            v.wait_ge(*W("shifted", 7))
            stt(bonus, banks(4), float(HD), xv, ALU.mult, ALU.mult).then_inc(S("bonus_v"), 1)
            v.wait_ge(*W("arz", 4))
            for t in range(TT):
                v.wait_ge(*W("v_turned", t + 1))
                for q in range(2):
                    ts(vz[:, q, t, :], ps[:, 6 + t, :], C("half")[:, q:q + 1], None, ALU.mult).then_inc(
                        S("v_tok"), 1)
            v.wait_ge(*W("q_root", 1))
            link(v.reciprocal(sb_sq_q, sb_sq_q))
            for q in range(2):
                stt(qz[:, q, :, :], q_raw, small[:, 20 + q:21 + q], sb_sq_q, ALU.mult, ALU.mult).then_inc(
                    S("qz"), 1)
            v.wait_ge(*W("k_root", 1))
            link(v.reciprocal(sb_sq_k, sb_sq_k))
            stt(kn, kn, V("sb_k_norm"), sb_sq_k, ALU.mult, ALU.mult).then_inc(S("kn"), 1)
            v.wait_ge(*W("w_end", 1))
            for sem, ab, rb, b0 in (("gram_b", ab_t, rb_t, 0), ("gram_k", ak_t, rk_t, 4)):
                for j in range(4):
                    v.wait_ge(*W(sem, j + 1))
                    src = ps[:, b0 + j, :].rearrange("p (i w n) -> p i w n", w=2, n=CH)
                    for w, o, mask in ((0, ab, "strict"), (1, rb, "incl")):
                        tt(o[:, 4 * j:4 * j + 4, :], src[:, :, w, :],
                           C(mask).unsqueeze(1).broadcast_to([P, 4, CH]), ALU.mult).then_inc(S(sem + "_masked"), 1)

            both = lambda name: C(name).unsqueeze(1).broadcast_to([P, 2, 384])

            def sb_softplus(p):
                g = p % 2
                v.wait_ge(*W("sb_ln", p + 1))
                link(stt(sb_sp[g], ps[:, 2 * g:2 * g + 2, 0:384], 0.0, sb_e[g], ALU.max, ALU.add))
                tt(sb_sp[g], sb_sp[g], both("causal"), ALU.mult).then_inc(S("sb_sp"), 1)

            def sb_exponent(p):
                g = p % 2
                v.wait_ge(*W("sb_sum", p + 1))
                if p >= 2:
                    v.wait_ge(*W("sb_o", p - 1))
                stt(sb_att[g], ps[:, 2 * g:2 * g + 2, 0:384], 0.0, both("causal_add"), ALU.min,
                    ALU.add).then_inc(S("sb_expo"), 1)

            sb_softplus(0)
            sb_softplus(1)
            for p in range(4):
                sb_exponent(p)
                if p + 2 < 4:
                    sb_softplus(p + 2)
            v.wait_ge(*W("sbo_root", 1))
            link(v.reciprocal(kn, kn))
            for k in range(4):
                stt(mix[0][:, k, :], banks(4)[:, k, :], V("sb_out_norm", k), kn[:, k, :], ALU.mult,
                    ALU.mult).then_inc(S("sb_out"), 1)
            for level in range(6):
                for t in range(TT):
                    i = 2 * level + t
                    s8 = slice(8 * t, 8 * t + 8)
                    if level < 5:
                        v.wait_ge(*W("inv_t", i + 1))
                        tt(inv_t[:, s8, :], inv_t[:, s8, :], ps[:, 2, :].rearrange("p (i n) -> p i n", n=CH),
                           ALU.add).then_inc(S("t_added"), 1)
                    v.wait_ge(*W("inv_tt", i + 1))
                    tt(inv_tt[:, s8, :], inv_tt[:, s8, :], ps[:, 3, :].rearrange("p (i n) -> p i n", n=CH),
                       ALU.add).then_inc(S("tt_added"), 1)
            for c in range(NCH):
                rows_ = slice((c % 2) * CH, (c % 2 + 1) * CH)
                v.wait_ge(*W("rec_u", c + 1))
                v.wait_ge(*W("u_zero", 1))
                v.tensor_copy(u_z[rows_, c % 2, :], ps[rows_, 1, :]).then_inc(S("u_kept"), 1)
                if c < NCH - 1:
                    v.wait_ge(*W("rec_state", c + 1))
                    sums = ps[:, 4, 0:256].rearrange("p (k n) -> p k n", k=4)
                    if c:
                        v.wait_ge(*W("rec_y", c))
                        link(tt(state_sum, sums, state[:, c % 2, :, :], ALU.add))
                        sums = state_sum
                    tt(state[:, (c + 1) % 2, :, :], sums, w_end[:, :, c].unsqueeze(2).broadcast_to([P, 4, HD]),
                       ALU.mult).then_inc(S("state"), 1)
            for j in range(2):
                v.wait_ge(*W("y_mean", j + 1))
                tt(y_c[:, 2 * j:2 * j + 2, :], y_rw[:, 2 * j:2 * j + 2, :],
                   ps[:, 4 + j, :].rearrange("p (f n) -> p f n", f=2), ALU.subtract).then_inc(S("y_centred"), 1)
            v.wait_ge(*W("y_root", 1))
            link(v.reciprocal(y_n, y_n))
            link(tt(y_n, y_c, y_n, ALU.mult))
            for k in range(4):
                m = ts(y_n[:, k, :], y_n[:, k, :], V("rw_ln_w", k), V("rw_ln_b", k), ALU.mult, ALU.add)
            link(m)
            link(tt(y_n, y_n, bonus, ALU.add))
            tt(mix[1], y_n, g_rw, ALU.mult).then_inc(S("rw_out"), 1)
            for n in range(HI_RING):
                split(N_FFN2 + n)
            add_rows("x2_done", N_WOUT + 4, 1.0)
            norm_rows("n3")
            norm_cols_lo("n3", lambda k: V("norm_ffn2", k))
            for t in range(TT):
                v.wait_ge(*W("ctx_root", t + 1))
                link(v.reciprocal(small[:, 24 + t:25 + t], small[:, 24 + t:25 + t]))
                ts(ctx_x[:, t, :], ctx_x[:, t, :], small[:, 24 + t:25 + t], None, ALU.mult).then_inc(
                    S("ctx_scaled"), 1)
            ffn(N_FFN2, "f2")
            v.wait_ge(*W("mod_sums", 2))
            mod_columns([(0, 0, "norm1_g_2"), (2, 0, "norm1_g_2")])
            add_rows("x3_done", N_FFN2 + 3 * FFC, 0.5)
            def mod(j, k):
                return modc[:, 8 * j + k:8 * j + k + 1]

            l0 = VEC_AT["lam_q1_2"][0]
            tt(small[:, 34:36], vec[:, l0:l0 + 2], vec[:, l0 + 2:l0 + 4], ALU.mult).then_inc(S("lam_prod"), 1)
            ts(small[:, 44:45], V("subln_g_2"), 1.0 - LAM_INIT, None, ALU.mult).then_inc(S("head_gain"), 1)
            v.wait_ge(*W("mod_cols", 3))
            norm_cols("ctx", lambda k: mod(5, k), lambda k: mod(4, k), 0, 0)
            norm_rows("n4")
            norm_cols("n4", lambda k: mod(1, k), lambda k: mod(0, k), 4)

            swap = list(range(16, 32)) + list(range(16))
            wide = lambda name: C(name).unsqueeze(1).broadcast_to([P, 2, T])
            for j in range(8):
                g = j % 2
                v.wait_ge(*W("w2_copied", j + 1))
                link(v.stream_shuffle(rope_sh[g], rope_raw[g], swap))
                tt(rope_sh[g], rope_sh[g], wide("sin"), ALU.mult).then_inc(S("rope_part"), 1)
                tt(rope_raw[g], rope_raw[g], wide("cos"), ALU.mult).then_inc(S("rope_part"), 1)
                v.wait_ge(*W("rope_part", 2 * j + 2))
                if j < 4:
                    tt(k_all[:, 2 * j:2 * j + 2, T:2 * T], rope_raw[g], rope_sh[g], ALU.add).then_inc(
                        S("roped_k"), 1)
                    v.wait_ge(*W("roped_k", j + 1))
                    v.sem_inc(S("roped"), 1)
                else:
                    link(tt(rope_raw[g], rope_raw[g], rope_sh[g], ALU.add))
                    for i in range(2):
                        m = ts(qz2[:, i, 2 * (j - 4):2 * (j - 4) + 2, :], rope_raw[g], C("half")[:, i:i + 1], None,
                               ALU.mult)
                        m.then_inc(S("roped" if i else "roped_half"), 1)
                    v.wait_ge(*W("roped", j + 1))
                    v.sem_inc(S("roped_q"), 1)

            def row_max(n):
                t = n % 2
                v.wait_ge(*W("att_s", n + 1))
                mx = small[:, 46 + 2 * t:48 + 2 * t]
                link(v.tensor_reduce(mx, ps[:, 4 + 2 * t:6 + 2 * t, :], AX_X, ALU.max))
                ts(small[:, 28 + 2 * t:30 + 2 * t], mx, -HD ** -0.5, None, ALU.mult).then_inc(S("att_max"), 1)

            def combine(n):
                h, t = n // 2, n % 2
                s_ = small[:, 36 + 2 * (n % 4):38 + 2 * (n % 4)]
                v.wait_ge(*W("att_p", 2 * n + 2))
                link(v.reciprocal(s_, s_))
                tt(s_[:, 1:2], s_[:, 1:2], small[:, 45:46], ALU.mult).then_inc(S("att_r"), 1)
                if n >= 4:
                    v.wait_ge(*W("att_turned", n - 3))
                o = att[h % 2][:, t, :]
                link(ts(o, probs[n % 4][:, 0, :], s_[:, 0:1], None, ALU.mult))
                v.wait_ge(*W("att_r", n + 1))
                stt(o, probs[n % 4][:, 1, :], s_[:, 1:2], o, ALU.mult, ALU.add).then_inc(S("att_a"), 1)

            row_max(0)
            row_max(1)
            v.wait_ge(*W("lam_exp", 1))
            link(tt(small[:, 45:46], small[:, 33:34], small[:, 32:33], ALU.subtract))
            link(ts(small[:, 45:46], small[:, 45:46], -LAM_INIT, None, ALU.add))
            for n in range(16):
                combine(n)
                if n + 2 < 16:
                    row_max(n + 2)

            v.wait_ge(*W("heads_kept", 8))
            v.wait_ge(*W("head_gain", 1))
            for j in range(2):
                v.wait_ge(*W("heads_root", 2 * j + 2))
                hr = heads_rms[:, 4 * j:4 * j + 4, :]
                link(v.reciprocal(hr, hr))
                ho = heads[:, 4 * j:4 * j + 4, :]
                stt(ho, ho, small[:, 44:45], hr, ALU.mult, ALU.mult).then_inc(S("heads_normed"), 1)
            v.wait_ge(*W("gates_sig", 2))
            for c in range(2):
                v.wait_ge(*W("w_used", N_FO + c + 1))
                tt(y_mix[:, 4 * c:4 * c + 4, :], gf[:, 4 * c:4 * c + 4, :], banks(2 * c), ALU.mult).then_inc(
                    S("y_four"), 1)
            for c in range(4):
                s2 = slice(2 * c, 2 * c + 2)
                v.wait_ge(*W("w_used", N_AO + c + 1))
                link(tt(ga[:, s2, :], ga[:, s2, :], ps[:, 4 + c, :].rearrange("p (f n) -> p f n", f=2), ALU.mult))
                tt(y_mix[:, s2, :], y_mix[:, s2, :], ga[:, s2, :], ALU.add).then_inc(S("y_mix"), 1)

            def add_gated(tag, gate, used=None, sem=None):
                if sem:
                    v.wait_ge(*W(sem, 1))
                else:
                    v.wait_ge(*W("w_used", used))
                for t in range(TT):
                    for h in range(2):
                        s = slice(h * 512, (h + 1) * 512)
                        link(tt(gated[:, t, s], ps[:, 4 + 2 * t + h, :], gb[:, gate, s], ALU.mult))
                        tt(x[:, t, s], x[:, t, s], gated[:, t, s], ALU.add).then_inc(S(tag), 1)

            add_gated("x4_done", 0, N_O2 + 4)
            norm_rows("n5")
            norm_cols("n5", lambda k: mod(3, k), lambda k: mod(2, k))

            r16 = lambda j: rt(j).rearrange("p (t e) -> p t e", t=TT)
            r4 = lambda j: rt(j, 8).rearrange("p (t e) -> p t e", t=TT)
            r1 = lambda j: rt(j, 2)
            b16 = lambda m: m.unsqueeze(2).broadcast_to([P, TT, 16])
            b4 = lambda m: m.unsqueeze(2).broadcast_to([P, TT, 4])
            rev16 = C("rev").unsqueeze(1).broadcast_to([P, TT, 16])
            rev4 = C("rev")[:, 0:4].unsqueeze(1).broadcast_to([P, TT, 4])
            logit = ps[:, 0, 0:64].rearrange("p (t n) -> p t n", t=TT)
            BIG = 1e30

            def first_of(o, values, top, rev, bc, tmp, best):
                link(tt(tmp, values, bc(top), ALU.is_equal))
                link(tt(tmp, tmp, rev, ALU.mult))
                link(v.tensor_reduce(best, tmp, AX_X, ALU.max))
                link(tt(o, rev, bc(best), ALU.is_equal))

            v.wait_ge(*W("logits", 1))
            link(v.tensor_copy(r4(0), logit[:, :, 0:4]))
            link(v.tensor_copy(r16(1), logit[:, :, 4:20]))
            link(v.tensor_reduce(r1(2), r4(0), AX_X, ALU.max))
            tt(r4(6), r4(0), b4(r1(2)), ALU.subtract).then_inc(S("route_max"), 1)
            first_of(r4(3), r4(0), r1(2), rev4, b4, r4(4), r1(5))
            e44 = lambda m: m.rearrange("p t (g e) -> p (t g) e", g=4)
            gsel = rt(3, 8).unsqueeze(2).broadcast_to([P, 8, 4])
            link(tt(e44(r16(10)), e44(r16(1)), gsel, ALU.mult))
            link(ts(rt(11, 8), rt(3, 8), 1.0, BIG, ALU.subtract, ALU.mult))
            link(tt(e44(r16(10)), e44(r16(10)), rt(11, 8).unsqueeze(2).broadcast_to([P, 8, 4]), ALU.add))
            link(v.tensor_reduce(r1(12), r16(10), AX_X, ALU.max))
            first_of(r16(13), r16(10), r1(12), rev16, b16, r16(14), r1(5))
            link(stt(rt(10), rt(13), -BIG, rt(10), ALU.mult, ALU.add))
            link(v.tensor_reduce(r1(15), r16(10), AX_X, ALU.max))
            first_of(r16(16), r16(10), r1(15), rev16, b16, r16(14), r1(5))
            tt(r1(8), r1(15), r1(12), ALU.subtract).then_inc(S("route_diff"), 1)
            tt(rt(4), rt(13), rt(16), ALU.add).then_inc(S("chosen"), 1)
            v.wait_ge(*W("route_exp", 2))
            link(v.tensor_reduce(r1(17), r4(7), AX_X, ALU.add))
            link(ts(r1(18), r1(9), 1.0, None, ALU.add))
            link(tt(r1(17), r1(17), r1(18), ALU.mult))
            link(v.reciprocal(r1(17), r1(17)))
            link(tt(r1(18), r1(17), r1(9), ALU.mult))
            link(tt(r16(13), r16(13), b16(r1(17)), ALU.mult))
            link(tt(r16(16), r16(16), b16(r1(18)), ALU.mult))
            link(tt(rt(19), rt(13), rt(16), ALU.add))
            v.wait_ge(*W("chosen", 1))
            v.wait_ge(*W("places", 1))
            link(tt(rt(20), rt(4), ps[:, 1, 0:32], ALU.mult))
            link(ts(rt(21), rt(4), 1.0, 1e6, ALU.subtract, ALU.mult))
            link(tt(rt(20), rt(20), rt(21), ALU.add))
            turned = lambda m: m.rearrange("p (t e) -> p e t", t=TT)
            for r in range(4):
                tab = lambda m: m[:, 32 * r:32 * r + 32].rearrange("p (e t) -> p e t", t=TT)
                ts(tab(pos_tab), turned(rt(20)), -float(SLOTS * r), None, ALU.add).then_inc(S("tables"), 1)
                v.tensor_copy(tab(gate_tab), turned(rt(19))).then_inc(S("tables"), 1)
            ts(pos_tab[:, 128:132], C("iota")[:, 0:4], 0.0, None, ALU.mult).then_inc(S("tables"), 1)
            ts(gate_tab[:, 128:132], C("iota")[:, 0:4], 0.0, None, ALU.mult).then_inc(S("tables"), 1)
            link(v.tensor_reduce(rt(22, 1), ps[:, 1, 32:48], AX_X, ALU.max))
            for r in range(1, 4):
                m = ts(rt(23, 4)[:, r:r + 1], rt(22, 1), float(SLOTS * r), None, ALU.is_gt)
            link(m)
            link(v.tensor_reduce(rt(22, 1), rt(23, 4)[:, 1:4], AX_X, ALU.add))
            link(ts(rt(22, 1), rt(22, 1), 1.0, None, ALU.add))
            v.tensor_copy(n_rounds.bitcast(U32), rt(22, 1)).then_inc(S("rounds"), 1)
            v.wait_ge(*W("tables", 10))

            def build_picks(i):
                for t in range(TT):
                    for e in range(2):
                        p_ = pos_tab[:, bass.ds(i * 4 + (2 * e + t), 1)]
                        g_ = gate_tab[:, bass.ds(i * 4 + (2 * e + t), 1)]
                        s = slice(e * SLOTS, (e + 1) * SLOTS)
                        m = ts(pick[:, t, s], C("iota"), p_, None, ALU.is_equal)
                        m2 = ts(pick_g[:, t, s], C("iota"), p_, g_, ALU.is_equal, ALU.mult)
                        if t == 1 and e == 1:
                            m.then_inc(S("picked"), 1)
                            m2.then_inc(S("picked_g"), 1)

            build_picks(0)
            v.wait_ge(*W("rounds", 1))
            n_r = v.value_load(n_rounds[0:1, 0:1].bitcast(U32), min_val=1, max_val=4)
            with v.Fori(0, n_r * (E // 2)) as i:
                v.wait_ge(*W("gathered", i * 2 + 2))
                for k in range(4):
                    ts(h_sel[:, k, :], ps[:, 0, k * P:(k + 1) * P], mod(3, k), mod(2, k), ALU.mult,
                       ALU.add).then_inc(S("h_sel_v"), 1)
                for e in range(2):
                    half = slice(e * SLOTS, (e + 1) * SLOTS)
                    v.wait_ge(*W("w_used", i * 12 + (N_EXP + 4 * e + 4)))
                    v.wait_ge(*W("hs_silu", i * 2 + (e + 1)))
                    tt(hs[half, :], hs[half, :], ps[half, 1, :], ALU.mult).then_inc(S("hs"), 1)
                v.wait_ge(*W("pick_turned", i + 1))
                v.tensor_copy(pick_t, ps[:, 3, 0:T].rearrange("p (t n) -> p t n", t=TT)).then_inc(S("pick_t"), 1)
                build_picks(i + 1)
                v.wait_ge(*W("w_used", i * 12 + (N_EXP + 12)))
                v.tensor_copy(y_e[:, 512:1024], ps[:, 3, :]).then_inc(S("y_kept_v"), 1)
            add_gated("x5_done", 1, sem="moe_sum")
            v.wait_ge(*W("final_gain", 1))
            for t in range(TT):
                v.wait_ge(*W("n6_root", t + 1))
                link(v.reciprocal(rstd[:, t:t + 1], rstd[:, t:t + 1]))
                stt(xn[:, t, :].rearrange("p (b n) -> p b n", b=2), x[:, t, :].rearrange("p (b n) -> p b n", b=2),
                    rstd[:, t:t + 1], ps[:, 0:2, :], ALU.mult, ALU.mult).then_inc(S("final"), 1)


def kernel(**inputs):
    import concourse.bacc as bacc
    from concourse.bass_utils import run_bass_kernel_spmd

    nc = bacc.Bacc("TRN2", target_bir_lowering=False, num_devices=1)
    vectors, row_table = pack_vectors(inputs)
    arrays = {"consts": constant_table(), "vectors": vectors, "rows": row_table}
    for name in MATRICES:
        m = np.asarray(inputs[name])
        arrays[name] = np.ascontiguousarray(m.reshape(m.shape[-2:] if m.shape[0] == 1 and m.ndim == 3 else m.shape[1:]))
    aps = {name: nc.dram_tensor("in_" + name, m.shape, F32, kind="ExternalInput").ap() for name, m in arrays.items()}
    out = nc.dram_tensor("out", (T, D), F32, kind="ExternalOutput").ap()
    build(nc, aps, out)
    r = run_bass_kernel_spmd(nc, [{"in_" + k: m for k, m in arrays.items()}], core_ids=[0])
    return r.results[0]["out"].reshape(1, T, D)
```

```python
from contextlib import ExitStack

import numpy as np

import concourse.bass as bass
from concourse import mybir

P = 128
F32 = mybir.dt.float32
F32R = mybir.dt.float32r
U32 = mybir.dt.uint32
ACT = mybir.ActivationFunctionType
ALU = mybir.AluOpType
AX_X = mybir.AxisListType.X

T = 256
TT = T // P
D = 1024
KT = D // P
D_FF = 2816
FFC = D_FF // 256
HD = 64
CH = 64
NCH = T // CH
E = 16
EPG = 4
EH = 512
EPS = 1e-6
LNX_EPS = 64e-5
DECAY = float(np.exp(-0.5))
LAM_INIT = 0.8 - 0.6

SLOT = 2048
RING = 6
HI_RING = 3

CONSTS = {}


def _columns(name, n, _at=[0]):
    CONSTS[name] = (_at[0], n)
    _at[0] += n
    return _at[0]


for _n, _w in (("ident", 128), ("eps", 2), ("head_mean", 128), ("ones", 128), ("neg_tri", 128), ("neg_ones", 128),
               ("causal", 384), ("causal_add", 384), ("levels", 6 * 64), ("strict", 64), ("incl", 64),
               ("cos", 256), ("sin", 256), ("dft_d", 256), ("dft_n", 1024), ("iota", 64), ("rev", 16),
               ("eye_st", 64), ("half", 2), ("neg_half", 2)):
    N_CONST = _columns(_n, _w)


def constant_table():
    c = np.zeros((P, N_CONST), np.float64)

    def put(name, a):
        at, n = CONSTS[name]
        c[:, at:at + n] = np.asarray(a).reshape(P, n)

    i = np.arange(P)
    put("ident", np.eye(P))
    put("head_mean", (i[:, None] // HD == i[None, :] // HD) / HD)
    put("ones", np.ones((P, P)))
    put("neg_tri", -1.0 * (i[:, None] >= i[None, :]))
    put("neg_ones", -np.ones((P, P)))
    strict = (i[:, None] < i[None, :]) * 1.0
    put("causal", np.concatenate([strict, np.ones((P, P)), strict], 1))
    put("causal_add", np.concatenate([strict - 1, np.zeros((P, P)), strict - 1], 1) * 1e30)
    s, t = (i % CH)[:, None], np.arange(CH)[None, :]
    lev = [(s // (2 * b) == t // (2 * b)) & (s % (2 * b) < b) & (t % (2 * b) >= b) for b in (1, 2, 4, 8, 16, 32)]
    put("levels", np.concatenate(lev, 1))
    put("eps", np.tile([EPS, LNX_EPS], (P, 1)))
    put("eye_st", s == t)
    put("strict", s < t)
    put("incl", s <= t)
    inv = (1.0 / (np.float32(10000.0) ** (np.arange(16, dtype=np.float32) / np.float32(16)))).astype(np.float32)
    tok = np.arange(T)
    within = i % HD
    pos = np.where((within < 32)[:, None], (tok // 64)[None, :], (tok % 64)[None, :]).astype(np.float32)
    ang = (pos * inv[within % 16][:, None]).astype(np.float32).astype(np.float64)
    put("cos", np.cos(ang))
    put("sin", np.where((within % 32 < 16)[:, None], -np.sin(ang), np.sin(ang)))
    k = np.outer(i, i) % P
    put("dft_d", np.concatenate([np.cos(2 * np.pi * k / P), np.sin(2 * np.pi * k / P)], 1) / np.sqrt(T * P))
    kn = 2 * np.pi * (np.outer(tok, tok) % T) / T
    dn = np.stack([np.cos(kn), -np.sin(kn)], 1).reshape(TT, P, 2, T)
    put("dft_n", dn.transpose(1, 0, 2, 3))
    half = (i[:, None] // CH == np.arange(2)[None, :]) * 1.0
    put("half", half)
    put("neg_half", -half)
    put("iota", np.tile(np.arange(64), (P, 1)))
    put("rev", np.tile(16 - np.arange(16), (P, 1)))
    return c.astype(np.float32)


VECS = [("norm_ffn1", 8), ("norm_mix", 8), ("norm_ffn2", 8), ("norm1_g_2", 8), ("norm2_g_2", 8),
        ("sb_q_norm", 1), ("sb_k_norm", 1), ("sb_out_norm", 4), ("rw_mu", 14), ("rw_w0", 4), ("rw_a0", 4),
        ("rw_k_k", 4), ("rw_k_a", 4), ("rw_r_k", 4), ("rw_ln_w", 4), ("rw_ln_b", 4), ("b_mod_2", 48),
        ("subln_g_2", 1), ("c_2", 8), ("c_ctx_2", 8), ("lam_q1_2", 1), ("lam_q2_2", 1), ("lam_k1_2", 1),
        ("lam_k2_2", 1)]
VEC_AT, _a = {}, 0
for _n, _w in VECS:
    VEC_AT[_n] = (_a, _w)
    _a += _w
N_VEC = _a
ROWS = [("final_g_2", 1024), ("b_router_group_2", 4), ("b_router_expert_2", 16), ("b_mod_2", 6144)]
ROW_AT, _a = {}, 0
for _n, _w in ROWS:
    ROW_AT[_n] = (_a, _w)
    _a += _w
N_ROW = _a


def pack_vectors(inputs):
    v = np.zeros((P, N_VEC), np.float32)
    for name, (at, n) in VEC_AT.items():
        a = np.asarray(inputs[name]).reshape(-1)
        if a.size == HD:
            a = np.concatenate([a, a]) if name.startswith("sb_") else np.concatenate([a, np.zeros(HD, np.float32)])
        v[:, at:at + n] = a.reshape(n, P).T
    r = np.zeros((1, N_ROW), np.float32)
    for name, (at, n) in ROW_AT.items():
        r[0, at:at + n] = np.asarray(inputs[name]).reshape(-1)
    return v, r


MATRICES = ["x", "ffn1_gate", "ffn1_up", "ffn1_down", "w_in", "rw_w2", "rw_a2", "rw_g2", "w_out", "ffn2_gate",
            "ffn2_up", "ffn2_down", "ctx_2", "w_mod_2", "w_in_2", "w_attn_out_2", "w_four_out_2", "w_out_2",
            "w_router_group_2", "w_router_expert_2", "w_exp_gate_2", "w_exp_up_2", "w_exp_down_2"]


def build(nc, a, out):
    ctx = ExitStack()
    with ctx:
        shared = {
            "act_mix": [("tanh_w", 1), ("sig_g", 1), ("sig_w", 4), ("sig_a", 4), ("decays", 3), ("w_end", 1),
                        ("kk_sq", 1), ("g_copied", 2), ("kk_norm", 1), ("q_sq", 1), ("q_root", 1), ("k_sq", 1),
                        ("b_tok", 2), ("k_root", 1), ("k_tok", 2)],
            "act_rms": [("sbo_sq", 2), ("sbo_root", 1), ("y_sq", 2), ("y_root", 1)],
            "act_tail": [("dft_mid", 4), ("gates_sig", 2), ("heads_hi", 2), ("y_mix_hi", 4),
                         ("route_exp", 2)],
            "pe_mix": [("lora_w", 2), ("lora_a", 2), ("lora_g", 2), ("kk_ms", 2), ("bonus_sum", 2),
                       ("q_ms", 2), ("v_turned", 2), ("b_turned", 2), ("k_ms", 2), ("k_turned", 2),
                       ("gram_b", 4), ("gram_k", 4)],
            "pe_rms": [("sbo_ms", 2), ("y_mean", 2), ("y_var", 2)],
            "pe_tail": [("heads_ss", 4), ("dft_1", 4), ("dft_2", 2), ("logits", 1), ("places", 1), ("moe_sum", 2),
                        ("final_gain", 1)],
                        "dve_mix": [("cum", 2), ("kk_raw", 4), ("bonus_prod", 1), ("kk_unit", 1), ("b_bar", 1), ("k_bar", 1),
                        ("arz", 4), ("bonus_v", 1), ("qz", 2), ("v_tok", 4), ("kn", 1), ("gram_b_masked", 8),
                        ("gram_k_masked", 8)],
            "dve_out": [("sb_out", 4), ("y_centred", 2), ("rw_out", 1)],
            "dve_tail": [("lam_prod", 1), ("head_gain", 1), ("y_four", 2), ("y_mix", 4),
                         ("route_max", 1), ("route_diff", 1), ("chosen", 1), ("tables", 10), ("rounds", 1)],
        }
        for what, count, tags in (("ss", 2, ("n1", "n2", "n3", "ctx", "n4", "n5", "n6")),
                                  ("root", 2, ("n1", "n2", "n3", "ctx", "n4", "n5", "n6")),
                                  ("scaled", 2, ("n1", "n2", "n3", "ctx", "n4", "n5")),
                                  ("turned", 4, ("n1", "n2", "n3", "ctx", "n4", "n5")),
                                  ("cols_a", 4, ("n2", "ctx", "n4", "n5")),
                                  ("cols_v", 4, ("n2", "ctx", "n4", "n5")),
                                  ("hi", 8, ("n1", "n3")), ("lo", 8, ("n1", "n3")),
                                  ("silu", FFC, ("f1", "f2")), ("hidden", FFC, ("f1", "f2")),
                                  ("prod", FFC, ("f1", "f2")), ("hid_hi", FFC, ("f1", "f2"))):
            shared["each_" + what] = [(f"{tag}_{what}", count) for tag in tags]
        shared["mod_half"] = [("mod_half_1", 16 * 2), ("mod_half_2", 8 * 2 * 2)]
        shared["mod_prod"] = [("mod_prod_1", 16), ("mod_prod_2", 16)]
        shared["mod_kept"] = [("mod_kept_1", 16), ("mod_kept_2", 16)]
        sems, base = {}, {}
        for group, events in shared.items():
            count = 0
            for name, n in events:
                base[name] = (group, count)
                count += n

        def S(name):
            group = base.get(name, (name, 0))[0]
            if group not in sems:
                sems[group] = ctx.enter_context(nc.semaphore(group))
            return sems[group]

        def W(name, n):
            before = base.get(name, (name, 0))[1]
            return S(name), n + before if before else n

        def sb(name, shape):
            return ctx.enter_context(nc.sbuf_tensor(name, shape, F32))

        def with_r(name, shape):
            whole = sb(name, shape)
            offset = nc.sbuf_base - 4 * int(np.prod(shape[1:]))
            return whole, nc.alloc_sbuf_tensor_at(name + "_r", shape, F32R, offset=offset)

        ring, ring_r = with_r("ring", [P, RING * SLOT])
        cst = sb("cst", [P, N_CONST])
        vec = sb("vec", [P, N_VEC])
        x = sb("x", [P, TT, D])
        hall, hall_r = with_r("hall", [P, 2, KT, T])
        gb = sb("gb", [P, 2, D])
        arena, arena_r = with_r("arena", [P, 27 * 1024])
        modc = sb("modc", [P, 48])
        small = sb("small", [P, 72])
        ps = ctx.enter_context(nc.psum_tensor("ps", [P, 8, 512], F32))

        def C(name):
            at, n = CONSTS[name]
            return cst[:, at:at + n]

        def V(name, i=0):
            at, _ = VEC_AT[name]
            return vec[:, at + i:at + i + 1]

        def A(blk, n=1024, off=0):
            return arena[:, blk * 1024 + off:blk * 1024 + off + n]

        def AR(blk, n=1024, off=0):
            return arena_r[:, blk * 1024 + off:blk * 1024 + off + n]

        def tiles(blk, k=4, n=T, off=0):
            return A(blk, k * n, off).rearrange("p (k n) -> p k n", k=k)

        ident, ones, head_mean = C("ident"), C("ones"), C("head_mean")

        def slot(n):
            return ring[:, (n % RING) * SLOT:(n % RING + 1) * SLOT]

        def cols(n):
            return slot(n).rearrange("p (k n) -> p k n", k=KT)

        def rows(n):
            return slot(n).rearrange("p (k n) -> p k n", k=2)

        PAIR = 12

        def exp_slot(m):
            if m < RING:
                return slot(N_EXP + m)
            return A(11 + 2 * (m - RING), SLOT)

        def exp_loaded(m):
            if m < RING:
                s = (N_EXP + m) % RING
                return S(f"w_in_slot{s}"), 16 * len(range(s, N_EXP, RING))
            return S(f"w_in_more{m - RING}"), 0

        def hi(n):
            blocks = (15, 13, 17) if n < N_WIN2 else (15, 0, 17) if n < N_GATES else (
                (19, 0, 21) if n < N_FO else (11, 21, 6))
            return AR(blocks[n % HI_RING], SLOT)

        def lo(n):
            return ring_r[:, (n % RING) * SLOT:(n % RING + 1) * SLOT]

        def n_split(n):
            return n if n < N_WIN else n - (N_FFN2 - N_WIN)

        def hi_cols(n):
            return hi(n).rearrange("p (k n) -> p k n", k=KT)

        def lo_cols(n):
            return lo(n).rearrange("p (k n) -> p k n", k=KT)

        def hi_rows(n):
            return hi(n).rearrange("p (k n) -> p k n", k=2)

        def lo_rows(n):
            return lo(n).rearrange("p (k n) -> p k n", k=2)

        def at(static, it, per):
            return static if it is None else it * per + static

        def last_first(last, fs):
            if last:
                return [(f, t) for t in range(TT) for f in fs]
            return [(f, t) for f in fs for t in range(TT)]

        tag_of_norm = {"f1": "n1", "f2": "n3"}
        norm_after = {"n2": "x1_done", "n3": "x2_done", "n4": "x3_done", "n5": "x4_done"}

        N_FFN1 = 0
        N_WIN = N_FFN1 + 3 * FFC
        N_WOUT = N_WIN + 13
        N_FFN2 = N_WOUT + 4
        N_WIN2 = N_FFN2 + 3 * FFC
        N_GATES = N_WIN2 + 14
        N_FO = N_WIN2 + 22
        N_AO = N_FO + 2
        N_O2 = N_AO + 4
        N_EXP = N_O2 + 4

        def n_gate(i):
            return 0 if i == 0 else 3 * i - 1

        def n_up(i):
            return 1 if i == 0 else 3 * i

        def n_down(i):
            return 3 * i + 4 if i < FFC - 1 else 3 * FFC - 1

        def ffn_chunks(i):
            use = [n_gate(i), n_up(i)] + ([n_down(i - 1)] if i else [])
            return [n for n in use if n + HI_RING < 3 * FFC]

        FFN_PEEL = 3
        FFN_LOOP = (FFC - 2 - FFN_PEEL) // 2
        RW_ORDER = (6, 2, 3, 0, 1, 4, 5)

        wmod, wmod_2 = ([A(j, 2048).rearrange("p (k n) -> p k n", k=KT) for j in js] for js in ((0, 2), (4, 6)))
        mod_acc, mod_acc_2, ctx_acc = A(4, 4096), A(8, 2048), A(10, 2048)
        mod_prod = [A(2, 2048).rearrange("p (k n) -> p k n", k=KT)] * 2
        sg = A(19).rearrange("p (b n) -> p b n", b=2)
        hid, hid_lo, hid_hi = (m.rearrange("p (b f n) -> p b f n", b=2, f=2) for m in (A(20), AR(20), AR(12)))
        h_lo, h_hi = hall_r[:, 0], hall_r[:, 1]
        xn = A(25, 2048).rearrange("p (t n) -> p t n", t=TT)
        gate_rows = A(23, 2048)
        rw_x = {0: tiles(0), 4: tiles(1), 8: tiles(2)}
        xr, xk, xv = rw_x[0], rw_x[4], rw_x[8]
        x_wa, x_g, t_w, s_g = (A(3, 256, 256 * j) for j in range(4))
        ubuf = A(4, 1028).rearrange("p (b f n) -> p b f n", b=2, f=2)
        ushift = A(4, 512, 1028).rearrange("p (f n) -> p f n", f=2)
        sig_w, cum, av, w_in_, w_inv, w_ex, g_rw = (tiles(j) for j in (6, 7, 8, 9, 10, 11, 12))
        kk, sq, kf = tiles(13), tiles(14), tiles(15)
        arz = A(16, 4096).rearrange("p (q k c j n) -> p q k c j n", q=2, k=4, c=NCH, j=2)
        b_bar, k_bar, bonus = tiles(20), tiles(21), tiles(22)
        vz = A(0, 2048).rearrange("p (q t n) -> p q t n", q=2, t=TT)
        b_tok = A(13).rearrange("p (t n) -> p t n", t=TT)
        k_tok = A(10).rearrange("p (t n) -> p t n", t=TT)
        ab_t, rb_t, ak_t, rk_t = (A(j).rearrange("p (i n) -> p i n", n=CH) for j in (6, 7, 8, 9))
        q_raw, kn = tiles(23), tiles(24)
        v_sb = A(25).rearrange("p (t n) -> p t n", t=TT)
        qz = A(4, 2048).rearrange("p (q k n) -> p q k n", q=2, k=4)
        sb_e, sb_sp, sb_att = ([A(j, 768).rearrange("p (h n) -> p h n", h=2) for j in js]
                               for js in ((23, 20), (11, 21), (15, 3)))
        mix = [tiles(26), tiles(2)]
        inv_t, inv_tt, inv_x = (A(j).rearrange("p (i n) -> p i n", n=CH) for j in (23, 11, 15))
        def blocks_of(ap, level, odd):
            return ap.rearrange("p (b two n) -> p b two n", two=2, n=2 ** level)[:, :, odd, :]

        def blocks_of_8(ap, level, odd):
            return ap.rearrange("p i (b two n) -> p i b two n", two=2, n=2 ** level)[:, :, :, odd, :]

        level_a = [A(j).rearrange("p (i n) -> p i n", n=CH) for j in (20, 21)]
        rhs_z, u_z = (A(j).rearrange("p (q n) -> p q n", q=2) for j in (20, 21))
        state = A(23, 512).rearrange("p (b k n) -> p b k n", b=2, k=4)
        state_sum = A(23, 256, 512).rearrange("p (k n) -> p k n", k=4)
        y_rw, y_c, y_n = tiles(15), tiles(24), tiles(4)
        w_end = small[:, 0:16].rearrange("p (k c) -> p k c", k=4)
        ssum, rstd = small[:, 16:18], small[:, 18:20]
        sb_sq_q, sb_sq_k = tiles(14), tiles(3)
        small_w = {"w2": A(16, 512), "a2": A(16, 512), "g2": A(16, 512, 512)}
        r_scan = A(14)

        ctx_x = A(0, 2048).rearrange("p (t n) -> p t n", t=TT)
        both_hi, both_lo = AR(23, 4096).rearrange("p (c k n) -> p c k n", c=2, k=KT), hall_r
        qz2 = A(2, 4096).rearrange("p (i h n) -> p i h n", i=2, h=8)
        k_all = A(6, 4096).rearrange("p (h n) -> p h n", h=8)
        v_all = A(10, 4096).rearrange("p (t n) -> p t n", t=4)
        f_t, four_t = tiles(14), tiles(14)
        ga, gf = (A(j, 2048).rearrange("p (k n) -> p k n", k=8) for j in (15, 17))
        rope_raw, rope_sh = ([A(j + g, 512).rearrange("p (f n) -> p f n", f=2) for g in range(2)] for j in (19, 21))
        probs = [A(19 + j).rearrange("p (i n) -> p i n", i=2) for j in range(4)]
        att = [A(23 + j).rearrange("p (t n) -> p t n", t=TT) for j in range(2)]
        att_t = [tiles(j) for j in range(2)]
        heads = A(25, 2048).rearrange("p (h n) -> p h n", h=8)
        heads_sq, heads_rms = hall[:, 0], hall[:, 1]
        dft_mid = A(2, 2048).rearrange("p (t g n) -> p t g n", t=TT, g=4)
        four_hi, four_lo = (AR(j).rearrange("p (k n) -> p k n", k=4) for j in (13, 14))
        heads_hi, heads_lo, y_mix_hi, y_mix_lo = (AR(j, 2048).rearrange("p (k n) -> p k n", k=8)
                                                  for j in (23, 25, 2, 4))
        y_mix = A(4, 2048).rearrange("p (k n) -> p k n", k=8)
        gated = A(6, 2048).rearrange("p (t n) -> p t n", t=TT)
        SLOTS = 64
        w_route, row_f = A(9, 160).rearrange("p (k n) -> p k n", k=KT), A(9, 1044, 160)[0:1, :]
        h_sel = A(0).rearrange("p (k n) -> p k n", k=KT)
        hs, hs_t = A(1, 512), A(1, 512, 512).rearrange("p (k n) -> p k n", k=4)
        y_e = A(2)
        pick, pick_g = (A(3, 256, j).rearrange("p (t n) -> p t n", t=TT) for j in (0, 256))
        pick_t = A(3, 256, 512).rearrange("p (t n) -> p t n", t=TT)
        pos_tab, gate_tab = A(4, 132), A(4, 132, 132)
        n_rounds = A(4, 1, 264)
        rt = lambda j, n=32: A(8, n, 32 * j)
        zero_blk = A(7, 128)
        EPS_COL, LNX_COL = C("eps")[:, 0:1], C("eps")[:, 1:2]

        def banks(b0):
            return ps[:, b0:b0 + 2, :].rearrange("p b (f n) -> p (b f) n", f=2)

        block = ctx.enter_context(nc.Block())

        w_four = a["w_four_out_2"].rearrange("(k p) n -> p k n", p=P)
        w_gu = [a[k].rearrange("e (k p) n -> e p k n", p=P) for k in ("w_exp_gate_2", "w_exp_up_2")]
        w_dn = a["w_exp_down_2"].rearrange("e (k p) n -> e p k n", p=P)
        w_cols = {k: a[k].rearrange("(k p) n -> p k n", p=P) for k in
                  ("ffn1_gate", "ffn1_up", "w_in", "ffn2_gate", "ffn2_up", "w_mod_2", "w_in_2", "w_attn_out_2")}
        w_rows = {k: a[k].rearrange("(k p) n -> p k n", p=P) for k in
                  ("ffn1_down", "w_out", "ffn2_down", "w_out_2")}

        @block.sync
        def _(sp):
            def load(n, src, it=None, per=0):
                if n >= RING:
                    sp.wait_ge(*W("w_used", at(n - RING + 1, it, per)))
                view = slot(n).rearrange("p (k n) -> p k n", k=src.shape[1])
                sp.dma_start(view, src).then_inc(S(f"w_in_slot{n % RING}"), 16)

            def c256(name, c):
                return w_cols[name][:, :, bass.ds(c * 256, 256)]

            def r256(name, c):
                return w_rows[name][:, bass.ds(c * 2, 2), :]

            def ffn(n0, tag):
                def chunk(i, it=None):
                    load(n0 + n_gate(i), c256(tag + "_gate", at(i, it, 2)), it, 6)
                    load(n0 + n_up(i), c256(tag + "_up", at(i, it, 2)), it, 6)
                    if i >= 1:
                        load(n0 + n_down(i - 1), r256(tag + "_down", at(i - 1, it, 2)), it, 6)

                for i in range(FFN_PEEL):
                    chunk(i)
                with sp.Fori(0, FFN_LOOP) as it:
                    chunk(FFN_PEEL, it)
                    chunk(FFN_PEEL + 1, it)
                for i in range(FFN_PEEL + 2 * FFN_LOOP, FFC):
                    chunk(i)
                load(n0 + n_down(FFC - 1), r256(tag + "_down", FFC - 1))

            for t in range(TT):
                sp.dma_start(x[:, t, :], a["x"][t * P:(t + 1) * P, :]).then_inc(S(f"x_in{t}"), 16)
            ffn(N_FFN1, "ffn1")
            for j, c in enumerate([6 + c for c in RW_ORDER] + list(range(6))):
                load(N_WIN + j, c256("w_in", c))
            for c in range(4):
                load(N_WOUT + c, r256("w_out", c))
            ffn(N_FFN2, "ffn2")
            W2_ORDER = (4, 5, 6, 7, 0, 1, 2, 3) + tuple(range(8, 22))
            for j, c in enumerate(W2_ORDER):
                load(N_WIN2 + j, c256("w_in_2", c))
            for c in range(2):
                load(N_FO + c, w_four[:, :, c * 512:(c + 1) * 512])
            for c in range(4):
                load(N_AO + c, c256("w_attn_out_2", c))
            for c in range(4):
                load(N_O2 + c, r256("w_out_2", c))

            def expert_pair(e0, it, first=False):
                def load_expert(m, src):
                    if first and m < RING:
                        sp.wait_ge(*W("w_used", N_EXP + m - RING + 1))
                    elif first:
                        if m == RING:
                            sp.wait_ge(*W("y_mix_lo", 4))
                            sp.wait_ge(*W("w_used", N_EXP))
                    else:
                        sp.wait_ge(*W("w_used", it * PAIR + (N_EXP + m - PAIR + 1)))
                    sp.dma_start(exp_slot(m).rearrange("p (k n) -> p k n", k=src.shape[1]), src).then_inc(
                        exp_loaded(m)[0], 16)

                for e in range(2):
                    for w in range(2):
                        for c in range(2):
                            load_expert(4 * e + 2 * w + c,
                                        w_gu[w][bass.ds(e0 + e, 1), :, 4 * c:4 * c + 4, :].squeeze(0))
                for e in range(2):
                    for c in range(2):
                        load_expert(8 + 2 * e + c, w_dn[bass.ds(e0 + e, 1), :, 2 * c:2 * c + 2, :].squeeze(0))

            expert_pair(0, 0, True)
            with sp.Fori(1, E // 2 - 1) as pair:
                expert_pair(pair * 2, pair)
            sp.wait_ge(*W("rounds", 1))
            n_r = sp.value_load(n_rounds[0:1, 0:1].bitcast(U32), min_val=1, max_val=4)
            with sp.Fori(E // 2 - 1, n_r * (E // 2)) as i:
                expert_pair((i % (E // 2)) * 2, i)
            sp.wait_ge(*W("final", 2))
            for t in range(TT):
                sp.dma_start(out[t * P:(t + 1) * P, :], xn[:, t, :]).then_inc(S("stored"), 16)
            sp.wait_ge(*W("stored", 16 * 2))

        @block.gpsimd
        def _(pool):
            def modulate(tag, places, pairs, first, vectors):
                n = len(vectors)

                def load(b, col):
                    pool.dma_start(places[b], w_cols["w_mod_2"][:, :, bass.ds(col, 256)]).then_inc(
                        S(f"wmod_in{b}_{tag}"), 16)

                def chunk(b, it, done, load_next=True):
                    before = 2 * done + b
                    for i, (prod, o) in enumerate(vectors):
                        prod = prod[b]
                        pool.wait_ge(*W("mod_prod_" + tag, it * (2 * n) + (before * n + i + 1)))
                        pool.tensor_tensor(prod[:, 0:4, :], prod[:, 0:4, :], prod[:, 4:8, :], ALU.add).then_inc(
                            S("mod_half_" + tag), 1)
                        pool.wait_ge(*W("mod_half_" + tag, it * (4 * n) + (2 * (before * n + i) + 1)))
                        pool.tensor_tensor(prod[:, 0:2, :], prod[:, 0:2, :], prod[:, 2:4, :], ALU.add).then_inc(
                            S("mod_half_" + tag), 1)
                        pool.wait_ge(*W("mod_half_" + tag, it * (4 * n) + (2 * (before * n + i) + 2)))
                        pool.tensor_tensor(o[:, bass.ds(it * 512 + (done * 512 + b * 256), 256)], prod[:, 0, :],
                                           prod[:, 1, :], ALU.add).then_inc(S("mod_kept_" + tag), 1)
                    pool.wait_ge(*W("mod_kept_" + tag, it * (2 * n) + (before + 1) * n))
                    if load_next:
                        load(b, it * 512 + (first + 512 * (done + 1) + b * 256))

                load(0, first)
                load(1, first + 256)
                with pool.Fori(0, pairs - 1) as it:
                    for b in range(2):
                        chunk(b, it, 0)
                for b in range(2):
                    chunk(b, 0, pairs - 1, False)

            pool.wait_ge(*W("n1_lo", 8))
            modulate("1", wmod, 8, 2 * D, [(wmod, mod_acc)])
            pool.wait_ge(*W("w_used", N_FFN1 + 3 * FFC))
            pool.memset(r_scan, 1.0).then_inc(S("reset_ones"), 1)
            pool.wait_ge(*W("reset_ones", 1))
            pool.memset(r_scan.rearrange("p (c n) -> p c n", n=CH)[:, :, 0:1], 0.0).then_inc(S("reset_mask"), 1)
            pool.wait_ge(*W("gates_summed", 4))
            pool.memset(ubuf[:, :, :, 0:1], 0.0).then_inc(S("ubuf_zero"), 1)

            pool.wait_ge(*W("gram_b_masked", 8))
            pool.wait_ge(*W("sb_sum", 4))
            for m in (inv_t, inv_tt):
                pool.tensor_copy(m, C("eye_st").unsqueeze(1).broadcast_to([P, 16, CH])).then_inc(S("inv_init"), 1)
            pool.wait_ge(*W("sb_expo", 4))
            for level in range(6):
                for t in range(TT):
                    if level >= 2:
                        pool.wait_ge(*W("inv_x", 2 * (level - 2) + t + 1))
                        pool.wait_ge(*W("tt_added", 2 * (level - 2) + t + 1))
                    s8 = slice(8 * t, 8 * t + 8)
                    pool.tensor_tensor(level_a[level % 2][:, s8, :], ab_t[:, s8, :],
                                       C("levels")[:, level * CH:(level + 1) * CH].unsqueeze(1).broadcast_to(
                                           [P, 8, CH]), ALU.mult).then_inc(S("level_a"), 1)
            pool.wait_ge(*W("inv_x", 12))
            pool.memset(A(20, 2048), 0.0).then_inc(S("u_zero"), 1)
            pool.wait_ge(*W("w_used", N_FFN2))
            modulate("2", wmod_2, 4, 0, [(mod_prod, ctx_acc), (wmod_2, mod_acc_2)])
            pool.wait_ge(*W("x4_done", 4))
            pool.memset(y_e, 0.0).then_inc(S("y_kept_v"), 1)
            pool.memset(pick_t, 0.0).then_inc(S("pick_t"), 1)
            pool.memset(zero_blk, 0.0).then_inc(S("zeros"), 1)

        @block.tensor
        def _(pe):
            def weight(n, it=None, per=0):
                pe.wait_ge(*W(f"w_in_slot{n % RING}", at(16 * (n // RING + 1), it, 16 * per // RING)))

            def split_weight(n, it=None, per=0):
                pe.wait_ge(*W("w_lo", at(n_split(n) + 1, it, per)))

            def mm(out_, lhsT, rhs, start=True, stop=True, group=False):
                return pe.matmul(out_, lhsT, rhs, start=start, stop=stop, skip_group_check=group)

            def norm_transposes(tag, b0=0, src=None):
                for t in range(TT):
                    pe.wait_ge(*W(tag + "_scaled", t + 1))
                    for k in range(KT):
                        m = pe.transpose(ps[:, b0 + k // 2, (k % 2) * T + t * P:(k % 2) * T + (t + 1) * P],
                                         (xn if src is None else src)[:, t, k * P:(k + 1) * P], ident)
                        if t == TT - 1 and k % 2:
                            m.then_inc(S(tag + "_turned"), 1)

            def normed(tag):
                pe.wait_ge(*W(tag + "_cols_v", 4))
                pe.wait_ge(*W(tag + "_cols_a", 4))

            def mm3(out_, w, h, start=True, stop=True, group=False):
                for i, j in ((0, 0), (1, 0), (0, 1)):
                    m = pe.matmul(out_, w[i], h[j], start=start and i + j == 0, stop=stop and j == 1,
                                  skip_group_check=group)
                return m

            def ffn(n0, tag):
                def half(n, bank, it, first=False):
                    split_weight(n, it, 6)
                    for f in range(2):
                        for k in range(KT):
                            if first and f == 0:
                                pe.wait_ge(*W(tag_of_norm[tag] + "_lo", k + 1))
                            m = mm3(ps[:, bank, f * T:(f + 1) * T],
                                    [w[:, k, f * P:(f + 1) * P] for w in (hi_cols(n), lo_cols(n))],
                                    [h_hi[:, k, :], h_lo[:, k, :]], start=k == 0, stop=k == KT - 1)
                    m.then_inc(S("w_used"), 1)

                def down(i, it=None):
                    n = n0 + n_down(i)
                    split_weight(n, it, 6)
                    pe.wait_ge(*W(tag + "_hidden", at(i + 1, it, 2)))
                    for f, t in last_first(i == FFC - 1, range(2)):
                        for h in range(2):
                            m = mm3(ps[:, 4 + 2 * t + h, :],
                                    [z[:, i % 2, f, t * P:(t + 1) * P] for z in (hid_hi, hid_lo)],
                                    [w[:, f, h * 512:(h + 1) * 512] for w in (hi_rows(n), lo_rows(n))],
                                    start=i == 0 and f == 0, stop=i == FFC - 1 and f == 1, group=True)
                        if i == FFC - 1 and (f, t) == (1, 0):
                            m.then_inc(S("tile_0"), 1)
                    m.then_inc(S("w_used"), 1)

                def chunk(i, it=None):
                    if i >= 2:
                        pe.wait_ge(*W(tag + "_silu", at(i - 1, it, 2)))
                    half(n0 + n_gate(i), 2 * (i % 2), it, i == 0)
                    if i >= 2:
                        pe.wait_ge(*W(tag + "_hidden", at(i - 1, it, 2)))
                    half(n0 + n_up(i), 2 * (i % 2) + 1, it)
                    if i >= 1:
                        down(i - 1, it)

                for i in range(FFN_PEEL):
                    chunk(i)
                with pe.Fori(0, FFN_LOOP) as it:
                    chunk(FFN_PEEL, it)
                    chunk(FFN_PEEL + 1, it)
                for i in range(FFN_PEEL + 2 * FFN_LOOP, FFC):
                    chunk(i)
                if n0 == N_FFN2:
                    pe.wait_ge(*W("mod_kept_2", 16))
                    pe.wait_ge(*W("f2_hidden", FFC))
                    mod_columns(0, mod_acc_2)
                    mod_columns(32, ctx_acc).then_inc(S("mod_sums"), 1)
                down(FFC - 1)

            def out_rows(n0, c):
                weight(n0 + c)
                for f, t in last_first(c == 3, range(2)):
                    lhs = mix[c // 2][:, 2 * (c % 2) + f, :]
                    for h in range(2):
                        m = mm(ps[:, 4 + 2 * t + h, :], lhs[:, t * P:(t + 1) * P],
                               rows(n0 + c)[:, f, h * 512:(h + 1) * 512],
                               start=c == 0 and f == 0, stop=c == 3 and f == 1, group=True)
                    if c == 3 and (f, t) == (1, 0):
                        m.then_inc(S("tile_0"), 1)
                m.then_inc(S("w_used"), 1)

            def mod_columns(at_, sums):
                for k in range(16):
                    m = mm(ps[:, 0, at_ + k:at_ + k + 1], sums[:, k * P:(k + 1) * P], ones[:, 0:1])
                return m

            pe.wait_ge(*W("ident_in", 16))
            norm_transposes("n1", 4)
            ffn(N_FFN1, "f1")

            pe.wait_ge(*W("mod_kept_1", 16))
            pe.wait_ge(*W("consts", 16))
            pe.wait_ge(*W("gate_rows", 32))
            pe.wait_ge(*W("f1_hidden", FFC))
            mod_columns(16, mod_acc[:, D:3 * D]).then_inc(S("mod_sums"), 1)
            for g in range(2):
                for h in range(2):
                    bank = 1 + h if g == 0 else (3 if h == 0 else 0)
                    if bank == 0:
                        pe.wait_ge(*W("mod_cols", 1))
                    first = 3 * g * D + h * 512
                    mm(ps[:, bank, :], ones, mod_acc[:, first:first + 512], stop=False)
                    m = mm(ps[:, bank, :], ones[0:1, :], gate_rows[0:1, g * D + h * 512:g * D + h * 512 + 512],
                           start=False)
                    m.then_inc(S("gates_summed"), 1)

            norm_transposes("n2", 4)
            normed("n2")
            pe.wait_ge(*W("gates_kept", 4))
            h_t = hall[:, 1]

            def project(j, token_major=False):
                n = N_WIN + j
                weight(n)
                if j >= 4:
                    pe.wait_ge(*W("win_copied", j - 3))
                for f in range(2):
                    for k in range(KT):
                        if token_major:
                            m = mm(ps[:, j % 4, f * 256:(f + 1) * 256], h_t[:, k, f * P:(f + 1) * P],
                                   cols(n)[:, k, :], start=k == 0, stop=k == KT - 1)
                        else:
                            m = mm(ps[:, j % 4, f * T:(f + 1) * T], cols(n)[:, k, f * P:(f + 1) * P], h_t[:, k, :],
                                   start=k == 0, stop=k == KT - 1)
                m.then_inc(S("w_used"), 1)

            lora_w, lora_a, lora_g = small_w["w2"], small_w["a2"], small_w["g2"]

            def four(b0, f, sem):
                for k in range(4):
                    m = f(ps[:, b0 + k // 2, (k % 2) * T:(k % 2 + 1) * T], k)
                    if k % 2:
                        m.then_inc(S(sem), 1)

            project(0)
            project(1)
            pe.wait_ge(*W("small_w", 48))
            pe.wait_ge(*W("x1_done", 4))
            pe.wait_ge(*W("tanh_w", 1))
            four(4, lambda o, k: mm(o, lora_w[0:64, k * P:(k + 1) * P], t_w[0:64, :]), "lora_w")
            four(6, lambda o, k: mm(o, lora_a[64:128, k * P:(k + 1) * P], x_wa[64:128, :]), "lora_a")
            project(2)
            project(3)
            pe.wait_ge(*W("sig_g", 1))
            pe.wait_ge(*W("sig_w", 4))
            four(4, lambda o, k: mm(o, lora_g[:, k * P:(k + 1) * P], s_g), "lora_g")
            project(4)
            pe.wait_ge(*W("kk_sq", 1))
            pe.wait_ge(*W("sig_a", 4))
            four(6, lambda o, k: mm(o, head_mean, sq[:, k, :]), "kk_ms")
            project(5)
            project(6)
            pe.wait_ge(*W("g_copied", 2))
            pe.wait_ge(*W("bonus_prod", 1))
            four(4, lambda o, k: mm(o, head_mean, bonus[:, k, :]), "bonus_sum")
            project(7)
            project(8)
            project(9)
            def by_token(src, b0, sem):
                for t in range(TT):
                    for k in range(4):
                        m = pe.transpose(ps[:, b0 + t, k * P:(k + 1) * P], src[:, k, t * P:(t + 1) * P], ident)
                    m.then_inc(S(sem), 1)

            pe.wait_ge(*W("bonus_v", 1))
            pe.wait_ge(*W("q_sq", 1))
            four(4, lambda o, k: mm(o, head_mean, sb_sq_q[:, k, :]), "q_ms")
            pe.wait_ge(*W("kk_norm", 1))
            pe.wait_ge(*W("shifted", 7))
            by_token(xv, 6, "v_turned")
            project(10)
            pe.wait_ge(*W("q_root", 1))
            pe.wait_ge(*W("b_bar", 1))
            by_token(b_bar, 4, "b_turned")
            project(11, True)
            pe.wait_ge(*W("v_tok", 4))
            pe.wait_ge(*W("k_sq", 1))
            four(6, lambda o, k: mm(o, head_mean, sb_sq_k[:, k, :]), "k_ms")
            project(12, True)
            pe.wait_ge(*W("k_root", 1))
            pe.wait_ge(*W("k_bar", 1))
            by_token(k_bar, 6, "k_turned")

            def gram(src, t, b0, sem):
                for h in range(8):
                    for c in range(2):
                        m = mm(ps[c * CH:(c + 1) * CH, b0 + h // 4, (h % 4) * P:(h % 4 + 1) * P],
                               src[:, h // 2, (2 * t + c) * CH:(2 * t + c + 1) * CH],
                               arz[:, h % 2, h // 2, 2 * t + c, :, :])
                    if h % 4 == 3:
                        m.then_inc(S(sem), 1)

            pe.wait_ge(*W("arz", 4))
            pe.wait_ge(*W("win_copied", 13))
            gram(b_bar, 0, 0, "gram_b")
            gram(b_bar, 1, 2, "gram_b")
            pe.wait_ge(*W("qz", 2))
            pe.wait_ge(*W("kn", 1))
            pe.wait_ge(*W("k_tok", 2))
            pe.wait_ge(*W("b_tok", 2))
            gram(k_bar, 0, 4, "gram_k")
            gram(k_bar, 1, 6, "gram_k")

            def sb_scores(p):
                g = p % 2
                if p < 2:
                    pe.wait_ge(*W("gram_b_masked", 4 * (p + 1)))
                else:
                    pe.wait_ge(*W("sb_expo", p - 1))
                for h in range(2):
                    mm(ps[:, 2 * g + h, 0:256], kn[:, p, 0:P], qz[:, h, p, :], group=True)
                    m = mm(ps[:, 2 * g + h, 256:384], kn[:, p, P:T], qz[:, h, p, P:T], start=False, group=True)
                m.then_inc(S("sb_z"), 1)

            def sb_sums(p):
                g = p % 2
                pe.wait_ge(*W("sb_sp", p + 1))
                for h in range(2):
                    sp_ = sb_sp[g][:, h, :]
                    mm(ps[:, 2 * g + h, 0:256], C("neg_tri"), sp_[:, 0:256], start=False, group=True)
                    mm(ps[:, 2 * g + h, 128:256], C("neg_ones"), sp_[:, 256:384], start=False, group=True)
                    m = mm(ps[:, 2 * g + h, 256:384], C("neg_tri"), sp_[:, 256:384], start=False, group=True)
                m.then_inc(S("sb_sum"), 1)

            def sb_values(p):
                g = p % 2
                pe.wait_ge(*W("sb_att", p + 1))
                if p == 0:
                    pe.wait_ge(*W("gram_k_masked", 4))
                for h in range(2):
                    o = ps[h * HD:(h + 1) * HD, 4 + p // 2, (p % 2) * T:(p % 2 + 1) * T]
                    v_ = v_sb[:, :, (2 * p + h) * HD:(2 * p + h + 1) * HD]
                    mm(o, v_[:, 0, :], sb_att[g][:, h, 0:256], group=True)
                    m = mm(o[:, P:T], v_[:, 1, :], sb_att[g][:, h, 256:384], start=False, group=True)
                m.then_inc(S("sb_o"), 1)

            sb_scores(0)
            sb_scores(1)
            for p in range(4):
                sb_sums(p)
                if p >= 1:
                    sb_values(p - 1)
                if p + 2 < 4:
                    sb_scores(p + 2)
            sb_values(3)
            pe.wait_ge(*W("sbo_sq", 2))
            pe.wait_ge(*W("gram_k_masked", 8))
            four(6, lambda o, k: mm(o, head_mean, sq[:, k, :]), "sbo_ms")

            def inv(level, t, what):
                for h in range(8):
                    i = 8 * t + h
                    w, r, bank = {"x": (level_a[level % 2], inv_t, t), "t": (inv_tt, inv_x, 2),
                                  "tt": (inv_x, inv_tt, 3)}[what]
                    for q in range(2):
                        half = slice(q * CH, (q + 1) * CH)
                        if what == "x":
                            m = mm(ps[half, bank, h * CH:(h + 1) * CH], w[half, i, :], r[half, i, :])
                        else:
                            m = mm(ps[half, bank, h * CH // 2:(h + 1) * CH // 2], w[half, i, :],
                                   blocks_of(r[half, i, :], level, int(what == "tt")))
                m.then_inc(S("inv_" + what), 1)

            for level in range(6):
                for t in range(TT):
                    pe.wait_ge(*W("level_a", 2 * level + t + 1))
                    if level == 0:
                        pe.wait_ge(*W("inv_init", 2))
                        pe.wait_ge(*W("sb_expo", 4))
                    else:
                        pe.wait_ge(*W("t_added", 2 * level + t - 1))
                    inv(level, t, "x")
                for t in range(TT if level else 0):
                    pe.wait_ge(*W("x_kept", 2 * level + t - 1))
                    pe.wait_ge(*W("tt_added", 2 * level + t - 1))
                    if level < 5:
                        pe.wait_ge(*W("t_added", 2 * level + t))
                        inv(level, t, "t")
                    pe.wait_ge(*W("tt_added", 2 * level + t))
                    inv(level, t, "tt")

            for c in range(NCH):
                t, base = c // 2, (c % 2) * CH
                rows_ = slice(base, base + CH)
                pe.wait_ge(*W("tt_added", 12))
                if c:
                    pe.wait_ge(*W("state", c))
                for h in range(8):
                    o = ps[rows_, 0, h * CH:(h + 1) * CH]
                    if c:
                        mm(o, arz[:, h % 2, h // 2, c, 0, :], state[:, c % 2, h // 2, :], stop=False)
                    m = mm(o, ak_t[:, 8 * t + h, :], vz[:, c % 2, t, h * HD:(h + 1) * HD], start=c == 0)
                m.then_inc(S("rec_rhs"), 1)
                pe.wait_ge(*W("rhs_kept", c + 1))
                for h in range(8):
                    m = mm(ps[rows_, 1, h * CH:(h + 1) * CH], inv_tt[:, 8 * t + h, :],
                           rhs_z[:, c % 2, h * HD:(h + 1) * HD])
                m.then_inc(S("rec_u"), 1)
                pe.wait_ge(*W("u_kept", c + 1))
                if c == 0:
                    pe.wait_ge(*W("sb_out", 4))
                if c < NCH - 1:
                    for h in range(8):
                        o = ps[(h % 2) * HD:(h % 2 + 1) * HD, 4, (h // 2) * HD:(h // 2 + 1) * HD]
                        mm(o, b_tok[:, t, h * HD:(h + 1) * HD], u_z[:, c % 2, h * HD:(h + 1) * HD], stop=False)
                        m = mm(o, k_tok[:, t, h * HD:(h + 1) * HD], vz[:, c % 2, t, h * HD:(h + 1) * HD],
                               start=False)
                    m.then_inc(S("rec_state"), 1)
                if c >= 2:
                    pe.wait_ge(*W("y_kept", c - 1))
                for h in range(8):
                    o = ps[(h % 2) * HD:(h % 2 + 1) * HD, 2 + c % 2, (h // 2) * CH:(h // 2 + 1) * CH]
                    if c:
                        mm(o, state[:, c % 2, h // 2, :], arz[:, h % 2, h // 2, c, 1, :], stop=False)
                    mm(o, u_z[:, c % 2, h * HD:(h + 1) * HD], rb_t[:, 8 * t + h, :], start=c == 0, stop=False)
                    m = mm(o, vz[:, c % 2, t, h * HD:(h + 1) * HD], rk_t[:, 8 * t + h, :], start=False)
                m.then_inc(S("rec_y"), 1)
            pe.wait_ge(*W("y_kept", 4))
            four(0, lambda o, k: mm(o, head_mean, y_rw[:, k, :]), "y_mean")
            out_rows(N_WOUT, 0)
            pe.wait_ge(*W("y_sq", 2))
            four(2, lambda o, k: mm(o, head_mean, sq[:, k, :]), "y_var")
            out_rows(N_WOUT, 1)
            pe.wait_ge(*W("rw_out", 1))
            out_rows(N_WOUT, 2)
            out_rows(N_WOUT, 3)
            norm_transposes("n3", 4)
            ffn(N_FFN2, "f2")
            pe.wait_ge(*W("ctx_scaled", 2))
            pe.wait_ge(*W("mod_cols", 3))
            pe.wait_ge(*W("f2_hidden", FFC))
            norm_transposes("ctx", 0, ctx_x)

            def product(j, group, part=slice(0, 2)):
                n = N_WIN2 + j
                split_weight(n)
                if j >= 2:
                    pe.wait_ge(*W("w2_copied", j - 1))
                b0 = 2 * (j % 2)
                if group == "v":
                    for t in range(4):
                        for k in range(KT):
                            m = mm3(ps[:, b0 + t // 2, (t % 2) * 256:(t % 2 + 1) * 256],
                                    [z[:, t // 2, k, (t % 2) * P:(t % 2 + 1) * P] for z in (both_hi, both_lo)],
                                    [hi_cols(n)[:, k, :], lo_cols(n)[:, k, :]], start=k == 0, stop=k == KT - 1)
                else:
                    for f in range(2):
                        for k in range(KT):
                            if group == "k":
                                o = ps[:, b0 + f, part.start * T:part.stop * T]
                                h = [z[:, part, k, :] for z in (both_hi, both_lo)]
                            else:
                                o = ps[:, b0, f * T:(f + 1) * T]
                                h = [z[:, 1, k, :] for z in (both_hi, both_lo)]
                            m = mm3(o, [w[:, k, f * P:(f + 1) * P] for w in (hi_cols(n), lo_cols(n))], h,
                                    start=k == 0, stop=k == KT - 1)
                if part.stop == 2:
                    m.then_inc(S("w_used"), 1)

            pe.wait_ge(*W("ctx_lo", 1))
            for j in range(2):
                product(j, "k", slice(0, 1))
            norm_transposes("n4", 4)
            pe.wait_ge(*W("n4_lo", 1))
            for j in range(2):
                product(j, "k", slice(1, 2))
            for j in range(2, 22):
                product(j, "k" if j < 4 else "q" if j < 8 else "v" if j < 12 else "f")

            def scores(h):
                pe.wait_ge(*W("roped_q", 4))
                pe.wait_ge(*W("roped_k", 4))
                for t in range(TT):
                    if h:
                        pe.wait_ge(*W("att_p", 2 * (2 * (h - 1) + t + 1)))
                    for i in range(2):
                        m = mm(ps[:, 4 + 2 * t + i, :], qz2[:, i, h, t * P:(t + 1) * P], k_all[:, h, :])
                    m.then_inc(S("att_s"), 1)

            pe.wait_ge(*W("w2_copied", 22))
            scores(0)
            pe.wait_ge(*W("lam_prod", 1))
            mm(ps[:, 1, 0:2], ones, small[:, 34:36]).then_inc(S("lam_sum"), 1)

            def weights_by_key(h):
                for t in range(TT):
                    pe.wait_ge(*W("att_a", 2 * h + t + 1))
                    if h:
                        pe.wait_ge(*W("att_t", 2 * (h - 1) + t + 1))
                    for k in range(4):
                        m = pe.transpose(ps[:, 2 + t, k * P:(k + 1) * P], att[h % 2][:, t, k * P:(k + 1) * P], ident)
                    m.then_inc(S("att_turned"), 1)

            def values(h):
                pe.wait_ge(*W("att_t", 2 * h + 2))
                pe.wait_ge(*W("lam_exp", 1))
                if h:
                    pe.wait_ge(*W("heads_kept", h))
                for k in range(4):
                    m = mm(ps[:, 1, 0:T], v_all[:, k, h * P:(h + 1) * P], att_t[h % 2][:, k, :], start=k == 0,
                           stop=k == 3)
                m.then_inc(S("att_o"), 1)

            for h in range(8):
                if h + 1 < 8:
                    scores(h + 1)
                if h:
                    values(h - 1)
                weights_by_key(h)
            values(7)

            pe.wait_ge(*W("att_p", 32))
            pe.wait_ge(*W("heads_sq", 8))
            for h in range(8):
                m = mm(ps[:, 4 + h // 2, (h % 2) * T:(h % 2 + 1) * T], ones, heads_sq[:, h, :])
                if h % 2:
                    m.then_inc(S("heads_ss"), 1)
            pe.wait_ge(*W("att_t", 16))
            pe.wait_ge(*W("heads_kept", 8))
            for t in range(TT):
                for g in range(4):
                    m = mm(ps[:, 2 * t + g // 2, (g % 2) * T:(g % 2 + 1) * T], f_t[:, g, t * P:(t + 1) * P],
                           C("dft_d"))
                    if g % 2:
                        m.then_inc(S("dft_1"), 1)
            pe.wait_ge(*W("dft_mid", 4))
            dft_n = C("dft_n").rearrange("p (t c n) -> p t c n", t=TT, c=2)
            for g in range(4):
                for t in range(TT):
                    for c in range(2):
                        m = mm(ps[:, g // 2, (g % 2) * T:(g % 2 + 1) * T], dft_mid[:, t, g, c * P:(c + 1) * P],
                               dft_n[:, t, c, :], start=t == 0 and c == 0, stop=t == 1 and c == 1)
                if g % 2:
                    m.then_inc(S("dft_2"), 1)
            pe.wait_ge(*W("four_lo", 2))
            for c in range(2):
                split_weight(N_FO + c)
                w = [z.rearrange("p (k n) -> p k n", k=4) for z in (hi(N_FO + c), lo(N_FO + c))]
                for m_ in range(4):
                    for k in range(4):
                        m = mm3(ps[:, 2 * c + m_ // 2, (m_ % 2) * T:(m_ % 2 + 1) * T],
                                [z[:, k, m_ * P:(m_ + 1) * P] for z in w], [four_hi[:, k, :], four_lo[:, k, :]],
                                start=k == 0, stop=k == 3)
                m.then_inc(S("w_used"), 1)
            for c in range(4):
                n = N_AO + c
                split_weight(n)
                for f in range(2):
                    for k in range(KT):
                        if c == 0 and f == 0:
                            pe.wait_ge(*W("heads_lo", k // 4 + 1))
                        m = mm3(ps[:, 4 + c, f * T:(f + 1) * T],
                                [w[:, k, f * P:(f + 1) * P] for w in (hi_cols(n), lo_cols(n))],
                                [heads_hi[:, k, :], heads_lo[:, k, :]], start=k == 0, stop=k == KT - 1)
                m.then_inc(S("w_used"), 1)
            for c in range(4):
                n = N_O2 + c
                split_weight(n)
                pe.wait_ge(*W("y_mix_lo", c + 1))
                for f, t in last_first(c == 3, range(2)):
                    for h in range(2):
                        m = mm3(ps[:, 2 * t + h, :],
                                [y[:, 2 * c + f, t * P:(t + 1) * P] for y in (y_mix_hi, y_mix_lo)],
                                [w[:, f, h * 512:(h + 1) * 512] for w in (hi_rows(n), lo_rows(n))],
                                start=c == 0 and f == 0, stop=c == 3 and f == 1, group=True)
                    if c == 3 and (f, t) == (1, 0):
                        m.then_inc(S("tile_0"), 1)
                m.then_inc(S("w_used"), 1)
            norm_transposes("n5", 4)
            normed("n5")

            pe.wait_ge(*W("route_in", 48))
            for t in range(TT):
                for k in range(KT):
                    mm(ps[:, 0, 32 * t:32 * t + 20], hall[:, 1, k, t * P:(t + 1) * P], w_route[:, k, :],
                       start=k == 0, stop=False)
                m = mm(ps[:, 0, 32 * t:32 * t + 20], ones[0:1, :], row_f[:, 1024:1044], start=False)
            m.then_inc(S("logits"), 1)
            pe.wait_ge(*W("chosen", 1))
            before = C("causal")[:, 0:P]
            sel = rt(4).rearrange("p (t e) -> p t e", t=TT)
            mm(ps[:, 1, 0:16], before, sel[:, 0, :])
            mm(ps[:, 1, 16:32], before, sel[:, 1, :], stop=False)
            mm(ps[:, 1, 16:32], ones, sel[:, 0, :], start=False)
            mm(ps[:, 1, 32:48], ones, sel[:, 0, :], stop=False)
            mm(ps[:, 1, 32:48], ones, sel[:, 1, :], start=False).then_inc(S("places"), 1)
            pe.wait_ge(*W("zeros", 1))
            pe.wait_ge(*W("x4_done", 4))
            for b in range(4):
                m = mm(ps[:, 4 + b, :], zero_blk, cst[:, 0:512], stop=False, group=True)
            m.then_inc(S("gathered"), 1)

            def scatter(i, sem=None):
                pe.wait_ge(*W("y_kept_v", i + 1))
                pe.wait_ge(*W("y_kept_a", i + 1))
                pe.wait_ge(*W("pick_t", i + 1))
                for t in range(TT):
                    for h in range(2):
                        m = mm(ps[:, 4 + 2 * t + h, :], pick_t[:, t, :], y_e[:, h * 512:(h + 1) * 512], start=False,
                               stop=False, group=True)
                    if sem:
                        m.then_inc(S(sem), 1)

            def expert_weight(m, i):
                sem, before = exp_loaded(m)
                pe.wait_ge(sem, i * 16 + (before + 16))

            pe.wait_ge(*W("rounds", 1))
            n_r = pe.value_load(n_rounds[0:1, 0:1].bitcast(U32), min_val=1, max_val=4)
            with pe.Fori(0, n_r * (E // 2)) as i:
                pe.wait_ge(*W("picked", i + 1))
                for k in range(KT):
                    for t in range(TT):
                        m = mm(ps[:, k // 4, (k % 4) * P:(k % 4 + 1) * P], xn[:, t, k * P:(k + 1) * P],
                               pick[:, t, :], start=t == 0, stop=t == 1)
                    if k % 4 == 3:
                        m.then_inc(S("gathered"), 1)
                scatter(i)
                pe.wait_ge(*W("h_sel_v", i * 4 + 4))
                pe.wait_ge(*W("h_sel_a", i * 4 + 4))
                for e in range(2):
                    for w in range(2):
                        for c in range(2):
                            n = 4 * e + 2 * w + c
                            expert_weight(n, i)
                            w_ = exp_slot(n).rearrange("p (k n) -> p k n", k=4)
                            for k in range(4):
                                m = mm(ps[e * SLOTS:(e + 1) * SLOTS, w, :],
                                       h_sel[:, 4 * c + k, e * SLOTS:(e + 1) * SLOTS], w_[:, k, :],
                                       start=c == 0 and k == 0, stop=c == 1 and k == 3)
                            m.then_inc(S("w_used"), 1)
                pe.wait_ge(*W("picked_g", i + 1))
                for t in range(TT):
                    m = pe.transpose(ps[:, 3, t * P:(t + 1) * P], pick_g[:, t, :], ident)
                m.then_inc(S("pick_turned"), 1)
                pe.wait_ge(*W("hs", i * 2 + 2))
                for k in range(4):
                    m = pe.transpose(ps[:, 2, k * P:(k + 1) * P], hs[:, k * P:(k + 1) * P], ident)
                m.then_inc(S("hs_turned"), 1)
                pe.wait_ge(*W("hs_t", i + 1))
                pe.wait_ge(*W("pick_t", i + 2))
                for e in range(2):
                    for c in range(2):
                        n = 8 + 2 * e + c
                        expert_weight(n, i)
                        w_ = exp_slot(n).rearrange("p (k n) -> p k n", k=2)
                        for f in range(2):
                            for h in range(2):
                                m = mm(ps[e * SLOTS:(e + 1) * SLOTS, 2 + h, :],
                                       hs_t[:, 2 * c + f, e * SLOTS:(e + 1) * SLOTS],
                                       w_[:, f, h * 512:(h + 1) * 512], start=c == 0 and f == 0,
                                       stop=c == 1 and f == 1, group=True)
                        m.then_inc(S("w_used"), 1)
            scatter(n_r * (E // 2), "moe_sum")
            for h in range(2):
                m = mm(ps[:, h, :], ones[0:1, :], row_f[:, h * 512:(h + 1) * 512])
            m.then_inc(S("final_gain"), 1)

        @block.scalar
        def _(act):
            def f(out_, in_, func, **kw):
                return act.activation(out_, in_, func, **kw)

            def norm(tag):
                for t in range(TT):
                    if tag == "n1":
                        act.wait_ge(*W(f"x_in{t}", 16))
                    else:
                        act.wait_ge(*W(norm_after[tag], 2 * (t + 1)))
                    f(xn[:, t, :], x[:, t, :], ACT.Square, accum_out=ssum[:, t:t + 1]).then_inc(S(tag + "_ss"), 1)
                    act.wait_ge(*W(tag + "_ss", t + 1))
                    f(rstd[:, t:t + 1], ssum[:, t:t + 1], ACT.Sqrt, scale=1.0 / D, bias=EPS_COL).then_inc(
                        S(tag + "_root"), 1)

            def norm_cols(tag, gain, shift=None, b0=0, c=1):
                for k in range(4, 8):
                    act.wait_ge(*W(tag + "_turned", k // 2 + 1))
                    f(hall[:, c, k, :], ps[:, b0 + k // 2, (k % 2) * T:(k % 2 + 1) * T], ACT.Identity,
                      scale=gain(k), bias=shift(k) if shift else 0.0).then_inc(S(tag + "_cols_a"), 1)

            def norm_cols_hi(tag, gain):
                for k in range(KT):
                    act.wait_ge(*W(tag + "_turned", k // 2 + 1))
                    f(h_hi[:, k, :], ps[:, 4 + k // 2, (k % 2) * T:(k % 2 + 1) * T], ACT.Copy,
                      scale=gain(k)).then_inc(S(tag + "_hi"), 1)

            def split(n, it=None, per=0):
                act.wait_ge(*W(f"w_in_slot{n % RING}", at(16 * (n // RING + 1), it, 16 * per // RING)))
                if n_split(n) >= HI_RING and not N_FFN2 <= n < N_FFN2 + HI_RING:
                    act.wait_ge(*W("w_used", at(n - HI_RING + 1, it, per)))
                f(hi(n), slot(n), ACT.Copy).then_inc(S("w_hi"), 1)

            early = CONSTS["ident"][1] + CONSTS["eps"][1]
            act.dma_start(vec[:, :], a["vectors"]).then_inc(S("vec_in"), 16)
            act.dma_start(cst[:, 0:early], a["consts"][:, 0:early]).then_inc(S("ident_in"), 16)
            act.wait_ge(*W("ident_in", 16))
            norm("n1")
            split(N_FFN1)
            act.dma_start(cst[:, early:], a["consts"][:, early:]).then_inc(S("consts"), 16)
            act.wait_ge(*W("vec_in", 16))
            norm_cols_hi("n1", lambda k: V("norm_ffn1", k))
            split(N_FFN1 + 1)
            split(N_FFN1 + 2)
            c0 = VEC_AT["c_2"][0]
            f(vec[:, c0:c0 + 16], vec[:, c0:c0 + 16], ACT.Silu).then_inc(S("c_silu"), 1)
            for g in range(2):
                first = ROW_AT["b_mod_2"][0] + (2 + 3 * g) * D
                act.dma_start(gate_rows[0:1, g * D:(g + 1) * D], a["rows"][:, first:first + D]).then_inc(
                    S("gate_rows"), 16)

            def ffn(n0, tag):
                def chunk(i, it=None):
                    act.wait_ge(*W("w_used", at(n0 + n_gate(i) + 1, it, 6)))
                    if i >= 2:
                        act.wait_ge(*W(tag + "_hidden", at(i - 1, it, 2)))
                    f(sg[:, i % 2, :], ps[:, 2 * (i % 2), :], ACT.Silu).then_inc(S(tag + "_silu"), 1)
                    for n in ffn_chunks(i):
                        split(n0 + n + HI_RING, it, 6)

                for i in range(FFN_PEEL):
                    chunk(i)
                with act.Fori(0, FFN_LOOP) as it:
                    chunk(FFN_PEEL, it)
                    chunk(FFN_PEEL + 1, it)
                for i in range(FFN_PEEL + 2 * FFN_LOOP, FFC):
                    chunk(i)

            ffn(N_FFN1, "f1")
            norm("n2")
            for g in range(2):
                for h in range(2):
                    bank = 1 + h if g == 0 else (3 if h == 0 else 0)
                    act.wait_ge(*W("gates_summed", 2 * g + h + 1))
                    f(gb[:, g, h * 512:(h + 1) * 512], ps[:, bank, :], ACT.Copy).then_inc(S("gates_kept"), 1)
            act.dma_start(small_w["w2"][0:64, :], a["rw_w2"]).then_inc(S("small_w"), 16)
            act.dma_start(small_w["a2"][64:128, :], a["rw_a2"]).then_inc(S("small_w"), 16)
            act.dma_start(small_w["g2"], a["rw_g2"]).then_inc(S("small_w"), 16)
            norm_cols("n2", lambda k: V("norm_mix", k), None, 4)

            def copy_out(j):
                act.wait_ge(*W("w_used", N_WIN + j + 1))
                bank = ps[:, j % 4, :].rearrange("p (f n) -> p f n", f=2)
                if j < 7:
                    if j >= 2:
                        act.wait_ge(*W("shifted", j - 1))
                    elif j == 0:
                        act.wait_ge(*W("ubuf_zero", 1))
                    o = ubuf[:, j % 2, :, 1:T + 1]
                elif j < 11:
                    o = (q_raw if j < 9 else kn)[:, 2 * ((j - 7) % 2):2 * ((j - 7) % 2) + 2, :]
                else:
                    o = v_sb[:, :, (j - 11) * 256:(j - 10) * 256]
                f(o, bank, ACT.Copy).then_inc(S("win_copied"), 1)

            copy_out(0)
            act.wait_ge(*W("shifted", 1))
            f(t_w[0:64, :], x_wa[0:64, :], ACT.Tanh).then_inc(S("tanh_w"), 1)
            f(s_g, x_g, ACT.Sigmoid).then_inc(S("sig_g"), 1)
            copy_out(1)
            for k in range(4):
                act.wait_ge(*W("lora_w", k // 2 + 1))
                f(sig_w[:, k, :], ps[:, 4 + k // 2, (k % 2) * T:(k % 2 + 1) * T], ACT.Sigmoid,
                  bias=V("rw_w0", k)).then_inc(S("sig_w"), 1)
            for k in range(4):
                act.wait_ge(*W("lora_a", k // 2 + 1))
                f(av[:, k, :], ps[:, 6 + k // 2, (k % 2) * T:(k % 2 + 1) * T], ACT.Sigmoid,
                  bias=V("rw_a0", k)).then_inc(S("sig_a"), 1)
            copy_out(2)
            act.wait_ge(*W("cum", 1))
            f(w_in_, cum, ACT.Exp, scale=-DECAY).then_inc(S("decays"), 1)
            f(w_inv, cum, ACT.Exp, scale=DECAY).then_inc(S("decays"), 1)
            act.wait_ge(*W("cum", 2))
            f(w_ex, sig_w, ACT.Exp, scale=-DECAY).then_inc(S("decays"), 1)
            act.wait_ge(*W("decays", 1))
            f(w_end, w_in_.rearrange("p k (c n) -> p k c n", n=CH)[:, :, :, CH - 1], ACT.Copy).then_inc(
                S("w_end"), 1)
            copy_out(3)
            act.wait_ge(*W("kk_raw", 4))
            f(sq, kk, ACT.Square).then_inc(S("kk_sq"), 1)
            for h in range(2):
                act.wait_ge(*W("lora_g", h + 1))
                f(g_rw[:, 2 * h:2 * h + 2, :], ps[:, 4 + h, :].rearrange("p (f n) -> p f n", f=2),
                  ACT.Copy).then_inc(S("g_copied"), 1)
            copy_out(4)
            act.wait_ge(*W("kk_ms", 2))
            f(sq, banks(6), ACT.Sqrt, scale=float(HD)).then_inc(S("kk_norm"), 1)
            copy_out(5)
            copy_out(6)
            copy_out(7)
            copy_out(8)
            act.wait_ge(*W("win_copied", 9))
            act.wait_ge(*W("kk_unit", 1))
            f(sb_sq_q, q_raw, ACT.Square).then_inc(S("q_sq"), 1)
            copy_out(9)
            act.wait_ge(*W("q_ms", 2))
            f(sb_sq_q, banks(4), ACT.Sqrt, bias=EPS_COL).then_inc(S("q_root"), 1)
            copy_out(10)
            act.wait_ge(*W("win_copied", 11))
            f(sb_sq_k, kn, ACT.Square).then_inc(S("k_sq"), 1)
            for t in range(TT):
                act.wait_ge(*W("b_turned", t + 1))
                f(b_tok[:, t, :], ps[:, 4 + t, :], ACT.Copy).then_inc(S("b_tok"), 1)
            copy_out(11)
            act.wait_ge(*W("k_ms", 2))
            f(sb_sq_k, banks(6), ACT.Sqrt, bias=EPS_COL).then_inc(S("k_root"), 1)
            copy_out(12)
            act.wait_ge(*W("arz", 4))
            for t in range(TT):
                act.wait_ge(*W("k_turned", t + 1))
                f(k_tok[:, t, :], ps[:, 6 + t, :], ACT.Copy).then_inc(S("k_tok"), 1)

            def sb_exp(p):
                g = p % 2
                z = ps[:, 2 * g:2 * g + 2, 0:384]
                act.wait_ge(*W("sb_z", p + 1))
                if p == 0:
                    act.wait_ge(*W("gram_k", 4))
                if p >= 2:
                    act.wait_ge(*W("sb_sp", p - 1))
                f(sb_e[g], z, ACT.Abs).then_inc(S("sb_abs"), 1)
                act.wait_ge(*W("sb_abs", p + 1))
                f(sb_e[g], sb_e[g], ACT.Exp, scale=-1.0).then_inc(S("sb_exp"), 1)

            def sb_log(p):
                g = p % 2
                act.wait_ge(*W("sb_exp", p + 1))
                f(sb_e[g], sb_e[g], ACT.Ln, bias=1.0).then_inc(S("sb_ln"), 1)

            def sb_weights(p):
                g = p % 2
                act.wait_ge(*W("sb_expo", p + 1))
                f(sb_att[g], sb_att[g], ACT.Exp).then_inc(S("sb_att"), 1)

            for p in range(4):
                if p >= 2:
                    sb_weights(p - 2)
                sb_exp(p)
                if p % 2:
                    sb_log(p - 1)
                    sb_log(p)
            sb_weights(2)
            sb_weights(3)
            for j in range(2):
                act.wait_ge(*W("sb_o", 2 * j + 2))
                f(sq[:, 2 * j:2 * j + 2, :], ps[:, 4 + j, :].rearrange("p (f n) -> p f n", f=2),
                  ACT.Square).then_inc(S("sbo_sq"), 1)
            act.wait_ge(*W("sbo_ms", 2))
            f(kn, banks(6), ACT.Sqrt, bias=EPS_COL).then_inc(S("sbo_root"), 1)

            act.wait_ge(*W("sb_out", 4))
            for level in range(1, 6):
                for t in range(TT):
                    i = 2 * level + t
                    act.wait_ge(*W("inv_x", i + 1))
                    if level > 1:
                        act.wait_ge(*W("inv_tt", i - 3))
                        act.wait_ge(*W("inv_t", i - 3))
                    f(inv_x[:, 8 * t:8 * t + 8, :], ps[:, t, :].rearrange("p (i n) -> p i n", n=CH),
                      ACT.Copy).then_inc(S("x_kept"), 1)
            for c in range(NCH):
                rows_ = slice((c % 2) * CH, (c % 2 + 1) * CH)
                act.wait_ge(*W("rec_rhs", c + 1))
                act.wait_ge(*W("u_zero", 1))
                f(rhs_z[rows_, c % 2, :], ps[rows_, 0, :], ACT.Copy).then_inc(S("rhs_kept"), 1)
                act.wait_ge(*W("rec_y", c + 1))
                f(y_rw[:, :, c * CH:(c + 1) * CH], ps[:, 2 + c % 2, 0:256].rearrange("p (k n) -> p k n", k=4),
                  ACT.Copy).then_inc(S("y_kept"), 1)
            for j in range(2):
                act.wait_ge(*W("y_centred", j + 1))
                f(sq[:, 2 * j:2 * j + 2, :], y_c[:, 2 * j:2 * j + 2, :], ACT.Square).then_inc(S("y_sq"), 1)
            act.wait_ge(*W("y_var", 2))
            f(y_n, banks(2), ACT.Sqrt, bias=LNX_COL).then_inc(S("y_root"), 1)
            for t in range(TT):
                act.dma_start(ctx_x[:, t, :], a["ctx_2"][t * P:(t + 1) * P, :]).then_inc(S(f"ctx_in{t}"), 16)
            for n in range(HI_RING):
                split(N_FFN2 + n)
            norm("n3")
            norm_cols_hi("n3", lambda k: V("norm_ffn2", k))
            for t in range(TT):
                act.wait_ge(*W(f"ctx_in{t}", 16))
                f(A(23 + t), ctx_x[:, t, :], ACT.Square, accum_out=small[:, 22 + t:23 + t]).then_inc(S("ctx_ss"), 1)
                act.wait_ge(*W("ctx_ss", t + 1))
                f(small[:, 24 + t:25 + t], small[:, 22 + t:23 + t], ACT.Sqrt, scale=1.0 / D,
                  bias=EPS_COL).then_inc(S("ctx_root"), 1)
            ffn(N_FFN2, "f2")
            def mod(j, k):
                return modc[:, 8 * j + k:8 * j + k + 1]

            def high(c, tag):
                act.wait_ge(*W(tag + "_cols_v", 4))
                act.wait_ge(*W(tag + "_cols_a", 4))
                f(both_hi[:, c], hall[:, c], ACT.Copy).then_inc(S(tag + "_high"), 1)

            split(N_WIN2)
            act.wait_ge(*W("mod_cols", 3))
            norm_cols("ctx", lambda k: mod(5, k), lambda k: mod(4, k), 0, 0)
            high(0, "ctx")
            split(N_WIN2 + 1)
            norm("n4")
            split(N_WIN2 + 2)
            norm_cols("n4", lambda k: mod(1, k), lambda k: mod(0, k), 4)
            high(1, "n4")
            halves = lambda b: ps[:, b, :].rearrange("p (f n) -> p f n", f=2)
            for j in range(22):
                act.wait_ge(*W("w_used", N_WIN2 + j + 1))
                b0 = 2 * (j % 2)
                if j < 4:
                    f(k_all[:, 2 * j:2 * j + 2, 0:T], ps[:, b0:b0 + 2, 0:T], ACT.Copy)
                if j < 8:
                    if j >= 2:
                        act.wait_ge(*W("roped", j - 1))
                    f(rope_raw[j % 2], ps[:, b0:b0 + 2, T:2 * T] if j < 4 else halves(b0),
                      ACT.Copy).then_inc(S("w2_copied"), 1)
                elif j < 12:
                    f(v_all[:, :, (j - 8) * 256:(j - 7) * 256], banks(b0), ACT.Copy).then_inc(S("w2_copied"), 1)
                else:
                    o = f_t if j < 14 else ga if j < 18 else gf
                    first = 2 * ((j - 12) % 2 if j < 14 else (j - 14) % 4)
                    f(o[:, first:first + 2, :], halves(b0), ACT.Copy).then_inc(S("w2_copied"), 1)
                if j + HI_RING < 22:
                    if j + HI_RING == 14:
                        act.wait_ge(*W("roped", 8))
                    split(N_WIN2 + j + HI_RING)

            def attend(h):
                for t in range(TT):
                    n = 2 * h + t
                    act.wait_ge(*W("att_max", n + 1))
                    if n >= 4:
                        act.wait_ge(*W("att_a", n - 3))
                    for i in range(2):
                        f(probs[n % 4][:, i, :], ps[:, 4 + 2 * t + i, :], ACT.Exp, scale=HD ** -0.5,
                          bias=small[:, 28 + 2 * t + i:29 + 2 * t + i],
                          accum_out=small[:, 36 + 2 * (n % 4) + i:37 + 2 * (n % 4) + i]).then_inc(S("att_p"), 1)

            def keep_head(h):
                act.wait_ge(*W("att_o", h + 1))
                f(heads[:, h, :], ps[:, 1, 0:T], ACT.Copy).then_inc(S("heads_kept"), 1)
                act.wait_ge(*W("heads_kept", h + 1))
                f(heads_sq[:, h, :], heads[:, h, :], ACT.Square).then_inc(S("heads_sq"), 1)

            attend(0)
            act.wait_ge(*W("lam_sum", 1))
            f(small[:, 32:34], ps[:, 1, 0:2], ACT.Exp).then_inc(S("lam_exp"), 1)
            for h in range(8):
                if h + 1 < 8:
                    attend(h + 1)
                if h:
                    keep_head(h - 1)
                for t in range(TT):
                    act.wait_ge(*W("att_turned", 2 * h + t + 1))
                    if h >= 2 and t == 0:
                        act.wait_ge(*W("att_o", h - 1))
                    f(att_t[h % 2][:, :, t * P:(t + 1) * P], ps[:, 2 + t, :].rearrange("p (k n) -> p k n", k=4),
                      ACT.Copy).then_inc(S("att_t"), 1)
            keep_head(7)
            act.dma_start(w_route[:, :, 0:4], a["w_router_group_2"].rearrange("(k p) n -> p k n", p=P)).then_inc(
                S("route_in"), 16)
            act.dma_start(w_route[:, :, 4:20], a["w_router_expert_2"].rearrange("(k p) n -> p k n", p=P)).then_inc(
                S("route_in"), 16)
            act.dma_start(row_f, a["rows"][:, 0:1044]).then_inc(S("route_in"), 16)
            split(N_FO)
            for j in range(4):
                act.wait_ge(*W("heads_ss", j + 1))
                f(heads_rms[:, 2 * j:2 * j + 2, :], halves(4 + j), ACT.Sqrt, scale=1.0 / P,
                  bias=EPS_COL).then_inc(S("heads_root"), 1)
            act.wait_ge(*W("att_turned", 16))
            for t in range(TT):
                for g in range(2):
                    act.wait_ge(*W("dft_1", 2 * t + g + 1))
                    f(dft_mid[:, t, 2 * g:2 * g + 2, :], halves(2 * t + g), ACT.Copy).then_inc(S("dft_mid"), 1)
            for g in range(2):
                act.wait_ge(*W("dft_2", g + 1))
                if g == 0:
                    act.wait_ge(*W("dft_mid", 4))
                f(four_t[:, 2 * g:2 * g + 2, :], halves(g), ACT.Copy).then_inc(S("four_t"), 1)
                act.wait_ge(*W("four_t", g + 1))
                f(four_hi[:, 2 * g:2 * g + 2, :], four_t[:, 2 * g:2 * g + 2, :], ACT.Copy).then_inc(S("four_hi"), 1)
            act.wait_ge(*W("att_a", 16))
            split(N_FO + 1)
            for m in (gf, ga):
                f(m, m, ACT.Sigmoid).then_inc(S("gates_sig"), 1)
            for n in range(N_AO, N_O2):
                split(n)
                if n == N_AO:
                    for j in range(2):
                        s4 = slice(4 * j, 4 * j + 4)
                        act.wait_ge(*W("heads_normed", j + 1))
                        f(heads_hi[:, s4, :], heads[:, s4, :], ACT.Copy).then_inc(S("heads_hi"), 1)
            for c in range(4):
                s2 = slice(2 * c, 2 * c + 2)
                split(N_O2 + c)
                act.wait_ge(*W("y_mix", c + 1))
                f(y_mix_hi[:, s2, :], y_mix[:, s2, :], ACT.Copy).then_inc(S("y_mix_hi"), 1)
            norm("n5")
            norm_cols("n5", lambda k: mod(3, k), lambda k: mod(2, k), 4)
            act.wait_ge(*W("route_max", 1))
            f(rt(7, 8), rt(6, 8), ACT.Exp).then_inc(S("route_exp"), 1)
            act.wait_ge(*W("route_diff", 1))
            f(rt(9, 2), rt(8, 2), ACT.Exp).then_inc(S("route_exp"), 1)

            act.wait_ge(*W("y_kept_v", 1))
            act.sem_inc(S("y_kept_a"), 1)
            act.wait_ge(*W("rounds", 1))
            n_r = act.value_load(n_rounds[0:1, 0:1].bitcast(U32), min_val=1, max_val=4)
            with act.Fori(0, n_r * (E // 2)) as i:
                act.wait_ge(*W("gathered", i * 2 + 3))
                for k in range(4, 8):
                    f(h_sel[:, k, :], ps[:, 1, (k - 4) * P:(k - 3) * P], ACT.Identity, scale=mod(3, k),
                      bias=mod(2, k)).then_inc(S("h_sel_a"), 1)
                for e in range(2):
                    half = slice(e * SLOTS, (e + 1) * SLOTS)
                    act.wait_ge(*W("w_used", i * 12 + (N_EXP + 4 * e + 2)))
                    f(hs[half, :], ps[half, 0, :], ACT.Silu).then_inc(S("hs_silu"), 1)
                act.wait_ge(*W("hs_turned", i + 1))
                f(hs_t, ps[:, 2, :].rearrange("p (k n) -> p k n", k=4), ACT.Copy).then_inc(S("hs_t"), 1)
                act.wait_ge(*W("w_used", i * 12 + (N_EXP + 12)))
                f(y_e[:, 0:512], ps[:, 2, :], ACT.Copy).then_inc(S("y_kept_a"), 1)
            for t in range(TT):
                act.wait_ge(*W("x5_done", 2 * (t + 1)))
                f(gated[:, t, :], x[:, t, :], ACT.Square, accum_out=ssum[:, t:t + 1]).then_inc(S("n6_ss"), 1)
                act.wait_ge(*W("n6_ss", t + 1))
                f(rstd[:, t:t + 1], ssum[:, t:t + 1], ACT.Sqrt, scale=1.0 / D, bias=EPS_COL).then_inc(
                    S("n6_root"), 1)

        @block.vector
        def _(v):
            steps = [0]

            def link(ins):
                steps[0] += 1
                ins.then_inc(S("v_step"), 1)
                v.wait_ge(*W("v_step", steps[0]))

            stt, ts, tt = v.scalar_tensor_tensor, v.tensor_scalar, v.tensor_tensor

            def norm_rows(tag):
                for t in range(TT):
                    v.wait_ge(*W(tag + "_root", t + 1))
                    link(v.reciprocal(rstd[:, t:t + 1], rstd[:, t:t + 1]))
                    ts(xn[:, t, :], x[:, t, :], rstd[:, t:t + 1], None, ALU.mult).then_inc(
                        S(tag + "_scaled"), 1)

            def split(n, it=None, per=0):
                v.wait_ge(*W("w_hi", at(n_split(n) + 1, it, per)))
                tt(lo(n), slot(n), hi(n), ALU.subtract).then_inc(S("w_lo"), 1)

            def norm_cols_lo(tag, gain):
                for k in range(KT):
                    v.wait_ge(*W(tag + "_hi", (k // 2 + 1) * 2))
                    stt(h_lo[:, k, :], ps[:, 4 + k // 2, (k % 2) * T:(k % 2 + 1) * T], gain(k), h_hi[:, k, :],
                        ALU.mult, ALU.subtract).then_inc(S(tag + "_lo"), 1)

            def norm_cols(tag, gain, shift=None, b0=0, c=1):
                for k in range(4):
                    v.wait_ge(*W(tag + "_turned", k // 2 + 1))
                    src = ps[:, b0 + k // 2, (k % 2) * T:(k % 2 + 1) * T]
                    o = hall[:, c, k, :]
                    if shift:
                        m = ts(o, src, gain(k), shift(k), ALU.mult, ALU.add)
                    else:
                        m = ts(o, src, gain(k), None, ALU.mult)
                    m.then_inc(S(tag + "_cols_v"), 1)

            def add_rows(tag, used, scale):
                tile_0_of = {"x1_done": 1, "x2_done": 2, "x3_done": 3}
                for t in range(TT):
                    v.wait_ge(*(W("w_used", used) if t else W("tile_0", tile_0_of[tag])))
                    for h in range(2):
                        s = slice(h * 512, (h + 1) * 512)
                        stt(x[:, t, s], ps[:, 4 + 2 * t + h, :], scale, x[:, t, s], ALU.mult, ALU.add).then_inc(
                            S(tag), 1)

            def products(tag, j, it=None):
                v.wait_ge(*W(f"wmod_in{j % 2}_{tag}", at(16 * (j // 2 + 1), it, 16 * MOD_PER_IT[tag] // 2)))
                w = (wmod if tag == "1" else wmod_2)[j % 2]
                if tag == "2":
                    if j:
                        v.wait_ge(*W("mod_kept_2", at(2 * j - 1, it, 2 * MOD_PER_IT[tag])))
                    for k in range(KT):
                        m = ts(mod_prod[0][:, k, :], w[:, k, :], V("c_ctx_2", k), None, ALU.mult)
                    m.then_inc(S("mod_prod_2"), 1)
                    n = at(2 * j + 1, it, 2 * MOD_PER_IT[tag])
                    v.wait_ge(*W("mod_prod_2", n))
                for k in range(KT):
                    m = ts(w[:, k, :], w[:, k, :], V("c_2", k), None, ALU.mult)
                m.then_inc(S("mod_prod_" + tag), 1)

            MOD_PER_IT = {"1": 4, "2": 2}
            MOD_BESIDE = {"1": {1: (0, 1), 2: (2, 3), 3: (4, 5), 4: (6, 7)}, "2": {2: (0, 1), 3: (2,), 4: (3,)}}

            def ffn(n0, tag):
                def chunk(i, it=None):
                    ahead = [n0 + n + HI_RING for n in ffn_chunks(i)]
                    for n in ahead[:1]:
                        split(n, it, 6)
                    v.wait_ge(*W("w_used", at(n0 + n_up(i) + 1, it, 6)))
                    v.wait_ge(*W(tag + "_silu", at(i + 1, it, 2)))
                    if i >= 2:
                        v.wait_ge(*W("w_used", at(n0 + n_down(i - 2) + 1, it, 6)))
                    h, h_high, h_low = (m[:, i % 2, :, :] for m in (hid, hid_hi, hid_lo))
                    tt(h, sg[:, i % 2, :].rearrange("p (f n) -> p f n", f=2),
                       ps[:, 2 * (i % 2) + 1, :].rearrange("p (f n) -> p f n", f=2), ALU.mult).then_inc(
                        S(tag + "_prod"), 1)
                    v.wait_ge(*W(tag + "_prod", at(i + 1, it, 2)))
                    v.tensor_copy(h_high, h).then_inc(S(tag + "_hid_hi"), 1)
                    v.wait_ge(*W(tag + "_hid_hi", at(i + 1, it, 2)))
                    tt(h_low, h, h_high, ALU.subtract).then_inc(S(tag + "_hidden"), 1)
                    for n in ahead[1:]:
                        split(n, it, 6)
                    for j in MOD_BESIDE[tag[1]].get(i, ()):
                        products(tag[1], j, it)

                for i in range(FFN_PEEL):
                    chunk(i)
                with v.Fori(0, FFN_LOOP) as it:
                    chunk(FFN_PEEL, it)
                    chunk(FFN_PEEL + 1, it)
                for i in range(FFN_PEEL + 2 * FFN_LOOP, FFC):
                    chunk(i)

            norm_rows("n1")
            split(N_FFN1)
            norm_cols_lo("n1", lambda k: V("norm_ffn1", k))
            split(N_FFN1 + 1)
            split(N_FFN1 + 2)
            v.wait_ge(*W("c_silu", 1))
            ffn(N_FFN1, "f1")
            add_rows("x1_done", N_FFN1 + 3 * FFC, 0.5)
            def mod_columns(pieces):
                for j, bias, gain in pieces:
                    at_b, g0 = VEC_AT["b_mod_2"][0] + bias, VEC_AT[gain][0]
                    c_ = modc[:, 16 * j + 8:16 * j + 16]
                    link(tt(modc[:, 16 * j:16 * j + 16], ps[:, 0, 16 * j:16 * j + 16], vec[:, at_b:at_b + 16],
                            ALU.add))
                    stt(c_, c_, 1.0, vec[:, g0:g0 + 8], ALU.add, ALU.mult).then_inc(S("mod_cols"), 1)

            norm_rows("n2")
            v.wait_ge(*W("mod_sums", 1))
            mod_columns([(1, 24, "norm2_g_2")])
            v.wait_ge(*W("consts", 16))
            for q in range(2):
                ts(small[:, 20 + q:21 + q], V("sb_q_norm"), C("half")[:, q:q + 1], 0.125, ALU.mult,
                   ALU.mult).then_inc(S("q_gain"), 1)
            norm_cols("n2", lambda k: V("norm_mix", k), None, 4)

            def shift(j):
                v.wait_ge(*W("win_copied", j + 1))
                if j:
                    v.wait_ge(*W("shifted", j))
                u = ubuf[:, j % 2, :, 1:T + 1]
                link(tt(ushift, ubuf[:, j % 2, :, 0:T], u, ALU.subtract))
                for f in range(2):
                    tile = 2 * RW_ORDER[j] + f
                    o = {12: x_wa, 13: x_g}.get(tile)
                    if o is None:
                        o = rw_x[tile // 4 * 4][:, tile % 4, :]
                    m = stt(o, ushift[:, f, :], V("rw_mu", tile), u[:, f, :], ALU.mult, ALU.add)
                m.then_inc(S("shifted"), 1)

            shift(0)
            shift(1)
            v.wait_ge(*W("sig_w", 4))
            v.wait_ge(*W("reset_mask", 1))
            v.tensor_tensor_scan(cum.rearrange("p k n -> p (k n)"), r_scan, sig_w.rearrange("p k n -> p (k n)"),
                                 0.0, ALU.mult, ALU.add).then_inc(S("cum"), 1)
            v.wait_ge(*W("cum", 1))
            tt(sig_w, cum, sig_w, ALU.subtract).then_inc(S("cum"), 1)
            shift(2)
            v.wait_ge(*W("shifted", 3))
            for k in range(4):
                ts(kk[:, k, :], xk[:, k, :], V("rw_k_k", k), None, ALU.mult).then_inc(S("kk_raw"), 1)
            v.wait_ge(*W("sig_a", 4))
            for k in range(4):
                m = ts(kf[:, k, :], av[:, k, :], 1.0, V("rw_k_a", k), ALU.subtract, ALU.mult)
            link(m)
            link(stt(kf, kf, 1.0, xk, ALU.add, ALU.mult))
            shift(3)
            shift(4)
            v.wait_ge(*W("shifted", 5))
            for k in range(4):
                m = stt(bonus[:, k, :], xr[:, k, :], V("rw_r_k", k), kf[:, k, :], ALU.mult, ALU.mult)
            m.then_inc(S("bonus_prod"), 1)
            v.wait_ge(*W("kk_norm", 1))
            link(ts(sq, sq, 1e-12, None, ALU.max))
            link(v.reciprocal(sq, sq))
            stt(kk, kk, 1.0, sq, ALU.mult, ALU.mult).then_inc(S("kk_unit"), 1)
            v.wait_ge(*W("kk_unit", 1))
            link(tt(av, kk, av, ALU.mult))
            v.wait_ge(*W("decays", 3))
            tt(b_bar, av, w_inv, ALU.mult).then_inc(S("b_bar"), 1)
            tt(k_bar, kf, w_inv, ALU.mult).then_inc(S("k_bar"), 1)
            chunks = lambda m: m.rearrange("p k (c n) -> p (k c) n", n=CH)
            v.wait_ge(*W("g_copied", 2))
            for j, src, scale, w in ((0, kk, "neg_half", w_ex), (1, xr, "half", w_in_)):
                for q in range(2):
                    stt(arz[:, q, :, :, j, :].rearrange("p k c n -> p (k c) n"), chunks(src),
                        C(scale)[:, q:q + 1], chunks(w), ALU.mult, ALU.mult).then_inc(S("arz"), 1)
            shift(5)
            shift(6)
            v.wait_ge(*W("bonus_sum", 2))
            v.wait_ge(*W("shifted", 7))
            stt(bonus, banks(4), float(HD), xv, ALU.mult, ALU.mult).then_inc(S("bonus_v"), 1)
            v.wait_ge(*W("q_root", 1))
            link(v.reciprocal(sb_sq_q, sb_sq_q))
            for q in range(2):
                stt(qz[:, q, :, :], q_raw, small[:, 20 + q:21 + q], sb_sq_q, ALU.mult, ALU.mult).then_inc(
                    S("qz"), 1)
            v.wait_ge(*W("arz", 4))
            for t in range(TT):
                v.wait_ge(*W("v_turned", t + 1))
                for q in range(2):
                    ts(vz[:, q, t, :], ps[:, 6 + t, :], C("half")[:, q:q + 1], None, ALU.mult).then_inc(
                        S("v_tok"), 1)
            v.wait_ge(*W("k_root", 1))
            link(v.reciprocal(sb_sq_k, sb_sq_k))
            stt(kn, kn, V("sb_k_norm"), sb_sq_k, ALU.mult, ALU.mult).then_inc(S("kn"), 1)
            v.wait_ge(*W("w_end", 1))
            for sem, ab, rb, b0 in (("gram_b", ab_t, rb_t, 0), ("gram_k", ak_t, rk_t, 4)):
                for j in range(4):
                    v.wait_ge(*W(sem, j + 1))
                    src = ps[:, b0 + j, :].rearrange("p (i w n) -> p i w n", w=2, n=CH)
                    for w, o, mask in ((0, ab, "strict"), (1, rb, "incl")):
                        tt(o[:, 4 * j:4 * j + 4, :], src[:, :, w, :],
                           C(mask).unsqueeze(1).broadcast_to([P, 4, CH]), ALU.mult).then_inc(S(sem + "_masked"), 1)

            both = lambda name: C(name).unsqueeze(1).broadcast_to([P, 2, 384])

            def sb_softplus(p):
                g = p % 2
                v.wait_ge(*W("sb_ln", p + 1))
                link(stt(sb_sp[g], ps[:, 2 * g:2 * g + 2, 0:384], 0.0, sb_e[g], ALU.max, ALU.add))
                tt(sb_sp[g], sb_sp[g], both("causal"), ALU.mult).then_inc(S("sb_sp"), 1)

            def sb_exponent(p):
                g = p % 2
                v.wait_ge(*W("sb_sum", p + 1))
                if p >= 2:
                    v.wait_ge(*W("sb_o", p - 1))
                stt(sb_att[g], ps[:, 2 * g:2 * g + 2, 0:384], 0.0, both("causal_add"), ALU.min,
                    ALU.add).then_inc(S("sb_expo"), 1)

            for p in (0, 2):
                sb_softplus(p)
                sb_softplus(p + 1)
                sb_exponent(p)
                sb_exponent(p + 1)
            v.wait_ge(*W("sbo_root", 1))
            link(v.reciprocal(kn, kn))
            for k in range(4):
                stt(mix[0][:, k, :], banks(4)[:, k, :], V("sb_out_norm", k), kn[:, k, :], ALU.mult,
                    ALU.mult).then_inc(S("sb_out"), 1)
            for t in range(TT):
                s8 = slice(8 * t, 8 * t + 8)
                v.wait_ge(*W("inv_x", t + 1))
                tt(inv_t[:, s8, :], inv_t[:, s8, :], ps[:, t, :].rearrange("p (i n) -> p i n", n=CH),
                   ALU.add).then_inc(S("t_added"), 1)
                tt(inv_tt[:, s8, :], inv_tt[:, s8, :], level_a[0][:, s8, :], ALU.add).then_inc(S("tt_added"), 1)
            for level in range(1, 6):
                for t in range(TT):
                    i = 2 * level + t
                    s8 = slice(8 * t, 8 * t + 8)
                    if level < 5:
                        v.wait_ge(*W("inv_t", i - 1))
                        cols = blocks_of_8(inv_t[:, s8, :], level, 0)
                        tt(cols, cols, ps[:, 2, 0:256].rearrange("p (i b n) -> p i b n", i=8, n=2 ** level),
                           ALU.add).then_inc(S("t_added"), 1)
                    v.wait_ge(*W("inv_tt", i - 1))
                    cols = blocks_of_8(inv_tt[:, s8, :], level, 1)
                    tt(cols, cols, ps[:, 3, 0:256].rearrange("p (i b n) -> p i b n", i=8, n=2 ** level),
                       ALU.add).then_inc(S("tt_added"), 1)
            for c in range(NCH):
                rows_ = slice((c % 2) * CH, (c % 2 + 1) * CH)
                v.wait_ge(*W("rec_u", c + 1))
                v.wait_ge(*W("u_zero", 1))
                v.tensor_copy(u_z[rows_, c % 2, :], ps[rows_, 1, :]).then_inc(S("u_kept"), 1)
                if c < NCH - 1:
                    v.wait_ge(*W("rec_state", c + 1))
                    sums = ps[:, 4, 0:256].rearrange("p (k n) -> p k n", k=4)
                    if c:
                        v.wait_ge(*W("rec_y", c))
                        link(tt(state_sum, sums, state[:, c % 2, :, :], ALU.add))
                        sums = state_sum
                    tt(state[:, (c + 1) % 2, :, :], sums, w_end[:, :, c].unsqueeze(2).broadcast_to([P, 4, HD]),
                       ALU.mult).then_inc(S("state"), 1)
            for j in range(2):
                v.wait_ge(*W("y_mean", j + 1))
                tt(y_c[:, 2 * j:2 * j + 2, :], y_rw[:, 2 * j:2 * j + 2, :],
                   ps[:, j, :].rearrange("p (f n) -> p f n", f=2), ALU.subtract).then_inc(S("y_centred"), 1)
            for k in range(4):
                m = ts(bonus[:, k, :], bonus[:, k, :], V("rw_ln_b", k), None, ALU.add)
            link(m)
            link(tt(bonus, bonus, g_rw, ALU.mult))
            v.wait_ge(*W("y_centred", 2))
            v.wait_ge(*W("y_sq", 2))
            for k in range(4):
                m = stt(y_c[:, k, :], y_c[:, k, :], V("rw_ln_w", k), g_rw[:, k, :], ALU.mult, ALU.mult)
            link(m)
            v.wait_ge(*W("y_root", 1))
            link(v.reciprocal(y_n, y_n))
            link(tt(y_n, y_c, y_n, ALU.mult))
            tt(mix[1], y_n, bonus, ALU.add).then_inc(S("rw_out"), 1)
            for n in range(HI_RING):
                split(N_FFN2 + n)
            add_rows("x2_done", N_WOUT + 4, 1.0)
            norm_rows("n3")
            norm_cols_lo("n3", lambda k: V("norm_ffn2", k))
            for t in range(TT):
                v.wait_ge(*W("ctx_root", t + 1))
                link(v.reciprocal(small[:, 24 + t:25 + t], small[:, 24 + t:25 + t]))
                ts(ctx_x[:, t, :], ctx_x[:, t, :], small[:, 24 + t:25 + t], None, ALU.mult).then_inc(
                    S("ctx_scaled"), 1)
            ffn(N_FFN2, "f2")
            v.wait_ge(*W("mod_sums", 2))
            mod_columns([(0, 0, "norm1_g_2"), (2, 0, "norm1_g_2")])
            split(N_WIN2)
            add_rows("x3_done", N_FFN2 + 3 * FFC, 0.5)
            def mod(j, k):
                return modc[:, 8 * j + k:8 * j + k + 1]

            l0 = VEC_AT["lam_q1_2"][0]
            tt(small[:, 34:36], vec[:, l0:l0 + 2], vec[:, l0 + 2:l0 + 4], ALU.mult).then_inc(S("lam_prod"), 1)
            ts(small[:, 44:45], V("subln_g_2"), 1.0 - LAM_INIT, None, ALU.mult).then_inc(S("head_gain"), 1)
            v.wait_ge(*W("mod_cols", 3))
            def low(c, tag):
                v.wait_ge(*W(tag + "_high", 1))
                tt(both_lo[:, c], hall[:, c], both_hi[:, c], ALU.subtract).then_inc(S(tag + "_lo"), 1)

            norm_cols("ctx", lambda k: mod(5, k), lambda k: mod(4, k), 0, 0)
            low(0, "ctx")
            split(N_WIN2 + 1)
            norm_rows("n4")
            split(N_WIN2 + 2)
            norm_cols("n4", lambda k: mod(1, k), lambda k: mod(0, k), 4)
            low(1, "n4")

            swap = list(range(16, 32)) + list(range(16))
            wide = lambda name: C(name).unsqueeze(1).broadcast_to([P, 2, T])
            for j in range(8):
                if j:
                    split(N_WIN2 + j + 2)
                g = j % 2
                v.wait_ge(*W("w2_copied", j + 1))
                link(v.stream_shuffle(rope_sh[g], rope_raw[g], swap))
                tt(rope_sh[g], rope_sh[g], wide("sin"), ALU.mult).then_inc(S("rope_part"), 1)
                tt(rope_raw[g], rope_raw[g], wide("cos"), ALU.mult).then_inc(S("rope_part"), 1)
                v.wait_ge(*W("rope_part", 2 * j + 2))
                if j < 4:
                    tt(k_all[:, 2 * j:2 * j + 2, T:2 * T], rope_raw[g], rope_sh[g], ALU.add).then_inc(
                        S("roped_k"), 1)
                    v.wait_ge(*W("roped_k", j + 1))
                    v.sem_inc(S("roped"), 1)
                else:
                    link(tt(rope_raw[g], rope_raw[g], rope_sh[g], ALU.add))
                    for i in range(2):
                        m = ts(qz2[:, i, 2 * (j - 4):2 * (j - 4) + 2, :], rope_raw[g], C("half")[:, i:i + 1], None,
                               ALU.mult)
                        m.then_inc(S("roped" if i else "roped_half"), 1)
                    v.wait_ge(*W("roped", j + 1))
                    v.sem_inc(S("roped_q"), 1)

            for j in range(10, 22):
                split(N_WIN2 + j)

            def row_max(n):
                t = n % 2
                v.wait_ge(*W("att_s", n + 1))
                mx = small[:, 46 + 2 * t:48 + 2 * t]
                link(v.tensor_reduce(mx, ps[:, 4 + 2 * t:6 + 2 * t, :], AX_X, ALU.max))
                ts(small[:, 28 + 2 * t:30 + 2 * t], mx, -HD ** -0.5, None, ALU.mult).then_inc(S("att_max"), 1)

            def combine(n):
                h, t = n // 2, n % 2
                s_ = small[:, 36 + 2 * (n % 4):38 + 2 * (n % 4)]
                v.wait_ge(*W("att_p", 2 * n + 2))
                link(v.reciprocal(s_, s_))
                tt(s_[:, 1:2], s_[:, 1:2], small[:, 45:46], ALU.mult).then_inc(S("att_r"), 1)
                if n >= 4:
                    v.wait_ge(*W("att_turned", n - 3))
                o = att[h % 2][:, t, :]
                link(ts(o, probs[n % 4][:, 0, :], s_[:, 0:1], None, ALU.mult))
                v.wait_ge(*W("att_r", n + 1))
                stt(o, probs[n % 4][:, 1, :], s_[:, 1:2], o, ALU.mult, ALU.add).then_inc(S("att_a"), 1)

            row_max(0)
            row_max(1)
            v.wait_ge(*W("lam_exp", 1))
            link(tt(small[:, 45:46], small[:, 33:34], small[:, 32:33], ALU.subtract))
            link(ts(small[:, 45:46], small[:, 45:46], -LAM_INIT, None, ALU.add))
            for n in range(16):
                combine(n)
                if n + 2 < 16:
                    row_max(n + 2)

            split(N_FO)

            def invert(j):
                v.wait_ge(*W("heads_root", j + 1))
                hr = heads_rms[:, 2 * j:2 * j + 2, :]
                v.reciprocal(hr, hr).then_inc(S("heads_inv"), 1)

            def four_rest(g):
                v.wait_ge(*W("four_hi", g + 1))
                tt(four_lo[:, 2 * g:2 * g + 2, :], four_t[:, 2 * g:2 * g + 2, :], four_hi[:, 2 * g:2 * g + 2, :],
                   ALU.subtract).then_inc(S("four_lo"), 1)

            invert(0)
            invert(1)
            four_rest(0)
            invert(2)
            four_rest(1)
            split(N_FO + 1)
            v.wait_ge(*W("heads_kept", 8))
            v.wait_ge(*W("head_gain", 1))
            for j in range(2):
                if j:
                    invert(3)
                v.wait_ge(*W("heads_inv", 2 * j + 2))
                ho, s4 = heads[:, 4 * j:4 * j + 4, :], slice(4 * j, 4 * j + 4)
                stt(ho, ho, small[:, 44:45], heads_rms[:, s4, :], ALU.mult, ALU.mult).then_inc(S("heads_normed"), 1)
                if j:
                    split(N_AO)
                v.wait_ge(*W("heads_hi", j + 1))
                tt(heads_lo[:, s4, :], ho, heads_hi[:, s4, :], ALU.subtract).then_inc(S("heads_lo"), 1)
            v.wait_ge(*W("gates_sig", 2))
            for c in range(2):
                v.wait_ge(*W("w_used", N_FO + c + 1))
                tt(y_mix[:, 4 * c:4 * c + 4, :], gf[:, 4 * c:4 * c + 4, :], banks(2 * c), ALU.mult).then_inc(
                    S("y_four"), 1)
            split(N_AO + 1)
            split(N_AO + 2)
            for c in range(4):
                s2 = slice(2 * c, 2 * c + 2)
                if c == 0:
                    split(N_AO + 3)
                v.wait_ge(*W("w_used", N_AO + c + 1))
                link(tt(ga[:, s2, :], ga[:, s2, :], ps[:, 4 + c, :].rearrange("p (f n) -> p f n", f=2), ALU.mult))
                tt(y_mix[:, s2, :], y_mix[:, s2, :], ga[:, s2, :], ALU.add).then_inc(S("y_mix"), 1)
                split(N_O2 + c)
                v.wait_ge(*W("y_mix_hi", c + 1))
                tt(y_mix_lo[:, s2, :], y_mix[:, s2, :], y_mix_hi[:, s2, :], ALU.subtract).then_inc(
                    S("y_mix_lo"), 1)

            def add_gated(tag, gate, b0, used=None):
                for t in range(TT):
                    v.wait_ge(*(W("moe_sum", t + 1) if used is None else W("w_used", used) if t else
                                W("tile_0", 4)))
                    for h in range(2):
                        s = slice(h * 512, (h + 1) * 512)
                        link(tt(gated[:, t, s], ps[:, b0 + 2 * t + h, :], gb[:, gate, s], ALU.mult))
                        tt(x[:, t, s], x[:, t, s], gated[:, t, s], ALU.add).then_inc(S(tag), 1)

            add_gated("x4_done", 0, 0, N_O2 + 4)
            norm_rows("n5")
            norm_cols("n5", lambda k: mod(3, k), lambda k: mod(2, k), 4)

            r16 = lambda j: rt(j).rearrange("p (t e) -> p t e", t=TT)
            r4 = lambda j: rt(j, 8).rearrange("p (t e) -> p t e", t=TT)
            r1 = lambda j: rt(j, 2)
            b16 = lambda m: m.unsqueeze(2).broadcast_to([P, TT, 16])
            b4 = lambda m: m.unsqueeze(2).broadcast_to([P, TT, 4])
            rev16 = C("rev").unsqueeze(1).broadcast_to([P, TT, 16])
            rev4 = C("rev")[:, 0:4].unsqueeze(1).broadcast_to([P, TT, 4])
            logit = ps[:, 0, 0:64].rearrange("p (t n) -> p t n", t=TT)
            BIG = 1e30

            def first_of(o, values, top, rev, bc, tmp, best):
                link(tt(tmp, values, bc(top), ALU.is_equal))
                link(tt(tmp, tmp, rev, ALU.mult))
                link(v.tensor_reduce(best, tmp, AX_X, ALU.max))
                link(tt(o, rev, bc(best), ALU.is_equal))

            v.wait_ge(*W("logits", 1))
            link(v.tensor_copy(r4(0), logit[:, :, 0:4]))
            link(v.tensor_copy(r16(1), logit[:, :, 4:20]))
            link(v.tensor_reduce(r1(2), r4(0), AX_X, ALU.max))
            tt(r4(6), r4(0), b4(r1(2)), ALU.subtract).then_inc(S("route_max"), 1)
            first_of(r4(3), r4(0), r1(2), rev4, b4, r4(4), r1(5))
            e44 = lambda m: m.rearrange("p t (g e) -> p (t g) e", g=4)
            gsel = rt(3, 8).unsqueeze(2).broadcast_to([P, 8, 4])
            link(tt(e44(r16(10)), e44(r16(1)), gsel, ALU.mult))
            link(ts(rt(11, 8), rt(3, 8), 1.0, BIG, ALU.subtract, ALU.mult))
            link(tt(e44(r16(10)), e44(r16(10)), rt(11, 8).unsqueeze(2).broadcast_to([P, 8, 4]), ALU.add))
            link(v.tensor_reduce(r1(12), r16(10), AX_X, ALU.max))
            first_of(r16(13), r16(10), r1(12), rev16, b16, r16(14), r1(5))
            link(stt(rt(10), rt(13), -BIG, rt(10), ALU.mult, ALU.add))
            link(v.tensor_reduce(r1(15), r16(10), AX_X, ALU.max))
            first_of(r16(16), r16(10), r1(15), rev16, b16, r16(14), r1(5))
            tt(r1(8), r1(15), r1(12), ALU.subtract).then_inc(S("route_diff"), 1)
            tt(rt(4), rt(13), rt(16), ALU.add).then_inc(S("chosen"), 1)
            v.wait_ge(*W("route_exp", 2))
            link(v.tensor_reduce(r1(17), r4(7), AX_X, ALU.add))
            link(ts(r1(18), r1(9), 1.0, None, ALU.add))
            link(tt(r1(17), r1(17), r1(18), ALU.mult))
            link(v.reciprocal(r1(17), r1(17)))
            link(tt(r1(18), r1(17), r1(9), ALU.mult))
            link(tt(r16(13), r16(13), b16(r1(17)), ALU.mult))
            link(tt(r16(16), r16(16), b16(r1(18)), ALU.mult))
            link(tt(rt(19), rt(13), rt(16), ALU.add))
            v.wait_ge(*W("chosen", 1))
            v.wait_ge(*W("places", 1))
            link(tt(rt(20), rt(4), ps[:, 1, 0:32], ALU.mult))
            link(ts(rt(21), rt(4), 1.0, 1e6, ALU.subtract, ALU.mult))
            link(tt(rt(20), rt(20), rt(21), ALU.add))
            turned = lambda m: m.rearrange("p (t e) -> p e t", t=TT)
            for r in range(4):
                tab = lambda m: m[:, 32 * r:32 * r + 32].rearrange("p (e t) -> p e t", t=TT)
                ts(tab(pos_tab), turned(rt(20)), -float(SLOTS * r), None, ALU.add).then_inc(S("tables"), 1)
                v.tensor_copy(tab(gate_tab), turned(rt(19))).then_inc(S("tables"), 1)
            ts(pos_tab[:, 128:132], C("iota")[:, 0:4], 0.0, None, ALU.mult).then_inc(S("tables"), 1)
            ts(gate_tab[:, 128:132], C("iota")[:, 0:4], 0.0, None, ALU.mult).then_inc(S("tables"), 1)
            link(v.tensor_reduce(rt(22, 1), ps[:, 1, 32:48], AX_X, ALU.max))
            for r in range(1, 4):
                m = ts(rt(23, 4)[:, r:r + 1], rt(22, 1), float(SLOTS * r), None, ALU.is_gt)
            link(m)
            link(v.tensor_reduce(rt(22, 1), rt(23, 4)[:, 1:4], AX_X, ALU.add))
            link(ts(rt(22, 1), rt(22, 1), 1.0, None, ALU.add))
            v.tensor_copy(n_rounds.bitcast(U32), rt(22, 1)).then_inc(S("rounds"), 1)
            v.wait_ge(*W("tables", 10))

            def build_picks(i):
                for t in range(TT):
                    for e in range(2):
                        p_ = pos_tab[:, bass.ds(i * 4 + (2 * e + t), 1)]
                        g_ = gate_tab[:, bass.ds(i * 4 + (2 * e + t), 1)]
                        s = slice(e * SLOTS, (e + 1) * SLOTS)
                        m = ts(pick[:, t, s], C("iota"), p_, None, ALU.is_equal)
                        m2 = ts(pick_g[:, t, s], C("iota"), p_, g_, ALU.is_equal, ALU.mult)
                        if t == 1 and e == 1:
                            m.then_inc(S("picked"), 1)
                            m2.then_inc(S("picked_g"), 1)

            build_picks(0)
            v.wait_ge(*W("rounds", 1))
            n_r = v.value_load(n_rounds[0:1, 0:1].bitcast(U32), min_val=1, max_val=4)
            with v.Fori(0, n_r * (E // 2)) as i:
                v.wait_ge(*W("gathered", i * 2 + 2))
                for k in range(4):
                    ts(h_sel[:, k, :], ps[:, 0, k * P:(k + 1) * P], mod(3, k), mod(2, k), ALU.mult,
                       ALU.add).then_inc(S("h_sel_v"), 1)
                for e in range(2):
                    half = slice(e * SLOTS, (e + 1) * SLOTS)
                    v.wait_ge(*W("w_used", i * 12 + (N_EXP + 4 * e + 4)))
                    v.wait_ge(*W("hs_silu", i * 2 + (e + 1)))
                    tt(hs[half, :], hs[half, :], ps[half, 1, :], ALU.mult).then_inc(S("hs"), 1)
                v.wait_ge(*W("pick_turned", i + 1))
                v.tensor_copy(pick_t, ps[:, 3, 0:T].rearrange("p (t n) -> p t n", t=TT)).then_inc(S("pick_t"), 1)
                build_picks(i + 1)
                v.wait_ge(*W("w_used", i * 12 + (N_EXP + 12)))
                v.tensor_copy(y_e[:, 512:1024], ps[:, 3, :]).then_inc(S("y_kept_v"), 1)
            add_gated("x5_done", 1, 4)
            v.wait_ge(*W("final_gain", 1))
            for t in range(TT):
                v.wait_ge(*W("n6_root", t + 1))
                link(v.reciprocal(rstd[:, t:t + 1], rstd[:, t:t + 1]))
                stt(xn[:, t, :].rearrange("p (b n) -> p b n", b=2), x[:, t, :].rearrange("p (b n) -> p b n", b=2),
                    rstd[:, t:t + 1], ps[:, 0:2, :], ALU.mult, ALU.mult).then_inc(S("final"), 1)


def kernel(**inputs):
    import concourse.bacc as bacc
    from concourse.bass_utils import run_bass_kernel_spmd

    nc = bacc.Bacc("TRN2", target_bir_lowering=False, num_devices=1)
    vectors, row_table = pack_vectors(inputs)
    arrays = {"consts": constant_table(), "vectors": vectors, "rows": row_table}
    for name in MATRICES:
        m = np.asarray(inputs[name])
        arrays[name] = np.ascontiguousarray(m.reshape(m.shape[-2:] if m.shape[0] == 1 and m.ndim == 3 else m.shape[1:]))
    aps = {name: nc.dram_tensor("in_" + name, m.shape, F32, kind="ExternalInput").ap() for name, m in arrays.items()}
    out = nc.dram_tensor("out", (T, D), F32, kind="ExternalOutput").ap()
    build(nc, aps, out)
    r = run_bass_kernel_spmd(nc, [{"in_" + k: m for k, m in arrays.items()}], core_ids=[0])
    return r.results[0]["out"].reshape(1, T, D)
```
